# Optimizing a Trainium2 kernel written in Bass

```python
import math
import jax
import jax.numpy as jnp
from jax import lax
import numpy as np
import jax, jax.numpy as jnp

D_MODEL = 1024
BATCH = 1
SEQ = 256
DEPTH = 2

HEAD_DIM = 64
ATTN_SCALE = HEAD_DIM ** -0.5
SWA_HEADS = D_MODEL // 128
SWA_KV_HEADS = SWA_HEADS // 4
SWA_GROUP = SWA_HEADS // SWA_KV_HEADS
SWA_WINDOW = 128
SWA_BLOCK = 128
SC_WIDTH = D_MODEL // 2
SC_KSIZE = 3
MOBA_HEADS = D_MODEL // 128
MOBA_BLOCK = 256
MOBA_TOPK = 3
MOBA_QCHUNK = 32
N_ALIBI_HEADS = SWA_HEADS + MOBA_HEADS
FFN_HIDDEN = -(-8 * D_MODEL // (3 * 256)) * 256
ALPHA = (2 * DEPTH) ** 0.25
BETA = (8 * DEPTH) ** -0.25
LN_EPS = 1e-5

A_Q = SWA_HEADS * HEAD_DIM
A_KV = SWA_KV_HEADS * HEAD_DIM
C_QKV = MOBA_HEADS * HEAD_DIM
PROJ_SIZES = (A_Q, A_KV, A_KV,
              SC_WIDTH, SC_WIDTH, SC_WIDTH,
              C_QKV, C_QKV, C_QKV,
              D_MODEL, D_MODEL, D_MODEL)
PROJ_SPLITS = tuple(int(s) for s in np.cumsum(PROJ_SIZES)[:-1])
PROJ_WIDTH = int(sum(PROJ_SIZES))


def alibi_slopes():
    i = jnp.arange(N_ALIBI_HEADS, dtype=jnp.float32)
    s = jnp.exp2(-8.0 * (i + 1.0) / N_ALIBI_HEADS)
    return s[:SWA_HEADS], s[SWA_HEADS:]

def layer_norm(x, g, b):
    xf = x.astype(jnp.float32)
    mu = jnp.mean(xf, axis=-1, keepdims=True)
    var = jnp.mean(jnp.square(xf - mu), axis=-1, keepdims=True)
    y = (xf - mu) * lax.rsqrt(var + LN_EPS) * g.astype(jnp.float32) + b.astype(jnp.float32)
    return y.astype(x.dtype)

def sliding_window_attention(q, k, v, sinks, slopes):
    B, S = q.shape[0], q.shape[1]
    nb = S // SWA_BLOCK
    qb = q.reshape(B, nb, SWA_BLOCK, SWA_KV_HEADS, SWA_GROUP, HEAD_DIM).astype(jnp.float32)
    kb = k.reshape(B, nb, SWA_BLOCK, SWA_KV_HEADS, HEAD_DIM)
    vb = v.reshape(B, nb, SWA_BLOCK, SWA_KV_HEADS, HEAD_DIM)
    shift = ((0, 0), (1, 0), (0, 0), (0, 0), (0, 0))
    kw = jnp.concatenate([jnp.pad(kb, shift)[:, :-1], kb], axis=2)
    vw = jnp.concatenate([jnp.pad(vb, shift)[:, :-1], vb], axis=2)
    logits = jnp.einsum('bnqhgd,bnkhd->bnhgqk', qb, kw.astype(jnp.float32)) * ATTN_SCALE
    blk = jnp.arange(nb)[:, None] * SWA_BLOCK
    qpos = blk + jnp.arange(SWA_BLOCK)[None, :]
    kpos = blk - SWA_BLOCK + jnp.arange(2 * SWA_BLOCK)[None, :]
    dist = qpos[:, :, None] - kpos[:, None, :]
    allowed = (dist >= 0) & (dist < SWA_WINDOW) & (kpos[:, None, :] >= 0)
    sl = slopes.reshape(SWA_KV_HEADS, SWA_GROUP)[:, :, None, None]
    logits = logits - sl * dist[:, None, None].astype(jnp.float32)
    logits = jnp.where(allowed[:, None, None], logits, -jnp.inf)
    sink = sinks.astype(jnp.float32).reshape(SWA_KV_HEADS, SWA_GROUP)[:, :, None, None]
    m = jnp.maximum(jnp.max(logits, axis=-1, keepdims=True), sink)
    p = jnp.exp(logits - m)
    denom = jnp.sum(p, axis=-1, keepdims=True) + jnp.exp(sink - m)
    out = jnp.einsum('bnhgqk,bnkhd->bnqhgd', p / denom, vw.astype(jnp.float32))
    return out.reshape(B, S, SWA_HEADS * HEAD_DIM).astype(q.dtype)

def gated_short_conv(h, gate_b, gate_c, conv_w):
    u = gate_c * h
    up = jnp.pad(u, ((0, 0), (SC_KSIZE - 1, 0), (0, 0)))
    S = h.shape[1]
    conv = up[:, 0:S] * conv_w[0] + up[:, 1:S + 1] * conv_w[1] + up[:, 2:S + 2] * conv_w[2]
    return gate_b * conv

def moba_attention(q, k, v, slopes):
    B, S = q.shape[0], q.shape[1]
    sp = -(-S // MOBA_BLOCK) * MOBA_BLOCK
    pad = ((0, 0), (0, sp - S), (0, 0), (0, 0))
    q, k, v = [jnp.pad(t, pad).transpose(0, 2, 1, 3) for t in (q, k, v)]
    nblk = sp // MOBA_BLOCK
    top = min(MOBA_TOPK, nblk)
    kbl = k.reshape(B, MOBA_HEADS, nblk, MOBA_BLOCK, HEAD_DIM)
    vbl = v.reshape(B, MOBA_HEADS, nblk, MOBA_BLOCK, HEAD_DIM)
    kmean = jnp.mean(kbl.astype(jnp.float32), axis=3)
    gate = jnp.einsum('bhsd,bhnd->bhsn', q.astype(jnp.float32), kmean)
    cur = jnp.arange(sp) // MOBA_BLOCK
    past = jnp.arange(nblk)[None, :] < cur[:, None]
    gate = jnp.where(past, gate, -jnp.inf)
    _, idx = lax.top_k(gate, top)
    nch = sp // MOBA_QCHUNK
    q_ch = q.reshape(B, MOBA_HEADS, nch, MOBA_QCHUNK, HEAD_DIM).transpose(2, 0, 1, 3, 4)
    idx_ch = idx.reshape(B, MOBA_HEADS, nch, MOBA_QCHUNK, top).transpose(2, 0, 1, 3, 4)
    bi = jnp.arange(B)[:, None, None, None]
    hi = jnp.arange(MOBA_HEADS)[None, :, None, None]
    sl4 = slopes[None, :, None, None]
    sl5 = slopes[None, :, None, None, None]
    koff = jnp.arange(MOBA_BLOCK)

    def chunk(args):
        c, qc, ic = args
        qpos = c * MOBA_QCHUNK + jnp.arange(MOBA_QCHUNK)
        own = (c * MOBA_QCHUNK) // MOBA_BLOCK
        qf = qc.astype(jnp.float32)
        kg = kbl[bi, hi, ic].astype(jnp.float32)
        vg = vbl[bi, hi, ic].astype(jnp.float32)
        ls = jnp.einsum('bhqd,bhqjkd->bhqjk', qf, kg) * ATTN_SCALE
        kpos_sel = ic[..., None] * MOBA_BLOCK + koff
        dist_sel = (qpos[None, None, :, None, None] - kpos_sel).astype(jnp.float32)
        valid = jnp.arange(top)[None, :] < (qpos // MOBA_BLOCK)[:, None]
        ls = jnp.where(valid[None, None, :, :, None], ls - sl5 * dist_sel, -jnp.inf)
        kown = lax.dynamic_index_in_dim(kbl, own, axis=2, keepdims=False).astype(jnp.float32)
        vown = lax.dynamic_index_in_dim(vbl, own, axis=2, keepdims=False).astype(jnp.float32)
        lo = jnp.einsum('bhqd,bhkd->bhqk', qf, kown) * ATTN_SCALE
        dist_own = qpos[:, None] - (own * MOBA_BLOCK + koff)[None, :]
        lo = jnp.where(dist_own >= 0, lo - sl4 * dist_own.astype(jnp.float32), -jnp.inf)
        logits = jnp.concatenate([ls.reshape(B, MOBA_HEADS, MOBA_QCHUNK, top * MOBA_BLOCK), lo], axis=-1)
        p = jax.nn.softmax(logits, axis=-1)
        ps = p[..., :top * MOBA_BLOCK].reshape(B, MOBA_HEADS, MOBA_QCHUNK, top, MOBA_BLOCK)
        po = p[..., top * MOBA_BLOCK:]
        return (jnp.einsum('bhqjk,bhqjkd->bhqd', ps, vg)
                + jnp.einsum('bhqk,bhkd->bhqd', po, vown))

    out = lax.map(chunk, (jnp.arange(nch), q_ch, idx_ch))
    out = out.transpose(1, 0, 3, 2, 4).reshape(B, sp, MOBA_HEADS * HEAD_DIM)[:, :S]
    return out.astype(q.dtype)

def hybrid_mixer(x, w_in, sinks, conv_w, w_br_a, w_br_b, w_br_c, w_out):
    B, S = x.shape[0], x.shape[1]
    proj = jnp.einsum('bsd,de->bse', x, w_in)
    a_q, a_k, a_v, b_h, b_b, b_c, c_q, c_k, c_v, g_a, g_b, g_c = jnp.split(proj, PROJ_SPLITS, axis=-1)
    slopes_a, slopes_c = alibi_slopes()
    y_a = sliding_window_attention(
        a_q.reshape(B, S, SWA_HEADS, HEAD_DIM),
        a_k.reshape(B, S, SWA_KV_HEADS, HEAD_DIM),
        a_v.reshape(B, S, SWA_KV_HEADS, HEAD_DIM), sinks, slopes_a)
    y_b = gated_short_conv(b_h, b_b, b_c, conv_w)
    y_c = moba_attention(
        c_q.reshape(B, S, MOBA_HEADS, HEAD_DIM),
        c_k.reshape(B, S, MOBA_HEADS, HEAD_DIM),
        c_v.reshape(B, S, MOBA_HEADS, HEAD_DIM), slopes_c)
    merged = (jax.nn.sigmoid(g_a) * (y_a @ w_br_a)
              + jax.nn.sigmoid(g_b) * (y_b @ w_br_b)
              + jax.nn.sigmoid(g_c) * (y_c @ w_br_c))
    return merged @ w_out

def swiglu(x, w_gate, w_up, w_down):
    return (jax.nn.silu(x @ w_gate) * (x @ w_up)) @ w_down

def first_inputs(seed: int = 0) -> dict:
    key = jax.random.key(seed)
    ks = jax.random.split(key, 16)
    f32 = jnp.float32
    nrm = lambda k, shape, s: jax.random.normal(k, shape, f32) * s
    L = DEPTH
    br_in = SWA_HEADS * HEAD_DIM
    return {
        'x': jax.random.normal(ks[0], (BATCH, SEQ, D_MODEL), f32),
        'w_in': nrm(ks[1], (L, D_MODEL, PROJ_WIDTH), D_MODEL ** -0.5),
        'attn_sinks': nrm(ks[2], (L, SWA_HEADS), 0.5),
        'conv_w': nrm(ks[3], (L, SC_KSIZE, SC_WIDTH), SC_KSIZE ** -0.5),
        'w_branch_a': nrm(ks[4], (L, br_in, D_MODEL), br_in ** -0.5 * BETA),
        'w_branch_b': nrm(ks[5], (L, SC_WIDTH, D_MODEL), SC_WIDTH ** -0.5 * BETA),
        'w_branch_c': nrm(ks[6], (L, MOBA_HEADS * HEAD_DIM, D_MODEL), (MOBA_HEADS * HEAD_DIM) ** -0.5 * BETA),
        'w_out': nrm(ks[7], (L, D_MODEL, D_MODEL), D_MODEL ** -0.5 * BETA),
        'ln1_g': 1.0 + nrm(ks[8], (L, D_MODEL), 0.02),
        'ln1_b': nrm(ks[9], (L, D_MODEL), 0.02),
        'w_ffn_gate': nrm(ks[10], (L, D_MODEL, FFN_HIDDEN), D_MODEL ** -0.5 * BETA),
        'w_ffn_up': nrm(ks[11], (L, D_MODEL, FFN_HIDDEN), D_MODEL ** -0.5 * BETA),
        'w_ffn_down': nrm(ks[12], (L, FFN_HIDDEN, D_MODEL), FFN_HIDDEN ** -0.5 * BETA),
        'ln2_g': 1.0 + nrm(ks[13], (L, D_MODEL), 0.02),
        'ln2_b': nrm(ks[14], (L, D_MODEL), 0.02),
    }

def first_block(x, w_in, attn_sinks, conv_w, w_branch_a, w_branch_b, w_branch_c, w_out,
              ln1_g, ln1_b, w_ffn_gate, w_ffn_up, w_ffn_down, ln2_g, ln2_b):
    for l in range(DEPTH):
        mix = hybrid_mixer(x, w_in[l], attn_sinks[l], conv_w[l], w_branch_a[l],
                           w_branch_b[l], w_branch_c[l], w_out[l])
        x = layer_norm(ALPHA * x + mix, ln1_g[l], ln1_b[l])
        ffn = swiglu(x, w_ffn_gate[l], w_ffn_up[l], w_ffn_down[l])
        x = layer_norm(ALPHA * x + ffn, ln2_g[l], ln2_b[l])
    return x


GRID_W = 64
CTX_LEN = 256
N_MIXERS = 2
N_A_LAYERS = (DEPTH + 1) // 2
N_B_LAYERS = DEPTH // 2
CHUNK = 64
EPS = 1e-6
N_MOD = 6
A_HEADS = 8
A_DK = D_MODEL // 16
A_DV = D_MODEL // 8
A_PROJ = 2 * A_HEADS * A_DK + 2 * A_HEADS * A_DV + 4 * A_HEADS
CONV_W = 5
B_HEADS = 8
B_DK = D_MODEL // B_HEADS
B_DV = D_MODEL // B_HEADS
B_PROJ = 2 * B_HEADS * B_DK + 2 * B_HEADS * B_DV
ROPE_BASE = 10000.0
N_EXPERTS = 16
EXPERT_FF = D_MODEL
CAPACITY_FACTOR = 2


def rmsnorm(x, g):
    xf = x.astype(jnp.float32)
    y = xf * lax.rsqrt(jnp.mean(xf * xf, axis=-1, keepdims=True) + EPS)
    return (y * g.astype(jnp.float32)).astype(x.dtype)

def modulate(h, shift, scale):
    return h * (1 + scale) + shift

def heads(a, n_heads):
    b, t, _ = a.shape
    return a.reshape(b, t, n_heads, -1).transpose(0, 2, 1, 3)

def dwconv_centred(x, w, b):
    pad = CONV_W // 2
    y = lax.conv_general_dilated(x, w[:, None, :].astype(x.dtype), window_strides=(1,),
                                 padding=[(pad, pad)], dimension_numbers=('NWC', 'WIO', 'NWC'),
                                 feature_group_count=x.shape[-1])
    return y + b.astype(x.dtype)

def to_chunks(a):
    b, h, t = a.shape[:3]
    return jnp.moveaxis(a.reshape(b, h, t // CHUNK, CHUNK, *a.shape[3:]), 2, 0)

def from_chunks(a):
    nc, b, h, l = a.shape[:4]
    return jnp.moveaxis(a, 0, 2).reshape(b, h, nc * l, *a.shape[4:])

def mlstm_scan(q, k, v, ig, lf, state):
    tril = jnp.tril(jnp.ones((CHUNK, CHUNK), bool))

    def step(carry, inp):
        C, n, m = carry
        qc, kc, vc, ic, fc = inp
        b = jnp.cumsum(fc, axis=-1)
        dmat = jnp.where(tril, b[..., :, None] - b[..., None, :] + ic[..., None, :], -jnp.inf)
        inter = b + m[..., None]
        m_row = jnp.maximum(inter, dmat.max(-1))
        s = jnp.einsum('bhid,bhjd->bhij', qc, kc) * jnp.exp(dmat - m_row[..., None])
        w_inter = jnp.exp(inter - m_row)
        num = jnp.einsum('bhij,bhjv->bhiv', s, vc) + w_inter[..., None] * jnp.einsum('bhid,bhdv->bhiv', qc, C)
        den = s.sum(-1) + w_inter * jnp.einsum('bhid,bhd->bhi', qc, n)
        h = num / jnp.maximum(jnp.abs(den), jnp.exp(-m_row))[..., None]
        b_last = b[..., -1]
        gk = b_last[..., None] - b + ic
        m_new = jnp.maximum(b_last + m, gk.max(-1))
        wk = jnp.exp(gk - m_new[..., None])
        wc = jnp.exp(b_last + m - m_new)
        C_new = wc[..., None, None] * C + jnp.einsum('bhj,bhjd,bhjv->bhdv', wk, kc, vc)
        n_new = wc[..., None] * n + jnp.einsum('bhj,bhjd->bhd', wk, kc)
        return (C_new, n_new, m_new), h

    xs = tuple(to_chunks(a) for a in (q, k, v, ig, lf))
    state, h = lax.scan(step, state, xs)
    return from_chunks(h), state

def retention_scan(q, k, v, logg, S):
    idx = jnp.arange(CHUNK, dtype=jnp.float32)
    tril = jnp.tril(jnp.ones((CHUNK, CHUNK), bool))
    diff = jnp.where(tril, idx[:, None] - idx[None, :], 0.0)
    dmat = jnp.where(tril, jnp.exp(diff * logg[:, None, None]), 0.0)
    inter = jnp.exp((idx + 1.0) * logg[:, None])
    kdec = jnp.exp((CHUNK - 1.0 - idx) * logg[:, None])
    sdec = jnp.exp(CHUNK * logg)

    def step(S, inp):
        qc, kc, vc = inp
        o = jnp.einsum('bhij,bhjv->bhiv', jnp.einsum('bhid,bhjd->bhij', qc, kc) * dmat, vc) \
            + inter[..., None] * jnp.einsum('bhid,bhdv->bhiv', qc, S)
        S_new = sdec[:, None, None] * S + jnp.einsum('hj,bhjd,bhjv->bhdv', kdec, kc, vc)
        return S_new, o

    xs = tuple(to_chunks(a) for a in (q, k, v))
    S, o = lax.scan(step, S, xs)
    return from_chunks(o), S

def run_bidirectional(scan_f, scan_b, ctx_f, lat_f, ctx_b, lat_b, state0):
    flip = lambda t: tuple(jnp.flip(a, 2) for a in t)
    oc_f, s = scan_f(ctx_f, state0)
    ol_f, _ = scan_f(lat_f, s)
    oc_b, s = scan_b(flip(ctx_b), state0)
    ol_b, _ = scan_b(flip(lat_b), s)
    return oc_f + jnp.flip(oc_b, 2), ol_f + jnp.flip(ol_b, 2)

def mlstm_mixer(h_ctx, h_lat, w_in, conv_w, conv_b, ig_b, fg_b, norm_g, w_out, need_ctx_out):
    nq = A_HEADS * A_DK
    nv = A_HEADS * A_DV
    f32 = jnp.float32

    def project(h):
        bn, t, _ = h.shape
        p = h @ w_in
        qk = jax.nn.silu(dwconv_centred(p[..., :2 * nq], conv_w, conv_b)).astype(f32)
        q = heads(qk[..., :nq], A_HEADS) * (A_DK ** -0.5)
        k = heads(qk[..., nq:], A_HEADS)
        v = heads(p[..., 2 * nq:2 * nq + nv].astype(f32), A_HEADS)
        o = p[..., 2 * nq + nv:2 * nq + 2 * nv]
        g = p[..., 2 * nq + 2 * nv:].astype(f32)
        ig = g[..., :2 * A_HEADS].reshape(bn, t, 2, A_HEADS) + ig_b.astype(f32)
        lf = jax.nn.log_sigmoid(g[..., 2 * A_HEADS:].reshape(bn, t, 2, A_HEADS) + fg_b.astype(f32))
        ig = jnp.transpose(ig, (0, 2, 3, 1))
        lf = jnp.transpose(lf, (0, 2, 3, 1))
        fwd = (q, k, v, ig[:, 0], lf[:, 0])
        bwd = (q, k, v, ig[:, 1], lf[:, 1])
        return fwd, bwd, o

    cf, cb, o_ctx = project(h_ctx)
    lf_, lb, o_lat = project(h_lat)
    bn = h_lat.shape[0]
    state0 = (jnp.zeros((bn, A_HEADS, A_DK, A_DV), f32), jnp.zeros((bn, A_HEADS, A_DK), f32),
              jnp.zeros((bn, A_HEADS), f32))
    scan = lambda args, s: mlstm_scan(*args, s)
    y_ctx, y_lat = run_bidirectional(scan, scan, cf, lf_, cb, lb, state0)

    def finish(y, o):
        b_, h_, t_, d_ = y.shape
        y = jnp.transpose(y, (0, 2, 1, 3))
        y = y * lax.rsqrt(jnp.mean(y * y, axis=-1, keepdims=True) + EPS)
        y = y.reshape(b_, t_, h_ * d_) * norm_g.astype(f32) * jax.nn.sigmoid(o.astype(f32))
        return y.astype(o.dtype) @ w_out

    out_ctx = finish(y_ctx, o_ctx) if need_ctx_out else None
    return out_ctx, finish(y_lat, o_lat)

def rope_angles(t):
    rows = t // GRID_W
    r = jnp.broadcast_to(jnp.arange(rows, dtype=jnp.float32)[:, None], (rows, GRID_W)).reshape(-1)
    col = jnp.broadcast_to(jnp.arange(GRID_W, dtype=jnp.float32)[None, :], (rows, GRID_W)).reshape(-1)
    nf = B_DK // 4
    inv = ROPE_BASE ** (-jnp.arange(nf, dtype=jnp.float32) / nf)
    return r[:, None] * inv, col[:, None] * inv

def rope(x, ang):
    x1, x2 = jnp.split(x, 2, axis=-1)
    cos, sin = jnp.cos(ang), jnp.sin(ang)
    return jnp.concatenate([x1 * cos - x2 * sin, x1 * sin + x2 * cos], axis=-1)

def rope2d(x, ang_r, ang_c):
    half = B_DK // 2
    return jnp.concatenate([rope(x[..., :half], ang_r), rope(x[..., half:], ang_c)], axis=-1)

def retention_mixer(h_ctx, h_lat, w_in, decay_logit, gn_g, w_out, need_ctx_out):
    n = B_HEADS * B_DK
    f32 = jnp.float32

    def project(h, angles):
        p = h @ w_in
        q = heads(p[..., :n].astype(f32), B_HEADS)
        k = heads(p[..., n:2 * n].astype(f32), B_HEADS) * (B_DK ** -0.5)
        v = heads(p[..., 2 * n:3 * n].astype(f32), B_HEADS)
        g = p[..., 3 * n:]
        if angles is not None:
            q = rope2d(q, *angles)
            k = rope2d(k, *angles)
        return (q, k, v), g

    c_args, g_ctx = project(h_ctx, None)
    l_args, g_lat = project(h_lat, rope_angles(h_lat.shape[1]))
    logg = jax.nn.log_sigmoid(decay_logit.astype(f32))
    bn = h_lat.shape[0]
    state0 = jnp.zeros((bn, B_HEADS, B_DK, B_DV), f32)
    scan_f = lambda args, s: retention_scan(*args, logg[0], s)
    scan_b = lambda args, s: retention_scan(*args, logg[1], s)
    y_ctx, y_lat = run_bidirectional(scan_f, scan_b, c_args, l_args, c_args, l_args, state0)

    def finish(y, g):
        b_, h_, t_, d_ = y.shape
        y = jnp.transpose(y, (0, 2, 1, 3))
        mu = jnp.mean(y, axis=-1, keepdims=True)
        var = jnp.mean(jnp.square(y - mu), axis=-1, keepdims=True)
        y = ((y - mu) * lax.rsqrt(var + EPS)).reshape(b_, t_, h_ * d_) * gn_g.astype(f32)
        y = y * jax.nn.silu(g.astype(f32))
        return y.astype(g.dtype) @ w_out

    out_ctx = finish(y_ctx, g_ctx) if need_ctx_out else None
    return out_ctx, finish(y_lat, g_lat)

def expert_choice_ffn(h, router, w_gate, w_up, w_down):
    bn, t, _ = h.shape
    cap = CAPACITY_FACTOR * t // N_EXPERTS
    aff = jax.nn.softmax(h.astype(jnp.float32) @ router.astype(jnp.float32), axis=-1)
    gate, idx = lax.top_k(jnp.swapaxes(aff, 1, 2), cap)
    bidx = jnp.arange(bn)[:, None, None]
    xs = h[bidx, idx]
    hid = jax.nn.silu(jnp.einsum('becd,edf->becf', xs, w_gate)) * jnp.einsum('becd,edf->becf', xs, w_up)
    y = jnp.einsum('becf,efd->becd', hid, w_down) * gate[..., None].astype(h.dtype)
    return jnp.zeros_like(h).at[bidx, idx].add(y)

def second_inputs(seed: int = 0) -> dict:
    key = jax.random.key(seed)
    ks = jax.random.split(key, 24)
    f32 = jnp.float32
    D = D_MODEL
    nqk = 2 * A_HEADS * A_DK
    nrm = lambda k, shape, s: jax.random.normal(k, shape, f32) * s
    fbase = jnp.linspace(3.0, 6.0, A_HEADS, dtype=f32)
    dbase = jnp.log(2.0 ** (5.0 + jnp.arange(B_HEADS, dtype=f32)) - 1.0)
    return {
        "x": nrm(ks[0], (BATCH, SEQ, D), 1.0),
        "c": nrm(ks[1], (BATCH, D), 1.0),
        "ctx": nrm(ks[2], (BATCH, CTX_LEN, D), 1.0),
        "c_ctx": nrm(ks[3], (D,), 1.0),
        "ada_w": nrm(ks[4], (DEPTH, D, N_MOD * D), 0.5 * D ** -0.5),
        "ada_b": nrm(ks[5], (DEPTH, N_MOD * D), 0.02),
        "norm_mix_g": 1.0 + nrm(ks[6], (DEPTH, D), 0.02),
        "norm_ffn_g": 1.0 + nrm(ks[7], (DEPTH, D), 0.02),
        "final_norm_g": 1.0 + nrm(ks[8], (D,), 0.02),
        "mlstm_w_in": nrm(ks[9], (N_A_LAYERS, D, A_PROJ), D ** -0.5),
        "mlstm_conv_w": nrm(ks[10], (N_A_LAYERS, CONV_W, nqk), CONV_W ** -0.5),
        "mlstm_conv_b": nrm(ks[11], (N_A_LAYERS, nqk), 0.02),
        "mlstm_igate_b": nrm(ks[12], (N_A_LAYERS, 2, A_HEADS), 0.1),
        "mlstm_fgate_b": fbase + nrm(ks[13], (N_A_LAYERS, 2, A_HEADS), 0.1),
        "mlstm_head_norm_g": 1.0 + nrm(ks[14], (N_A_LAYERS, A_HEADS * A_DV), 0.02),
        "mlstm_w_out": nrm(ks[15], (N_A_LAYERS, A_HEADS * A_DV, D), (A_HEADS * A_DV) ** -0.5),
        "ret_w_in": nrm(ks[16], (N_B_LAYERS, D, B_PROJ), D ** -0.5),
        "ret_decay_logit": dbase + nrm(ks[17], (N_B_LAYERS, 2, B_HEADS), 0.1),
        "ret_group_norm_g": 1.0 + nrm(ks[18], (N_B_LAYERS, B_HEADS * B_DV), 0.02),
        "ret_w_out": nrm(ks[19], (N_B_LAYERS, B_HEADS * B_DV, D), (B_HEADS * B_DV) ** -0.5),
        "moe_router": nrm(ks[20], (DEPTH, D, N_EXPERTS), D ** -0.5),
        "moe_w_gate": nrm(ks[21], (DEPTH, N_EXPERTS, D, EXPERT_FF), D ** -0.5),
        "moe_w_up": nrm(ks[22], (DEPTH, N_EXPERTS, D, EXPERT_FF), D ** -0.5),
        "moe_w_down": nrm(ks[23], (DEPTH, N_EXPERTS, EXPERT_FF, D), EXPERT_FF ** -0.5),
    }

def second_block(x, c, ctx, c_ctx, ada_w, ada_b, norm_mix_g, norm_ffn_g, final_norm_g,
              mlstm_w_in, mlstm_conv_w, mlstm_conv_b, mlstm_igate_b, mlstm_fgate_b,
              mlstm_head_norm_g, mlstm_w_out, ret_w_in, ret_decay_logit, ret_group_norm_g,
              ret_w_out, moe_router, moe_w_gate, moe_w_up, moe_w_down):
    c_lat = jax.nn.silu(c)[:, None, :]
    c_con = jax.nn.silu(c_ctx)[None, None, :]
    for i in range(DEPTH):
        last = i == DEPTH - 1
        mod_l = jnp.split(c_lat @ ada_w[i] + ada_b[i], N_MOD, axis=-1)
        mod_c = jnp.split(c_con @ ada_w[i] + ada_b[i], N_MOD, axis=-1)
        h_lat = modulate(rmsnorm(x, norm_mix_g[i]), mod_l[0], mod_l[1])
        h_ctx = modulate(rmsnorm(ctx, norm_mix_g[i]), mod_c[0], mod_c[1])
        j = i // N_MIXERS
        if i % N_MIXERS == 0:
            o_ctx, o_lat = mlstm_mixer(h_ctx, h_lat, mlstm_w_in[j], mlstm_conv_w[j], mlstm_conv_b[j],
                                       mlstm_igate_b[j], mlstm_fgate_b[j], mlstm_head_norm_g[j],
                                       mlstm_w_out[j], not last)
        else:
            o_ctx, o_lat = retention_mixer(h_ctx, h_lat, ret_w_in[j], ret_decay_logit[j],
                                           ret_group_norm_g[j], ret_w_out[j], not last)
        x = x + mod_l[2] * o_lat
        h_lat = modulate(rmsnorm(x, norm_ffn_g[i]), mod_l[3], mod_l[4])
        x = x + mod_l[5] * expert_choice_ffn(h_lat, moe_router[i], moe_w_gate[i], moe_w_up[i], moe_w_down[i])
        if not last:
            ctx = ctx + mod_c[2] * o_ctx
            h_ctx = modulate(rmsnorm(ctx, norm_ffn_g[i]), mod_c[3], mod_c[4])
            ctx = ctx + mod_c[5] * expert_choice_ffn(h_ctx, moe_router[i], moe_w_gate[i], moe_w_up[i], moe_w_down[i])
    return rmsnorm(x, final_norm_g)


def setup_inputs(seed=0):
    out = dict(first_inputs(seed))
    for name, value in second_inputs(seed + 1).items():
        if name != "x":
            out[name + "_2"] = value
    return out


def reference(
    x, w_in, attn_sinks, conv_w, w_branch_a, w_branch_b, w_branch_c, w_out, ln1_g, ln1_b,
    w_ffn_gate, w_ffn_up, w_ffn_down, ln2_g, ln2_b, c_2, ctx_2, c_ctx_2, ada_w_2, ada_b_2,
    norm_mix_g_2, norm_ffn_g_2, final_norm_g_2, mlstm_w_in_2, mlstm_conv_w_2, mlstm_conv_b_2,
    mlstm_igate_b_2, mlstm_fgate_b_2, mlstm_head_norm_g_2, mlstm_w_out_2, ret_w_in_2,
    ret_decay_logit_2, ret_group_norm_g_2, ret_w_out_2, moe_router_2, moe_w_gate_2, moe_w_up_2,
    moe_w_down_2,
):
    x = first_block(
        x, w_in, attn_sinks, conv_w, w_branch_a, w_branch_b, w_branch_c, w_out, ln1_g, ln1_b,
        w_ffn_gate, w_ffn_up, w_ffn_down, ln2_g, ln2_b,
    )
    return second_block(
        x, c_2, ctx_2, c_ctx_2, ada_w_2, ada_b_2, norm_mix_g_2, norm_ffn_g_2, final_norm_g_2,
        mlstm_w_in_2, mlstm_conv_w_2, mlstm_conv_b_2, mlstm_igate_b_2, mlstm_fgate_b_2,
        mlstm_head_norm_g_2, mlstm_w_out_2, ret_w_in_2, ret_decay_logit_2, ret_group_norm_g_2,
        ret_w_out_2, moe_router_2, moe_w_gate_2, moe_w_up_2, moe_w_down_2,
    )


_drawn_inputs = setup_inputs


def setup_inputs(seed=0):
    import zlib

    import numpy as np

    out = dict(_drawn_inputs(seed))
    spreads = {}
    factors = {'attn_sinks': 8.0,
     'norm_mix_g_2': 5.526,
     'norm_ffn_g_2': 5.124,
     'final_norm_g_2': 2.714,
     'mlstm_conv_b_2': 8.0,
     'mlstm_igate_b_2': 8.0,
     'mlstm_head_norm_g_2': 8.0,
     'ret_group_norm_g_2': 8.0}
    for name, (base, spread) in spreads.items():
        noise = np.random.default_rng([zlib.crc32(name.encode()), seed]).standard_normal(out[name].shape)
        drawn = base * np.exp(spread * noise) if base else spread * noise
        out[name] = jnp.asarray(drawn.astype(out[name].dtype))
    for name, factor in factors.items():
        out[name] = (out[name] * factor).astype(out[name].dtype)
    return out
```

```python
import concourse.bass as bass
from concourse import mybir
from contextlib import ExitStack

F32 = mybir.dt.float32
U32 = mybir.dt.uint32
ALU = mybir.AluOpType
ACT = mybir.ActivationFunctionType
X_AXIS = mybir.AxisListType.X

P = 128
D = 1024
KT = D // P
SEQ = 256
TT = SEQ // P
DEPTH = 2
ALPHA = (2 * DEPTH) ** 0.25
LN_EPS = 1e-5
RMS_EPS = 1e-6
HEADS = 8
HD = 64
SCALE = HD ** -0.5
SLOPES = [2.0 ** (-8.0 * (i + 1.0) / 16) for i in range(16)]
HALF = 512
HIDDEN = 2816
FFN_TILES = HIDDEN // P
RING = 6
PANEL = 4096
EXPERTS = 16
SLOTS = 32
BANKS = 8
COLS = {}
_at = 0
for _name, _n in (("a_q", 512), ("a_k", 128), ("a_v", 128), ("b_h", 512), ("b_b", 512), ("b_c", 512),
                  ("c_q", 512), ("c_k", 512), ("c_v", 512), ("g_a", D), ("g_b", D), ("g_c", D)):
    COLS[_name] = _at
    _at += _n


class BankPlan:
    REL, EV = "rel", "ev"

    def __init__(self):
        self.events, self.panels = 0, 0
        self.used = [0] * BANKS
        self.units, self.release, self.stage_panels = {}, {}, {}

    def plan(self, stage, entries, times=1):
        here, ev, n, pan = [0] * BANKS, 0, 0, []
        units = []
        for e in entries:
            if e == self.REL:
                pan.append(ev)
            elif e == self.EV:
                ev += 1
                pan.append(ev)
            else:
                ev += 1
                b = n % BANKS
                units.append((e, b, ev, here[b]))
                here[b] += 1
                n += 1
        for e, b, v, u in units:
            assert (stage, e) not in self.units, (stage, e)
            self.units[stage, e] = (b, self.events + v, ev, self.used[b] + u, here[b])
        self.stage_panels[stage] = (self.panels, len(pan))
        for i in range(times):
            for m, v in enumerate(pan):
                self.release[self.panels + i * len(pan) + m] = (self.events + i * ev + v, ev, len(pan))
        self.panels += len(pan) * times
        self.events += ev * times
        self.used = [a + h * times for a, h in zip(self.used, here)]

    def bank(self, stage, key):
        return self.units[stage, key][0]

    def full(self, stage, key, i=0):
        _, v, per, _, _ = self.units[stage, key]
        return i * per + v

    def free(self, stage, key, i=0):
        _, _, _, u, per = self.units[stage, key]
        return i * per + (u + 1)

    def emptied(self, stage, key, i=0):
        _, _, _, u, per = self.units[stage, key]
        return i * per + (u + 2)


class Chain:

    def __init__(self, eng, sem):
        self.eng, self.sem, self.n, self.off = eng, sem, 0, 0

    def __call__(self, ins):
        ins.then_inc(self.sem, 1)
        self.n += 1
        self.eng.wait_ge(self.sem, self.off + self.n)

    def enter(self, i, per):
        self.start, self.off, self.per = self.n, i * per, per

    def leave(self, times):
        got = self.n - self.start
        assert got == self.per, f"steps in the loop: {got}, not {self.per}"
        self.n = self.start + self.per * times
        self.off = 0


def view(ap, *dims):
    names = "abcd"[:len(dims)]
    return ap.rearrange(f"p ({' '.join(names)}) -> p {' '.join(names)}", **dict(zip(names[1:], dims[1:])))


def spread(ap, n):
    return ap.unsqueeze(2).to_broadcast([ap.shape[0], ap.shape[1], n])
BLOCK1_ONLY = False
OUT_STORES = 2
DVE_LAYER = 36


STREAMS = 2
CTX, LAT = 0, 1
DV = D // HEADS
CONV_TAPS = 5
GROUPS = EXPERTS // 4


def fwd_col(jt, it):
    return (0, 512, 896, 1152)[jt] + P * (it - jt)


def bwd_col(jt, it):
    return {(0, 0): 0, (0, 2): 128, (0, 3): 256, (1, 0): 384, (1, 1): 512, (1, 2): 640, (1, 3): 768,
            (2, 2): 896, (3, 2): 1024, (3, 3): 1152}[jt, it]


SEEN = [[(0,), (0, 1), (0, 1, 2), (0, 1, 2, 3)], [(0, 1), (1,), (0, 1, 2, 3), (0, 1, 3)]]
COL = [fwd_col, bwd_col]


BESIDE0 = {0: [("o", 0, t) for t in range(4)], 1: [("v", 1, 0), ("v", 1, 1)], 2: [("v", 1, 2), ("v", 1, 3)],
           3: [("o", 1, 0), ("o", 1, 1)], 4: [("o", 1, 2), ("o", 1, 3)]}
BESIDE1 = {0: [("v", 1, 0), ("v", 1, 1)], 1: [("v", 1, 2), ("v", 1, 3)], 2: [("g", 0, 2), ("g", 0, 3)],
           4: [("g", 1, 2), ("g", 1, 3)]}


def streams_of(layer):
    return (CTX, LAT) if layer == 0 else (LAT,)


def plan_second(banks):
    R = BankPlan.REL
    hT = [("hT", k) for k in range(KT)]
    mix0 = list(hT)
    mix0 += [("qk", m) for m in range(4)] + [R] + [("qk", m) for m in range(4, 8)] + [R] + [("gr",)]
    mix0 += [("v", 0, t) for t in range(4)] + [R, ("aT",)]
    for h in range(HEADS + 1):
        if h < HEADS:
            mix0 += [("mb", h, 0), ("mb", h, 1), ("s", h, 0), ("s", h, 1), ("s", h, 2)]
        for key in BESIDE0.get(h, ()):
            mix0 += [key] + [R] * (key[2] == 3)
        if h:
            mix0 += [("h", h - 1, i) for i in range(4)]
    mix0 += [("gbc", s, n) for s in (CTX, LAT) for n in range(2)] + [("yT", k) for k in range(KT)]
    for n in range(2):
        mix0 += [("wo", n, t) for t in range(4)] + [R]
    banks.plan("mix0", mix0)
    for m in range(2):
        banks.release[banks.stage_panels["mix0"][0] + m] = (banks.full("mix0", ("h", HEADS - 1, 3)), 0, 0)
    plan_moe(banks, 0)
    mix1 = list(hT)
    for n in range(2):
        mix1 += [("q", n, 0), ("q", n, 1), R, ("qs", n, 0), ("qs", n, 1)]
    for n in range(2):
        mix1 += [("k", 4 * n + m) for m in range(4)] + [R] + [("ks", 2 * n), ("ks", 2 * n + 1)]
    mix1 += [("v", 0, t) for t in range(4)] + [R]
    for h in range(HEADS + 1):
        if h < HEADS:
            mix1 += [("s", h, 0), ("s", h, 1)]
        for key in BESIDE1.get(h, ()):
            mix1 += [key] + [R] * (key[2] == 3)
        if h:
            mix1 += [("o", h - 1)]
    mix1 += [("gbc", LAT, n) for n in range(2)] + [("yT", m) for m in range(4)]
    for n in range(2):
        mix1 += [("wo", n, 2), ("wo", n, 3), R]
    banks.plan("mix1", mix1)
    banks.release[banks.stage_panels["mix1"][0] + 2] = (banks.full("mix1", ("o", HEADS - 1)), 0, 0)
    plan_moe(banks, 1)


def plan_moe(banks, layer):
    R = BankPlan.REL
    src = streams_of(layer)
    moe = [("hT", k) for k in range(KT)] + [("lg",), ("afT",)] + [("idx", s) for s in src]
    moe += [("xs", k, s) for k in range(KT) for s in src] + [("gbc", s, n) for s in src for n in range(2)]
    moe += [("it",), ("rep",)]
    banks.plan(f"moe{layer}", moe)
    per = []
    for q in range(4):
        per += [("g", q), R, R, ("u", q), R, R, ("t", q), ("y", q), R, R]
    per += [("c", s, t, n) for s in src for t in range(TT) for n in range(2)]
    banks.plan(f"exp{layer}", per, GROUPS)


def second_block(nc, ctx, banks, I, K, out, S):
    def sb(name, shape, dt=F32):
        return ctx.enter_context(nc.sbuf_tensor(name, shape, dt))

    def sem(name):
        return ctx.enter_context(nc.semaphore(name))

    ring, arena, ht, x, c, lnp, const, st = (S[n] for n in ("ring", "arena", "ht", "x", "c", "lnp", "const", "st"))
    ident, swap_mat, iota, tok_col, quad = (S[n] for n in ("ident", "swap_mat", "iota", "tok_col", "quad"))
    later_key, earlier_key, par, par2 = (S[n] for n in ("later_key", "earlier_key", "par", "par2"))
    mods = [S["mods_0"], S["mods_now"]]
    psum, pe_done, panel_in = S["psum"], S["pe_done"], S["panel_in"]
    one_col, rep_mat = const[:, 774:775], const[0:32, 776:904]

    router = sb("router", [P, DEPTH, P])
    coef = view(st[:, 146:210], 4, STREAMS, KT)
    ss, rs = st[:, 0:4], st[:, 4:8]
    hT = view(ht[:, :], KT, 2 * SEQ)
    tokens = [c[:, 0, :], c[:, 1, :], x[:, 0, :], x[:, 1, :]]
    lflat = lnp[:, :, :].rearrange("p a b -> p (a b)")
    qk = view(arena[:, 0:4096], KT, 2 * SEQ)
    va = view(arena[:, 4096:8224], 4, HEADS, DV + 1)
    og = view(arena[:, 8224:12320], 4, D)
    qk_pad = view(arena[:, 12320:14400], 4, STREAMS, SEQ + 4)
    conv_acc = view(arena[:, 14400:15424], 2, STREAMS, SEQ)
    gate_rows = arena[:, 15424:15936]
    xh0 = view(arena[:, 8224:12320], 4, D)
    lf_rows, b_rows = arena[:, 12320:12832], arena[:, 12832:13344]
    one_rows, t_rows = arena[:, 13344:13856], arena[:, 13856:14368]
    m_diag = view(arena[:, 12832:13856], 2, HALF)
    yt = view(arena[:, 13856:14880], 2, 4, DV)
    wbuf = [[ring[:, m, 0:1280], ring[:, m, 1280:2560]] for m in range(2)]
    wg32, wg = view(arena[:, 15936:16192], KT, 32), view(lnp[:, 1, :], KT, P)
    m_neg = view(lnp[:, 1, :], 2, HALF)
    aT = view(ring[:, 0, 2560:2816], 4, 64)
    em = view(arena[:, 16160:16320], 4, 40)
    head_ss, r2 = view(st[:, 32:64], 4, HEADS), st[:, 64:72]
    gate_bias = st[:, 251:252]
    gb = view(ht[:, 0:2048], STREAMS, D)
    gate_diag = view(ht[:, 2048:3072], 2, 4, P)
    res_tmp = view(ht[:, 3072:4096], 2, HALF)
    xh = view(arena[:, 8192:12288], 4, D)
    xs = arena[:, 0:8192]
    y_four = view(arena[:, 8192:10240], STREAMS, D)
    gb_moe = view(arena[:, 10240:12288], STREAMS, D)
    back_now = view(arena[:, 15360:15872], STREAMS, SEQ)
    pick = view(ht[:, 0:2048], STREAMS, TT, HALF)
    spread_back = view(ht[:, 2048:4096], STREAMS, GROUPS, SEQ)
    x_exp = view(ht[:, 0:1024], 2, KT * 64)
    sil_e = view(ht[:, 1024:2048], 2, HALF)
    hid_e, hidT = view(lflat[:, 0:1024], 2, HALF), view(lflat[:, 1024:2048], 2, HALF)
    s0 = 12288
    logit, aff2 = arena[:, s0:s0 + 64], view(arena[:, s0 + 64:s0 + 192], TT, 64)
    lmax = arena[:, s0 + 192:s0 + 196]
    aff_T, aff_work = arena[0:64, s0 + 256:s0 + 512], arena[0:64, s0 + 512:s0 + 768]
    top_val, top_idxf = arena[0:64, s0 + 768:s0 + 800], arena[0:64, s0 + 800:s0 + 832]
    top_idx = arena[0:64, s0 + 832:s0 + 864].bitcast(U32)
    block_idx = view(arena[0:64, s0 + 1024:s0 + 2048], STREAMS, HALF)
    sel_T = arena[0:32, s0 + 2048:s0 + 2176]
    sel_m = view(arena[:, s0 + 2176:s0 + 2208], STREAMS, GROUPS, 4)
    sel = view(arena[:, s0 + 2240:s0 + 2256], 2, STREAMS, GROUPS)
    qT, kT = view(arena[:, 0:2048], HEADS, SEQ), view(arena[:, 2048:6144], HEADS, 2 * SEQ)
    rv, rg = view(arena[:, 6144:10240], 4, D), view(arena[:, 10240:12288], TT, D)
    xh1 = view(arena[:, 12288:16384], 4, D)
    gaps = view(arena[:, 12288:14848], 5, HALF)
    rope_t = view(arena[:, 14848:15360], 2, SEQ)
    rot_a, rot_b = arena[:, 15360:15872], arena[:, 15872:16384]
    dec = view(ring[:, 4, :], 2, 4, HALF)
    ry = c[:, :, :]
    ryT = view(arena[:, 2048:4096], KT, SEQ)
    rsq = view(arena[:, 4096:6144], TT * HEADS, DV)
    logg, logg_t, mean = st[:, 80:96], st[:, 96:112], st[:, 128:144]
    var16 = st[:, 112:128]

    names = ("ctx_loaded", "gain_loaded", "wg_loaded", "gbias_clear", "gbias_loaded", "router_loaded", "ret_loaded",
             "decay_loaded", "gain_free", "squares_ready", "ms_ready", "rms_ready", "xh_ready", "conv_ready", "silu_ready",
             "wg_ready", "abs_ready", "softplus_ready", "rows_ready", "mdiag_ready", "exp_w_ready", "w_ready",
             "yt_ready", "head_ss_ready", "head_ms_ready", "head_rms_ready", "og_ready", "diag_ready", "streams_ready",
             "shift_ready", "aff_exp_ready", "aff_ready", "top_ready", "block_ready", "pick_ready", "back_ready",
             "x_exp_ready", "sil_e_ready", "raw_ready", "logg_abs_ready", "logg_sp_ready", "logg_ready", "decay_ready",
             "kt_ready", "final_ready", "inv_ready")
    Q = {n: sem(n) for n in names}

    def sync(sp, load_panel):
        n = [banks.stage_panels["mix0"][0]]

        def halves(src):
            v = src.rearrange("(h k p) n -> h p k n", h=2, p=P)
            return [(slice(4 * h, 4 * h + 4), v[h]) for h in range(2)]

        def load(width, parts):
            load_panel(n[0], width, parts)
            n[0] += 1

        def experts(layer):
            first = banks.stage_panels[f"exp{layer}"][0]
            assert first == n[0]
            w = [I[f"moe_w_{m}_2"] for m in ("gate", "up", "down")]
            per = 24

            def expert(q, e):
                for m in range(3):
                    for h in range(2):
                        slot = (first + 6 * q + 2 * m + h) % RING
                        src = w[m][layer, bass.ds(e, 1), :, :].rearrange("a k n -> (a k) n")
                        yield slot, 6 * q + 2 * m + h, (
                            (D, src[HALF * h:HALF * h + HALF, :].rearrange("(g k p) n -> g p k n", g=2, p=P)) if m == 2
                            else (HALF, src[:, HALF * h:HALF * h + HALF].rearrange("(g k p) n -> g p k n", g=2, p=P)))

            for q in range(4):
                for slot, m, (width, halves_) in expert(q, q):
                    k = PANEL // width // 2
                    load(width, [(slice(k * g, k * g + k), halves_[g]) for g in range(2)])
            with sp.Fori(1, GROUPS) as g4:
                for q in range(4):
                    for slot, m, (width, halves_) in expert(q, g4 * 4 + q):
                        if m >= RING:
                            v, ev, _ = banks.release[first + m - RING]
                            sp.wait_ge(pe_done, g4 * ev + v)
                        else:
                            v, ev, _ = banks.release[first + per + m - RING]
                            sp.wait_ge(pe_done, g4 * ev + (v - ev))
                        k = PANEL // width // 2
                        s_ = view(ring[:, slot, :], PANEL // width, width)
                        for g in range(2):
                            sp.dma_start(s_[:, k * g:k * g + k, :], halves_[g]).then_inc(panel_in[slot], 16)
            n[0] += per * (GROUPS - 1)

        wi = I["mlstm_w_in_2"][0]
        for m in (0, 1, 2, 4, 3, 5):
            load(HALF, halves(wi[:, HALF * m:HALF * m + HALF]))
        for m in range(2):
            load(HALF, halves(I["mlstm_w_out_2"][0][:, HALF * m:HALF * m + HALF]))
        experts(0)
        assert n[0] == banks.stage_panels["mix1"][0]
        for m in range(8):
            load(HALF, halves(I["ret_w_in_2"][0][:, HALF * m:HALF * m + HALF]))
        for m in range(2):
            load(HALF, halves(I["ret_w_out_2"][0][:, HALF * m:HALF * m + HALF]))
        experts(1)
        for t in range(TT):
            sp.wait_ge(Q["final_ready"], t + 1)
            sp.dma_start(out[0, P * t:P * t + P, :], x[:, t, :]).then_inc(S["out_stored"], 16)

    def gpsimd(pool):
        pool.dma_start(c[:, :, :], I["ctx_2"][0].rearrange("(t p) d -> p t d", p=P)).then_inc(Q["ctx_loaded"], 16)
        for l in range(DEPTH):
            pool.dma_start(view(router[:, l, :], KT, EXPERTS),
                           I["moe_router_2"][l].rearrange("(k p) e -> p k e", p=P)).then_inc(Q["router_loaded"], 16)
        pool.wait_ge(Q["gbias_clear"], 1)
        pool.dma_start(wg32, I["mlstm_w_in_2"][0][:, 3072:3104].rearrange("(k p) n -> p k n", p=P)).then_inc(Q["wg_loaded"], 16)
        for m, name in enumerate(("igate", "fgate")):
            for d in range(2):
                r = 64 * m + 32 * d
                pool.dma_start(gate_bias[r:r + 8, :], I[f"mlstm_{name}_b_2"][0, d].rearrange("(h a) -> h a", a=1)
                               ).then_inc(Q["gbias_loaded"], 16)
        pool.dma_start(lnp[:, 0, :], I["mlstm_head_norm_g_2"].to_broadcast([P, D])).then_inc(Q["gain_loaded"], 16)
        pool.wait_ge(Q["gain_free"], 1)
        pool.dma_start(lnp[:, 0, :], I["ret_group_norm_g_2"].to_broadcast([P, D])).then_inc(Q["gain_loaded"], 16)
        pool.dma_start(logg, I["ret_decay_logit_2"].rearrange("a b h -> a (b h)").to_broadcast([P, 16])
                       ).then_inc(Q["decay_loaded"], 16)
        pool.wait_ge(pe_done, banks.full("mix1", ("hT", KT - 1)))
        pool.dma_start(arena[:, 12288:14848], K["ret"]).then_inc(Q["ret_loaded"], 16)
        pool.dma_start(arena[:, 14848:15360], K["rope"]).then_inc(Q["ret_loaded"], 16)
        pool.wait_ge(Q["gain_free"], 2)
        pool.dma_start(lnp[:, 0, :], I["final_norm_g_2"].rearrange("(a d) -> a d", a=1).to_broadcast([P, D])
                       ).then_inc(Q["gain_loaded"], 16)

    def tensor(pe):
        mm, panel, state, transposes = nc.tensor.matmul, S["panel"], S["state"], S["transposes"]
        open_bank, wait_emptied = S["open_bank"], S["wait_emptied"]

        def norm_T(stage, n, src, tiles):
            pe.wait_ge(Q["xh_ready"], 2 * n)
            for k in range(KT):
                transposes(stage, ("hT", k), [src[:, t, P * k:P * k + P] for t in tiles])
            for k in range(KT):
                wait_emptied(pe, stage, ("hT", k))

        def project_wide(stage, keys, slot, rhs, n=2 * SEQ):
            for m, key in enumerate(keys):
                bank = open_bank(pe, stage, key)
                for k in range(KT):
                    last = mm(bank[:, 0:n], slot[:, k, P * m:P * m + P], rhs[:, k, :], start=k == 0, stop=k == KT - 1)
                last.then_inc(pe_done, 1)

        def project(stage, keys, slot, lhs):
            for t, key in keys:
                bank = open_bank(pe, stage, key)
                for k in range(KT):
                    last = mm(bank, lhs[:, k, P * t:P * t + P], slot[:, k, :], start=k == 0, stop=k == KT - 1)
                last.then_inc(pe_done, 1)

        def gate_rows_bcast(stage, src, first):
            for m, (s, n) in enumerate((s, n) for s in src for n in range(2)):
                bank = open_bank(pe, stage, ("gbc", s, n))
                pe.wait_ge(Q["diag_ready"], first + m + 1)
                mm(bank, one_col.to_broadcast([P, P]), gate_diag_of(stage)[:, m % 2].rearrange("p a b -> p (a b)"),
                   start=True, stop=True).then_inc(pe_done, 1)

        norm_T("mix0", 1, xh0, range(4))
        for n in range(2):
            project_wide("mix0", [("qk", 4 * n + m) for m in range(4)], panel(0, HALF), hT)
        bank = open_bank(pe, "mix0", ("gr",))
        pe.wait_ge(Q["wg_ready"], 1)
        for k in range(KT):
            last = mm(bank, wg[:, k, :], hT[:, k, :], start=k == 0, stop=k == KT - 1)
        last.then_inc(pe_done, 1)
        project("mix0", [(t, ("v", 0, t)) for t in range(4)], panel(0, HALF), hT)

        def beside(stage, keys):
            for key in keys:
                if key[2] == (2 if key[0] == "g" else 0):
                    state["beside"] = panel(0, HALF)
                project(stage, [(key[2], key)], state["beside"], hT)

        pe.wait_ge(Q["rows_ready"], 1)
        bank = open_bank(pe, "mix0", ("aT",))
        for m, rows in enumerate((gate_rows, b_rows)):
            for t in range(4):
                last = nc.tensor.transpose(bank[:, 256 * m + 64 * t:256 * m + 64 * t + 64], rows[0:64, P * t:P * t + P],
                                           ident[0:64, 0:64])
        last.then_inc(pe_done, 1)
        pe.wait_ge(Q["silu_ready"], 8)
        for h in range(HEADS + 1):
            if h in (1, 5):
                for t in range(4):
                    wait_emptied(pe, "mix0", ("v", h // 4, t))
            if h < HEADS:
                for d in range(2):
                    bank = open_bank(pe, "mix0", ("mb", h, d))
                    r = 32 * d + h
                    mm(bank, ident[0:64, r:r + 1].to_broadcast([64, P]), lf_rows[0:64, :], start=True,
                       stop=True).then_inc(pe_done, 1)
                q = qk[64 * (h % 2):64 * (h % 2) + 64, h // 2, :]
                k = qk[64 * (h % 2):64 * (h % 2) + 64, 4 + h // 2, :]
                for j in range(2):
                    bank = open_bank(pe, "mix0", ("s", h, j))
                    mm(bank, k[:, P * j:P * j + P], q, start=True, stop=True).then_inc(pe_done, 1)
                bank = open_bank(pe, "mix0", ("s", h, 2))
                for j in range(2):
                    last = mm(bank[:, SEQ * j:SEQ * j + SEQ], k[:, SEQ + P * j:SEQ + P * j + P], q[:, SEQ:2 * SEQ],
                              start=True, stop=True)
                last.then_inc(pe_done, 1)
            beside("mix0", BESIDE0.get(h, ()))
            if h:
                w = wbuf[(h - 1) % 2]
                pe.wait_ge(Q["w_ready"], h)
                for i in range(4):
                    bank = open_bank(pe, "mix0", ("h", h - 1, i))
                    for d in range(2):
                        for j in SEEN[d][i]:
                            a = COL[d](j, i)
                            last = mm(bank[:, (DV + 1) * d:(DV + 1) * (d + 1)], w[d][:, a:a + P], va[:, j, h - 1, :],
                                      start=j == SEEN[d][i][0], stop=j == SEEN[d][i][-1])
                    last.then_inc(pe_done, 1)
        gate_rows_bcast("mix0", (CTX, LAT), 0)
        pe.wait_ge(Q["og_ready"], 1)
        for k in range(KT):
            transposes("mix0", ("yT", k), [og[:, t, P * k:P * k + P] for t in range(4)])
        for k in range(KT):
            wait_emptied(pe, "mix0", ("yT", k))
        for n in range(2):
            project("mix0", [(t, ("wo", n, t)) for t in range(4)], panel(0, HALF), qk)

        def moe(layer):
            src = streams_of(layer)
            tiles = range(4) if layer == 0 else (2, 3)
            stage = f"moe{layer}"
            tok = SLOTS * len(src)
            col_groups = P // tok
            width = D // col_groups
            norm_T(stage, 2 * layer + 2, xh, tiles)
            pe.wait_ge(Q["router_loaded"], 32)
            rt = view(router[:, layer, :], KT, EXPERTS)
            bank = open_bank(pe, stage, ("lg",))
            for t in tiles:
                for k in range(KT):
                    last = mm(bank[:, 16 * t:16 * t + 16], hT[:, k, P * t:P * t + P], rt[:, k, :], start=k == 0,
                              stop=k == KT - 1)
            last.then_inc(pe_done, 1)
            pe.wait_ge(Q["aff_ready"], layer + 1)
            transposes(stage, ("afT",), [aff2[:, t, :] for t in range(TT)])
            for m, s in enumerate(src):
                bank = open_bank(pe, stage, ("idx", s))
                pe.wait_ge(Q["block_ready"], 2 * layer + m + 1)
                mm(bank, one_col[0:64, :].to_broadcast([64, P]), block_idx[:, s, :], start=True, stop=True).then_inc(pe_done, 1)
            pe.wait_ge(Q["pick_ready"], layer + 1)
            for k in range(KT):
                for s in src:
                    bank = open_bank(pe, stage, ("xs", k, s))
                    for t in range(TT):
                        last = mm(bank, xh[:, 2 * s + t, P * k:P * k + P], pick[:, s, t, :], start=t == 0, stop=t == 1)
                    last.then_inc(pe_done, 1)
            gate_rows_bcast(stage, src, 4 if layer == 0 else 10)
            transposes(stage, ("it",), [top_idxf, top_val])
            wait_emptied(pe, stage, ("it",))
            bank = open_bank(pe, stage, ("rep",))
            mm(bank[:, 0:P], rep_mat, sel_T, start=True, stop=True).then_inc(pe_done, 1)

            stage = f"exp{layer}"
            per = banks.stage_panels[stage][1]
            with pe.Fori(0, GROUPS) as g4:
                state["per"] = per
                for q in range(4):
                    xe = view(x_exp[:, q % 2, :], KT, 64)
                    pe.wait_ge(Q["x_exp_ready"], g4 * 4 + (17 * layer + q + 1))

                    def up(key):
                        slots = [panel(g4, HALF), panel(g4, HALF)]
                        bank = open_bank(pe, stage, key, g4)
                        for k in range(KT):
                            for j in range(col_groups):
                                at = width * j
                                last = mm(bank[tok * j:tok * j + tok, 0:width], xe[:, k, 0:tok],
                                          slots[at // HALF][:, k, at % HALF:at % HALF + width],
                                          start=k == 0, stop=k == KT - 1)
                        last.then_inc(pe_done, 1)

                    up(("g", q))
                    up(("u", q))
                    wait_emptied(pe, stage, ("u", q), g4)
                    transposes(stage, ("t", q), [hid_e[:, q % 2, P * m:P * m + P] for m in range(width // P)], g4)
                    wait_emptied(pe, stage, ("t", q), g4)
                    slots = [panel(g4, D), panel(g4, D)]
                    bank = open_bank(pe, stage, ("y", q), g4)
                    for f in range(KT):
                        jf, m = divmod(f, width // P)
                        hcol = P * m + tok * jf
                        for j in range(col_groups):
                            last = mm(bank[tok * j:tok * j + tok, 0:width], hidT[:, q % 2, hcol:hcol + tok],
                                      slots[f // 4][:, f % 4, width * j:width * j + width], start=f == 0, stop=f == KT - 1)
                    last.then_inc(pe_done, 1)
                wait_emptied(pe, stage, ("y", 3), g4)
                for s in src:
                    for t in range(TT):
                        for n in range(2):
                            bank = open_bank(pe, stage, ("c", s, t, n), g4)
                            mm(bank, back_now[:, s, P * t:P * t + P], y_four[:, s, HALF * n:HALF * n + HALF],
                               start=True, stop=True).then_inc(pe_done, 1)
            state["panel"] += (GROUPS - 1) * per
            state["per"] = 0

        moe(0)

        norm_T("mix1", 3, xh1, range(4))
        hT_lat = view(ht[:, :], KT, 2, SEQ)[:, :, 1, :]
        for n in range(2):
            slot = panel(0, HALF)
            for m in range(2):
                bank = open_bank(pe, "mix1", ("q", n, m))
                for h in range(2):
                    for k in range(KT):
                        last = mm(bank[:, SEQ * h:SEQ * h + SEQ], slot[:, k, P * (2 * m + h):P * (2 * m + h + 1)],
                                  hT_lat[:, k, :], start=k == 0, stop=k == KT - 1)
                last.then_inc(pe_done, 1)
            for m in range(2):
                wait_emptied(pe, "mix1", ("q", n, m))
                bank = open_bank(pe, "mix1", ("qs", n, m))
                h = 4 * n + 2 * m
                mm(bank, swap_mat, qT[:, h:h + 2, :], start=True, stop=True).then_inc(pe_done, 1)
        for n in range(2):
            project_wide("mix1", [("k", 4 * n + m) for m in range(4)], panel(0, HALF), hT)
            for m in range(2):
                h = 4 * n + 2 * m
                wait_emptied(pe, "mix1", ("k", h))
                wait_emptied(pe, "mix1", ("k", h + 1))
                bank = open_bank(pe, "mix1", ("ks", 2 * n + m))
                mm(bank, swap_mat, kT[:, h:h + 2, SEQ:2 * SEQ], start=True, stop=True).then_inc(pe_done, 1)
        project("mix1", [(t, ("v", 0, t)) for t in range(4)], panel(0, HALF), hT)
        pe.wait_ge(Q["kt_ready"], 8)
        for h in range(HEADS + 1):
            if h in (1, 5):
                for t in range(4):
                    wait_emptied(pe, "mix1", ("v", h // 4, t))
            if h < HEADS:
                for s in (CTX, LAT):
                    bank = open_bank(pe, "mix1", ("s", h, s))
                    for j in range(2):
                        a = SEQ * s + P * j
                        last = mm(bank[:, SEQ * j:SEQ * j + SEQ], kT[:, h, a:a + P], qT[:, h, :], start=True, stop=True)
                    last.then_inc(pe_done, 1)
            beside("mix1", BESIDE1.get(h, ()))
            if h:
                pe.wait_ge(Q["w_ready"], HEADS + h)
                bank = open_bank(pe, "mix1", ("o", h - 1))
                for i in range(TT):
                    m = 0
                    for s, e in ((CTX, 2), (LAT, 0)):
                        for j in range(2):
                            a = SEQ * j + P * i
                            last = mm(bank[:, P * i:P * i + P], dec[:, (h - 1) % 2, e, a:a + P],
                                      rv[:, 2 * s + j, DV * (h - 1):DV * h], start=m == 0, stop=m == 3)
                            m += 1
                last.then_inc(pe_done, 1)
        gate_rows_bcast("mix1", (LAT,), 8)
        pe.wait_ge(Q["og_ready"], 2)
        for m in range(4):
            transposes("mix1", ("yT", m), [ry[:, t, P * k:P * k + P] for k in (2 * m, 2 * m + 1) for t in range(TT)])
        for m in range(4):
            wait_emptied(pe, "mix1", ("yT", m))
        for n in range(2):
            slot = panel(0, HALF)
            for t in range(TT):
                bank = open_bank(pe, "mix1", ("wo", n, 2 + t))
                for k in range(KT):
                    last = mm(bank, ryT[:, k, P * t:P * t + P], slot[:, k, :], start=k == 0, stop=k == KT - 1)
                last.then_inc(pe_done, 1)
        moe(1)

    def gate_diag_of(stage):
        return gate_diag if stage.startswith("mix") else view(lflat[:, 0:1024], 2, 4, P)

    def scalar(act):
        step, full_bank, wait_emptied = S["astep"], S["full_bank"], S["wait_emptied"]
        A = nc.scalar.activation

        def squares(tiles, scratch, n):
            act.wait_ge(Q["streams_ready"], n)
            for t in list(tiles)[:len(tiles) // 2]:
                ins = A(scratch[:, t, :], tokens[t], ACT.Square, accum_out=ss[:, t:t + 1])
            ins.then_inc(Q["squares_ready"], 1)
            act.wait_ge(Q["ms_ready"], n)
            A(rs, rs, ACT.Sqrt).then_inc(Q["rms_ready"], 1)
            if n < 5:
                act.wait_ge(Q["inv_ready"], n)
                for t in list(tiles)[:len(tiles) // 2]:
                    ins = A(scratch[:, t, :], tokens[t], ACT.Copy, scale=rs[:, t:t + 1])
                ins.then_inc(Q["xh_ready"], 1)

        def take(stage, key, dst, func=ACT.Copy, part=None, scale=1.0, i=0):
            bank, freed = full_bank(act, stage, key, i)
            bank = bank if part is None else bank[:, 0:part]
            if len(dst.shape) == 3:
                bank = view(bank, dst.shape[1], dst.shape[2])
            A(dst, bank, func, scale=scale).then_inc(freed, 1)

        def modulated(stage, n, src):
            for k in range(0, KT, 2):
                bank, freed = full_bank(act, stage, ("hT", k))
                for m, s in enumerate(src):
                    ins = A(hT[:, k, SEQ * s:SEQ * s + SEQ], bank[:, SEQ * m:SEQ * m + SEQ], ACT.Identity,
                            scale=coef[:, n, s, k:k + 1], bias=shift_of(n, s, k))
                ins.then_inc(freed, 1)

        def norm_and_gates(stage, src, dst):
            for s in src:
                for n in range(2):
                    take(stage, ("gbc", s, n), dst[:, s, HALF * n:HALF * n + HALF])

        act.wait_ge(Q["ctx_loaded"], 16)
        squares(range(4), xh0, 1)
        modulated("mix0", 0, (CTX, LAT))
        for m in range(8):
            if m >= 4:
                act.wait_ge(Q["conv_ready"], m - 3)
            bank, freed = full_bank(act, "mix0", ("qk", m))
            A(qk_pad[:, m % 4, :, 2:2 + SEQ], view(bank, STREAMS, SEQ), ACT.Copy).then_inc(freed, 1)
            if m % 2 and m >= 3:
                silus(act, m - 3)
        silus(act, 6)

        def value_out(n, t):
            take("mix0", ("v", n, t), va[:, t, 4 * n:4 * n + 4, 0:DV])

        for t in range(4):
            value_out(0, t)
        act.wait_ge(Q["abs_ready"], 1)
        step(A(t_rows[64:128, :], t_rows[64:128, :], ACT.Exp, scale=-1.0))
        A(t_rows[64:128, :], t_rows[64:128, :], ACT.Ln, bias=1.0).then_inc(Q["softplus_ready"], 1)
        bank, freed = full_bank(act, "mix0", ("aT",))
        A(aT, view(bank[:, 0:256], 4, 64), ACT.Copy)
        step(A(em, view(bank[:, 256:512], 4, 64)[:, :, 0:40], ACT.Exp))
        A(st[:, 248:249], em[:, 0, 0:1], ACT.Copy).then_inc(freed, 1)
        wait_emptied(act, "mix0", ("aT",))
        for h in range(HEADS + 1):
            if h < HEADS:
                if h:
                    act.wait_ge(Q["mdiag_ready"], 2 * h)
                    act.wait_ge(Q["exp_w_ready"], h)
                for d in range(2):
                    take("mix0", ("mb", h, d), m_neg[:, d, :])
                w = wbuf[h % 2]
                if h >= 2:
                    act.wait_ge(pe_done, banks.full("mix0", ("h", h - 2, 3)))
                for d in range(2):
                    wait_emptied(act, "mix0", ("mb", h, d))
                    act.wait_ge(Q["mdiag_ready"], 2 * h + d + 1)
                    for j in range(4):
                        bias = aT[:, j, 32 * d + h:32 * d + h + 1]
                        a = COL[d](j, j)
                        A(w[d][:, a:a + P], m_diag[:, d, P * j:P * j + P], ACT.Exp, bias=bias)
                        if d == 0 and j < 3:
                            A(w[d][:, a + P:a + P * (4 - j)], m_neg[:, d, P * (j + 1):HALF], ACT.Exp, bias=bias)
                        elif d == 1 and j == 0:
                            A(w[d][:, P:3 * P], m_neg[:, d, SEQ:HALF], ACT.Exp, bias=bias)
                        elif d == 1 and j == 1:
                            A(w[d][:, a - P:a], m_neg[:, d, 0:P], ACT.Exp, bias=bias)
                            A(w[d][:, a + P:a + 3 * P], m_neg[:, d, SEQ:HALF], ACT.Exp, bias=bias)
                        elif d == 1 and j == 3:
                            A(w[d][:, a - P:a], m_neg[:, d, SEQ:SEQ + P], ACT.Exp, bias=bias)
                A(st[:, 249:250], em[:, 0, 0:1], ACT.Copy).then_inc(Q["exp_w_ready"], 1)
            for kind, n, t in BESIDE0.get(h, ()):
                if kind == "v":
                    value_out(n, t)
                else:
                    take("mix0", (kind, n, t), og[:, t, HALF * n:HALF * n + HALF], ACT.Sigmoid)
            if h:
                act.wait_ge(Q["yt_ready"], h)
                for i in range(4):
                    ins = A(sq_dump[:, :], yt[:, (h - 1) % 2, i, :], ACT.Square, accum_out=head_ss[:, i, h - 1:h])
                    if i < 3:
                        step(ins)
                ins.then_inc(Q["head_ss_ready"], 1)
                act.wait_ge(Q["head_ss_ready"], h)
        act.wait_ge(Q["head_ms_ready"], 1)
        A(st[:, 32:64], st[:, 32:64], ACT.Sqrt).then_inc(Q["head_rms_ready"], 1)
        norm_and_gates("mix0", (CTX, LAT), gb)
        for k in range(0, KT, 2):
            take("mix0", ("yT", k), qk[:, k, :])

        def moe(layer):
            src = streams_of(layer)
            tiles = range(4) if layer == 0 else (2, 3)
            stage = f"moe{layer}"
            squares(tiles, xh, 2 * layer + 2)
            modulated(stage, 2 * layer + 1, src)
            act.wait_ge(Q["shift_ready"], layer + 1)
            A(logit, logit, ACT.Exp).then_inc(Q["aff_exp_ready"], 1)
            for k in range(0, KT, 2):
                for s in src:
                    bank, freed = full_bank(act, stage, ("xs", k, s))
                    A(xs_of(layer)[:, k, :, SLOTS * src.index(s):SLOTS * src.index(s) + SLOTS], view(bank, EXPERTS, SLOTS),
                      ACT.Identity, scale=coef[:, 2 * layer + 1, s, k:k + 1], bias=shift_of(2 * layer + 1, s, k)
                      ).then_inc(freed, 1)
            norm_and_gates(stage, src, gb_moe)
            stage = f"exp{layer}"
            width = HALF if layer == 0 else SEQ
            with act.Fori(0, GROUPS) as g4:
                for q in range(4):
                    bank, freed = full_bank(act, stage, ("g", q), g4)
                    if q >= 2:
                        wait_emptied(act, stage, ("u", q - 2), g4)
                    else:
                        wait_emptied(act, stage, ("u", q + 2), g4 - 1)
                    A(sil_e[:, q % 2, 0:width], bank[:, 0:width], ACT.Silu).then_inc(freed, 1)
                    bank, freed = full_bank(act, stage, ("t", q), g4)
                    A(hidT[:, q % 2, 0:width], bank[:, 0:width], ACT.Copy).then_inc(freed, 1)

        moe(0)

        squares(range(4), xh1, 3)
        modulated("mix1", 2, (CTX, LAT))
        for n in range(2):
            for m in range(2):
                h = 4 * n + 2 * m
                take("mix1", ("q", n, m), qT[:, h:h + 2, :])
        for h in range(HEADS):
            take("mix1", ("k", h), kT[:, h, :], scale=DV ** -0.5)
        for t in range(4):
            take("mix1", ("v", 0, t), rv[:, t, 0:HALF])
        act.wait_ge(Q["logg_abs_ready"], 1)
        step(A(logg_t, logg_t, ACT.Exp, scale=-1.0))
        A(logg_t, logg_t, ACT.Ln, bias=1.0).then_inc(Q["logg_sp_ready"], 1)
        act.wait_ge(Q["logg_ready"], 1)
        act.wait_ge(Q["ret_loaded"], 32)
        for h in range(HEADS + 1):
            if h < HEADS:
                if h >= 2:
                    act.wait_ge(pe_done, banks.full("mix1", ("o", h - 2)))
                for m in range(4):
                    lg = logg[:, 8 * (m % 2) + h:8 * (m % 2) + h + 1]
                    ins = A(dec[:, h % 2, m, :], gaps[:, m, :], ACT.Exp, scale=lg)
                ins.then_inc(Q["decay_ready"], 1)
            for kind, n, t in BESIDE1.get(h, ()):
                if kind == "v":
                    take("mix1", (kind, n, t), rv[:, t, HALF * n:HALF * n + HALF])
                else:
                    take("mix1", (kind, n, t), rg[:, t - 2, HALF * n:HALF * n + HALF], ACT.Silu)
            if h:
                bank, freed = full_bank(act, "mix1", ("o", h - 1))
                A(ry[:, :, DV * (h - 1):DV * h], view(bank[:, 0:SEQ], TT, DV), ACT.Copy).then_inc(freed, 1)
        act.wait_ge(Q["head_ms_ready"], 2)
        A(var16, var16, ACT.Sqrt).then_inc(Q["head_rms_ready"], 1)
        norm_and_gates("mix1", (LAT,), gb)
        for m in range(0, 4, 2):
            take("mix1", ("yT", m), ryT[:, 2 * m:2 * m + 2, :])
        moe(1)
        squares((2, 3), xh, 5)

    sq_dump = sb("sq_dump", [P, DV])

    def silus(act, m):
        for j in (m, m + 1):
            act.wait_ge(Q["conv_ready"], j + 1)
            nc.scalar.activation(qk[:, j, :], conv_acc[:, j % 2].rearrange("p a b -> p (a b)"), ACT.Silu
                                 ).then_inc(Q["silu_ready"], 1)

    def shift_of(n, s, k):
        return mods[n // 2][:, 24 * (n % 2) + k, 1 - s:2 - s]

    def xs_of(layer):
        return view(xs[:, 0:KT * EXPERTS * SLOTS * (2 - layer)], KT, EXPERTS, SLOTS * (2 - layer))

    def vector(dve):
        V = nc.vector
        step, full_bank, wait_emptied = S["vstep"], S["full_bank"], S["wait_emptied"]
        TS, STT, TTo = V.tensor_scalar, V.scalar_tensor_tensor, V.tensor_tensor
        count = {"diag": 0}

        def spot(m):
            return st[:, 240 + m:241 + m]

        def mark(name, m):
            step(V.memset(spot(m), 0.0))
            V.memset(spot(m), 0.0).then_inc(Q[name], 1)

        def own_squares(tiles, scratch):
            for t in list(tiles)[len(tiles) // 2:]:
                ins = V.tensor_tensor_reduce(out=scratch[:, t, :], in0=tokens[t], in1=tokens[t], scale=1.0, scalar=0.0,
                                             op0=ALU.mult, op1=ALU.add, accum_out=ss[:, t:t + 1])
            step(ins)

        def rms(n, tiles, dst):
            own_squares(tiles, dst)
            dve.wait_ge(Q["squares_ready"], n)
            TS(rs, ss, 1.0 / D, RMS_EPS, ALU.mult, ALU.add).then_inc(Q["ms_ready"], 1)
            dve.wait_ge(Q["rms_ready"], n)
            V.reciprocal(rs, rs).then_inc(Q["inv_ready"], 1)
            dve.wait_ge(Q["inv_ready"], n)
            for t in list(tiles)[len(tiles) // 2:]:
                ins = TS(dst[:, t, :], tokens[t], rs[:, t:t + 1], None, ALU.mult)
            ins.then_inc(Q["xh_ready"], 1)

        def modulated(stage, n, src):
            for k in range(1, KT, 2):
                bank, freed = full_bank(dve, stage, ("hT", k))
                for m, s in enumerate(src):
                    ins = TS(hT[:, k, SEQ * s:SEQ * s + SEQ], bank[:, SEQ * m:SEQ * m + SEQ], coef[:, n, s, k:k + 1],
                             shift_of(n, s, k), ALU.mult, ALU.add)
                ins.then_inc(freed, 1)

        def diagonals(stage, layer, part, src):
            buf = gate_diag_of(stage)
            for m, (s, n) in enumerate((s, n) for s in src for n in range(2)):
                if m >= 2:
                    dve.wait_ge(pe_done, banks.full(stage, ("gbc", src[(m - 2) // 2], m % 2)))
                col = mods[layer][:, 8 * part + 4 * n:8 * part + 4 * n + 4, 1 - s]
                TTo(buf[:, m % 2], ident.unsqueeze(1).to_broadcast([P, 4, P]), spread(col, P), ALU.mult
                    ).then_inc(Q["diag_ready"], 1)

        def residual(stage, keys, gates, i=0):
            for m, (key, s, t, n) in enumerate(keys):
                if stage.startswith("mix"):
                    wait_emptied(dve, stage, ("gbc", s, n))
                bank, freed = full_bank(dve, stage, key, i)
                tmp = res_of(stage)[:, m % 2, :]
                TTo(tmp, bank, gates[:, s, HALF * n:HALF * n + HALF], ALU.mult).then_inc(freed, 1)
                wait_emptied(dve, stage, key, i)
                xs_ = tokens[2 * s + t][:, HALF * n:HALF * n + HALF]
                step(TTo(xs_, xs_, tmp, ALU.add))

        for l in range(DEPTH):
            step(TTo(mods[l][:, :, :], mods[l][:, :, :], spread(par[:, 48 * l:48 * l + 48], 2), ALU.add))
        for n in range(4):
            for s in (CTX, LAT):
                scale = mods[n // 2][:, 24 * (n % 2) + 8:24 * (n % 2) + 16, 1 - s]
                gain = par[:, 96 + 16 * (n % 2) + 8 * (n // 2):104 + 16 * (n % 2) + 8 * (n // 2)]
                step(STT(out=coef[:, n, s, :], in0=scale, scalar=1.0, in1=gain, op0=ALU.add, op1=ALU.mult))
        step(V.memset(gate_bias, 0.0))
        step(V.memset(wg[:, :, :], 0.0))
        step(V.memset(qk_pad[:, :, :, 0:2], 0.0))
        step(V.memset(qk_pad[:, :, :, 2 + SEQ:4 + SEQ], 0.0))
        V.memset(spot(8), 0.0).then_inc(Q["gbias_clear"], 1)
        V.memset(spot(7), 0.0).then_inc(Q["streams_ready"], 1)

        rms(1, range(4), xh0)
        step(V.memset(va[:, :, :, DV:DV + 1], 1.0))
        dve.wait_ge(Q["wg_loaded"], 16)
        for m in range(4):
            ins = V.tensor_copy(wg[:, :, 32 * m:32 * m + 8], wg32[:, :, 8 * m:8 * m + 8])
        ins.then_inc(Q["wg_ready"], 1)
        modulated("mix0", 0, (CTX, LAT))
        for m in range(0, 8, 2):
            pair = (m, m + 1)
            for j in pair:
                wait_emptied(dve, "mix0", ("qk", j))
            if m:
                dve.wait_ge(Q["silu_ready"], m)
            for tap in range(CONV_TAPS):
                for j in pair:
                    src, w = qk_pad[:, j % 4, :, tap:tap + SEQ], par2[:, 8 * tap + j:8 * tap + j + 1]
                    acc = conv_acc[:, j % 2]
                    if tap == 0:
                        ins = TS(acc, src, w, par2[:, 40 + j:41 + j], ALU.mult, ALU.add)
                    else:
                        ins = STT(out=acc, in0=src, scalar=w, in1=acc, op0=ALU.mult, op1=ALU.add)
                    if tap == CONV_TAPS - 1:
                        ins.then_inc(Q["conv_ready"], 1)
                if tap < CONV_TAPS - 1:
                    step(ins)
        dve.wait_ge(Q["silu_ready"], 8)
        dve.wait_ge(Q["gbias_loaded"], 64)
        dve.wait_ge(Q["conv_ready"], 8)
        bank, freed = full_bank(dve, "mix0", ("gr",))
        TS(gate_rows, bank, gate_bias, None, ALU.add).then_inc(freed, 1)
        wait_emptied(dve, "mix0", ("gr",))
        STT(out=t_rows[64:128, :], in0=gate_rows[64:128, :], scalar=-1.0, in1=gate_rows[64:128, :], op0=ALU.mult,
            op1=ALU.max).then_inc(Q["abs_ready"], 1)
        step(V.memset(one_rows, 1.0))
        dve.wait_ge(Q["softplus_ready"], 1)
        step(STT(out=lf_rows[0:64, :], in0=gate_rows[64:128, :], scalar=0.0, in1=t_rows[64:128, :], op0=ALU.min,
                 op1=ALU.subtract))
        scan = V.tensor_tensor_scan

        def scans(dst, src, op0, op1):
            scan(dst[0:32, :], one_rows[0:32, :], src[0:32, :], 0.0, op0, op1)
            step(scan(dst[32:64, 0:SEQ][:, ::-1], one_rows[32:64, 0:SEQ], src[32:64, 0:SEQ][:, ::-1], 0.0, op0, op1))
            step(scan(dst[32:64, SEQ:][:, ::-1], one_rows[32:64, 0:SEQ], src[32:64, SEQ:][:, ::-1], dst[32:64, 0:1],
                      op0, op1))

        scans(b_rows, lf_rows, ALU.mult, ALU.add)
        step(TTo(gate_rows[0:64, :], gate_rows[0:64, :], b_rows[0:64, :], ALU.subtract))
        scans(lf_rows, gate_rows, ALU.mult, ALU.max)
        step(STT(out=b_rows[0:64, :], in0=b_rows[0:64, :], scalar=-1.0, in1=lf_rows[0:64, :], op0=ALU.mult,
                 op1=ALU.subtract))
        step(TS(lf_rows[0:64, :], lf_rows[0:64, :], -1.0, None, ALU.mult))
        V.memset(spot(9), 0.0).then_inc(Q["rows_ready"], 1)
        wait_emptied(dve, "mix0", ("aT",))
        masks = (later_key, earlier_key)
        for h in range(HEADS + 1):
            if h < HEADS:
                if h:
                    dve.wait_ge(Q["exp_w_ready"], h)
                for d in range(2):
                    wait_emptied(dve, "mix0", ("mb", h, d))
                    TTo(view(m_diag[:, d, :], 4, P), view(m_neg[:, d, :], 4, P),
                        masks[d].unsqueeze(1).to_broadcast([P, 4, P]), ALU.add).then_inc(Q["mdiag_ready"], 1)
                dve.wait_ge(Q["exp_w_ready"], h + 1)
                w = wbuf[h % 2]

                def weigh(d, a, bank, col, n):
                    return STT(out=w[d][:, a:a + n], in0=bank[:, col:col + n], scalar=SCALE, in1=w[d][:, a:a + n],
                               op0=ALU.mult, op1=ALU.mult)

                bank, freed = full_bank(dve, "mix0", ("s", h, 0))
                weigh(0, 0, bank, 0, HALF)
                weigh(1, 0, bank, 0, P)
                weigh(1, P, bank, SEQ, SEQ).then_inc(freed, 1)
                bank, freed = full_bank(dve, "mix0", ("s", h, 1))
                weigh(0, 512, bank, P, 3 * P)
                weigh(1, 384, bank, 0, HALF).then_inc(freed, 1)
                bank, freed = full_bank(dve, "mix0", ("s", h, 2))
                weigh(0, 896, bank, 0, SEQ)
                weigh(0, 1152, bank, SEQ + P, P)
                weigh(1, 896, bank, 0, P)
                weigh(1, 1024, bank, SEQ, SEQ).then_inc(freed, 1)
                wait_emptied(dve, "mix0", ("s", h, 2))
                V.memset(spot(6), 0.0).then_inc(Q["w_ready"], 1)
            if h:
                y = yt[:, (h - 1) % 2]
                if h >= 3:
                    dve.wait_ge(Q["head_ss_ready"], h - 2)
                both = []
                for i in range(4):
                    bank, freed = full_bank(dve, "mix0", ("h", h - 1, i))
                    both.append((view(bank[:, 0:2 * (DV + 1)], 2, DV + 1), freed))
                    ins = STT(out=r2[:, 2 * i:2 * i + 2], in0=both[i][0][:, :, DV], scalar=-1.0,
                              in1=em[:, i, h - 1:h + 32:32], op0=ALU.mult, op1=ALU.max)
                step(ins)
                for i in range(4):
                    ins = TTo(r2[:, 2 * i:2 * i + 2], r2[:, 2 * i:2 * i + 2], both[i][0][:, :, DV], ALU.max)
                step(ins)
                step(V.reciprocal(r2, r2))
                for i in range(4):
                    ins = TS(y[:, i, :], both[i][0][:, 0, 0:DV], r2[:, 2 * i:2 * i + 1], None, ALU.mult)
                step(ins)
                for i in range(4):
                    STT(out=y[:, i, :], in0=both[i][0][:, 1, 0:DV], scalar=r2[:, 2 * i + 1:2 * i + 2], in1=y[:, i, :],
                        op0=ALU.mult, op1=ALU.add).then_inc(both[i][1], 1)
                for i in range(4):
                    wait_emptied(dve, "mix0", ("h", h - 1, i))
                V.memset(spot(5), 0.0).then_inc(Q["yt_ready"], 1)
                if h in (1, 5):
                    for t in range(4):
                        wait_emptied(dve, "mix0", ("o", h // 4, t))
                o = og[:, :, DV * (h - 1):DV * h]
                step(TTo(o, o, y, ALU.mult))
        dve.wait_ge(Q["head_ss_ready"], HEADS)
        TS(st[:, 32:64], st[:, 32:64], 1.0 / DV, RMS_EPS, ALU.mult, ALU.add).then_inc(Q["head_ms_ready"], 1)
        diagonals("mix0", 0, 2, (CTX, LAT))
        dve.wait_ge(Q["gain_loaded"], 16)
        for t in range(4):
            ins = TTo(og[:, t, :], og[:, t, :], lnp[:, 0, :], ALU.mult)
        step(ins)
        dve.wait_ge(Q["head_rms_ready"], 1)
        step(V.reciprocal(st[:, 32:64], st[:, 32:64]))
        ov = og.rearrange("p t (h d) -> p (t h) d", h=HEADS)
        step(TTo(ov, ov, spread(st[:, 32:64], DV), ALU.mult))
        V.memset(spot(4), 0.0).then_inc(Q["og_ready"], 1)
        for k in range(1, KT, 2):
            bank, freed = full_bank(dve, "mix0", ("yT", k))
            V.tensor_copy(qk[:, k, :], bank).then_inc(freed, 1)
        residual("mix0", [(("wo", n, t), t // 2, t % 2, n) for n in range(2) for t in range(4)], gb)
        V.memset(spot(7), 0.0).then_inc(Q["streams_ready"], 1)

        def moe(layer):
            src = streams_of(layer)
            tiles = range(4) if layer == 0 else (2, 3)
            lo = 16 * tiles[0]
            stage = f"moe{layer}"
            rms(2 * layer + 2, tiles, xh)
            modulated(stage, 2 * layer + 1, src)
            step(V.memset(aff2, 0.0))
            bank, freed = full_bank(dve, stage, ("lg",))
            lv = view(logit, 4, EXPERTS)[:, tiles[0]:4, :]
            V.tensor_copy(logit[:, lo:64], bank[:, lo:64]).then_inc(freed, 1)
            wait_emptied(dve, stage, ("lg",))
            if lo:
                step(V.memset(logit[:, 0:lo], 0.0))
            mx = lmax[:, tiles[0]:4]
            step(V.reduce_max(mx, lv, X_AXIS))
            TTo(lv, lv, spread(mx, EXPERTS), ALU.subtract).then_inc(Q["shift_ready"], 1)
            dve.wait_ge(Q["aff_exp_ready"], layer + 1)
            step(V.reduce_sum(mx, lv, X_AXIS))
            step(V.reciprocal(mx, mx))
            for s in src:
                ins = TTo(aff2[:, :, 32 * s:32 * s + 16], view(logit, 4, EXPERTS)[:, 2 * s:2 * s + 2, :],
                          spread(lmax[:, 2 * s:2 * s + 2], EXPERTS), ALU.mult)
            ins.then_inc(Q["aff_ready"], 1)
            bank, freed = full_bank(dve, stage, ("afT",))
            V.tensor_copy(aff_T, bank[0:64, 0:SEQ]).then_inc(freed, 1)
            wait_emptied(dve, stage, ("afT",))
            row = aff_T
            for r in range(0, SLOTS, 8):
                step(V.max(top_val[:, r:r + 8], row))
                step(V.max_index(top_idx[:, r:r + 8], top_val[:, r:r + 8], row))
                if r + 8 < SLOTS:
                    step(V.match_replace(aff_work, top_val[:, r:r + 8], row, -1.0))
                    row = aff_work
            step(V.tensor_copy(top_idxf, top_idx))
            for s in src:
                TTo(view(block_idx[:, s, :], EXPERTS, SLOTS), spread(ident[0:64, 32 * s:32 * s + 16], SLOTS),
                    top_idxf.unsqueeze(1).to_broadcast([64, EXPERTS, SLOTS]), ALU.mult).then_inc(Q["block_ready"], 1)
            if layer:
                V.memset(spot(3), 0.0).then_inc(Q["block_ready"], 1)
            for s in src:
                bank, freed = full_bank(dve, stage, ("idx", s))
                for t in range(TT):
                    ins = TS(pick[:, s, t, :], bank, tok_col[:, t:t + 1], None, ALU.is_equal)
                ins.then_inc(freed, 1)
                wait_emptied(dve, stage, ("idx", s))
            V.memset(spot(2), 0.0).then_inc(Q["pick_ready"], 1)
            for k in range(1, KT, 2):
                for m, s in enumerate(src):
                    bank, freed = full_bank(dve, stage, ("xs", k, s))
                    TS(xs_of(layer)[:, k, :, SLOTS * m:SLOTS * m + SLOTS], view(bank, EXPERTS, SLOTS),
                       coef[:, 2 * layer + 1, s, k:k + 1], shift_of(2 * layer + 1, s, k), ALU.mult, ALU.add
                       ).then_inc(freed, 1)
            diagonals(stage, layer, 5, src)
            bank, freed = full_bank(dve, stage, ("it",))
            V.tensor_copy(view(sel_T, 2, 64), view(bank[0:32, 0:256], 2, P)[:, :, 0:64]).then_inc(freed, 1)
            bank, freed = full_bank(dve, stage, ("rep",))
            for w in range(2):
                rows = view(bank[:, 64 * w:64 * w + 64], STREAMS, 8, 4)[:, :, 0:4, :]
                ins = TTo(sel_m, rows, quad.unsqueeze(1).unsqueeze(1).to_broadcast([P, 2, 4, 4]), ALU.mult)
                step(ins)
                ins = V.reduce_sum(sel[:, w], sel_m, X_AXIS)
                if w:
                    ins.then_inc(freed, 1)
                    wait_emptied(dve, stage, ("rep",))
                else:
                    step(ins)
            for s in src:
                for g in range(GROUPS):
                    ins = TS(spread_back[:, s, g, :], iota, sel[:, 0, s, g:g + 1], sel[:, 1, s, g:g + 1], ALU.is_equal,
                             ALU.mult)
            step(ins)
            for k in range(0, KT, 2):
                for s in src:
                    wait_emptied(dve, stage, ("xs", k, s))
            for k in range(1, KT, 2):
                for s in src:
                    wait_emptied(dve, stage, ("xs", k, s))

            tok = SLOTS * len(src)
            col_groups, width = P // tok, D * tok // P
            xsv = xs_of(layer)
            stage = f"exp{layer}"

            def fetch(e, b):
                TS(view(x_exp[:, b, :], KT, 64)[:, :, 0:tok], xsv[:, :, bass.ds(e, 1), :].rearrange("p k a t -> p k (a t)")
                   if not isinstance(e, int) else xsv[:, :, e, :], 1.0, None, ALU.mult).then_inc(Q["x_exp_ready"], 1)

            fetch(0, 0)
            for s in src:
                for n in range(2):
                    wait_emptied(dve, f"moe{layer}", ("gbc", s, n))
            with dve.Fori(0, GROUPS) as g4:
                step.enter(g4, 4 * len(src))
                for s in src:
                    TS(back_now[:, s, :], spread_back[:, s, bass.ds(g4, 1), :].rearrange("p a n -> p (a n)"), 1.0, None,
                       ALU.mult)
                for q in range(4):
                    if q < 3:
                        if q:
                            dve.wait_ge(pe_done, banks.full(stage, ("u", q - 1), g4))
                        else:
                            dve.wait_ge(pe_done, banks.full(stage, ("u", 3), g4 - 1))
                        fetch(g4 * 4 + (q + 1), (q + 1) % 2)
                    else:
                        dve.wait_ge(pe_done, banks.full(stage, ("u", 2), g4))
                        fetch((g4 * 4 + 4) % EXPERTS, 0)
                    bank, freed = full_bank(dve, stage, ("u", q), g4)
                    wait_emptied(dve, stage, ("g", q), g4)
                    TTo(hid_e[:, q % 2, 0:width], sil_e[:, q % 2, 0:width], bank[:, 0:width], ALU.mult).then_inc(freed, 1)
                    bank, freed = full_bank(dve, stage, ("y", q), g4)
                    for j in range(col_groups):
                        for m, s in enumerate(src):
                            r = tok * j + SLOTS * m
                            ins = V.tensor_copy(y_four[32 * q:32 * q + 32, s, width * j:width * j + width],
                                                bank[r:r + 32, 0:width])
                    ins.then_inc(freed, 1)
                residual(stage, [(("c", s, t, n), s, t, n) for s in src for t in range(TT) for n in range(2)], gb_moe, g4)
            step.leave(GROUPS)
            V.memset(spot(7), 0.0).then_inc(Q["streams_ready"], 1)
            V.memset(spot(1), 0.0).then_inc(Q["gain_free"], 1)

        moe(0)

        rms(3, range(4), xh1)
        modulated("mix1", 2, (CTX, LAT))
        dve.wait_ge(Q["decay_loaded"], 16)
        STT(out=logg_t, in0=logg, scalar=-1.0, in1=logg, op0=ALU.mult, op1=ALU.max).then_inc(Q["logg_abs_ready"], 1)
        dve.wait_ge(Q["ret_loaded"], 32)
        cos, sin = (rope_t[:, m, :].unsqueeze(1).to_broadcast([P, 2, SEQ]) for m in range(2))
        ra, rb = view(rot_a, 2, SEQ), view(rot_b, 2, SEQ)

        def rotate(heads, key, raw_keys):
            for k_ in raw_keys:
                wait_emptied(dve, "mix1", k_)
            step(TTo(ra, heads, cos, ALU.mult))
            bank, freed = full_bank(dve, "mix1", key)
            TTo(rb, view(bank, 2, SEQ), sin, ALU.mult).then_inc(freed, 1)
            wait_emptied(dve, "mix1", key)
            TTo(heads, ra, rb, ALU.add).then_inc(Q["kt_ready"], 1)
            dve.wait_ge(Q["kt_ready"], count["diag"] + 1)
            count["diag"] += 1

        for n in range(2):
            for m in range(2):
                h = 4 * n + 2 * m
                rotate(qT[:, h:h + 2, :], ("qs", n, m), [("q", n, m)])
        for n in range(2):
            for m in range(2):
                h = 4 * n + 2 * m
                rotate(kT[:, h:h + 2, SEQ:2 * SEQ], ("ks", 2 * n + m), [("k", h), ("k", h + 1)])
        dve.wait_ge(Q["logg_sp_ready"], 1)
        STT(out=logg, in0=logg, scalar=0.0, in1=logg_t, op0=ALU.min, op1=ALU.subtract).then_inc(Q["logg_ready"], 1)
        for h in range(HEADS):
            e = dec[:, h % 2]
            dve.wait_ge(Q["decay_ready"], h + 1)
            step(TTo(e[:, 0, :], e[:, 0, :], e[:, 1, :], ALU.mult))
            TTo(e[:, 0, :], e[:, 0, :], gaps[:, 4, :], ALU.add)
            step(TTo(e[:, 2, :], e[:, 2, :], e[:, 3, :], ALU.add))
            for s, m in ((CTX, 2), (LAT, 0)):
                bank, freed = full_bank(dve, "mix1", ("s", h, s))
                TTo(e[:, m, :], e[:, m, :], bank, ALU.mult).then_inc(freed, 1)
            wait_emptied(dve, "mix1", ("s", h, LAT))
            V.memset(spot(6), 0.0).then_inc(Q["w_ready"], 1)
        wait_emptied(dve, "mix1", ("o", HEADS - 1))
        yv = ry.rearrange("p t (h d) -> p (t h) d", h=HEADS)
        step(V.reduce_sum(mean, yv, X_AXIS))
        step(TS(mean, mean, 1.0 / DV, None, ALU.mult))
        step(TTo(yv, yv, spread(mean, DV), ALU.subtract))
        step(TTo(rsq, yv, yv, ALU.mult))
        step(V.reduce_sum(var16, rsq, X_AXIS))
        TS(var16, var16, 1.0 / DV, RMS_EPS, ALU.mult, ALU.add).then_inc(Q["head_ms_ready"], 1)
        diagonals("mix1", 1, 2, (LAT,))
        dve.wait_ge(Q["gain_loaded"], 32)
        for n in range(2):
            for t in range(TT):
                wait_emptied(dve, "mix1", ("g", n, 2 + t))
        for t in range(TT):
            ins = TTo(rg[:, t, :], rg[:, t, :], lnp[:, 0, :], ALU.mult)
        step(ins)
        dve.wait_ge(Q["head_rms_ready"], 2)
        step(V.reciprocal(var16, var16))
        step(TTo(yv, yv, spread(var16, DV), ALU.mult))
        TTo(ry, ry, rg, ALU.mult).then_inc(Q["og_ready"], 1)
        for m in range(1, 4, 2):
            bank, freed = full_bank(dve, "mix1", ("yT", m))
            V.tensor_copy(ryT[:, 2 * m:2 * m + 2, :], view(bank, 2, SEQ)).then_inc(freed, 1)
        residual("mix1", [(("wo", n, 2 + t), LAT, t, n) for n in range(2) for t in range(TT)], gb)
        V.memset(spot(7), 0.0).then_inc(Q["streams_ready"], 1)
        moe(1)

        own_squares((2, 3), xh)
        dve.wait_ge(Q["squares_ready"], 5)
        TS(rs, ss, 1.0 / D, RMS_EPS, ALU.mult, ALU.add).then_inc(Q["ms_ready"], 1)
        dve.wait_ge(Q["rms_ready"], 5)
        step(V.reciprocal(rs, rs))
        dve.wait_ge(Q["gain_loaded"], 48)
        for t in range(TT):
            STT(out=x[:, t, :], in0=x[:, t, :], scalar=rs[:, 2 + t:3 + t], in1=lnp[:, 0, :], op0=ALU.mult,
                op1=ALU.mult).then_inc(Q["final_ready"], 1)

    def res_of(stage):
        return res_tmp if stage.startswith("mix") else view(arena[:, 12288:13312], 2, HALF)

    return {"sync": sync, "gpsimd": gpsimd, "tensor": tensor, "scalar": scalar, "vector": vector}


def program(nc, I, K, out):
    banks = BankPlan()
    R, EV = BankPlan.REL, BankPlan.EV

    def attend(kind):
        return [(f"pt{kind}", 0), (f"pt{kind}", 1), (f"pt{kind}", 2), (f"pt{kind}", 3), (f"pv{kind}", 0),
                (f"pt{kind}", 4), (f"pt{kind}", 5), (f"pv{kind}", 1), (f"pt{kind}", 6), (f"pt{kind}", 7),
                (f"pv{kind}", 2), (f"pv{kind}", 3)]

    def gates(kind):
        return [(f"g{kind}", 0), (f"g{kind}", 1), R, (f"g{kind}", 2), (f"g{kind}", 3), R]

    def branch(kind):
        return [(f"m{kind}", m) for m in range(4)] + [R]

    layer = [("xT", t, m) for t in range(TT) for m in range(2)]
    for b in range(3):
        layer += [("b", b, 0), ("b", b, 1), R]
    layer += [("aq", 0), ("aq", 1), R, ("ak",), ("av",), R] + [("sa", h) for h in range(HEADS)]
    layer += [("cq", 0), ("cq", 1), R, ("ck", 0), ("ck", 1), R] + [("sc", h) for h in range(HEADS)]
    layer += [("cv", 0), ("cv", 1), R] + gates("b") + attend("a") + branch("b") + gates("a") + branch("a")
    layer += gates("c") + attend("c") + branch("c")
    layer += [("wo", 0, 0), ("wo", 0, 1), R, ("wo", 1, 0), ("wo", 1, 1), R] + [("x1T", t, m) for t in range(TT) for m in range(2)]
    for p in range(FFN_TILES // 2):
        layer += [("ff", 2 * p), ("ff", 2 * p + 1), R, ("ada", p), R]
        if p:
            layer += [("adaT", p - 1)]
    layer += [("ada", 11), R, ("adaT", 10)] + [EV] * 5 + [("dn", t, n) for t in range(TT) for n in range(2)]
    layer += [R, ("adaT", 11)]
    banks.plan("pre", [("par", 0)])
    banks.plan("layer", layer, DEPTH)
    LAYER_PANELS = banks.stage_panels["layer"][1]
    assert LAYER_PANELS % RING == 0
    if not BLOCK1_ONLY:
        plan_second(banks)

    w_in, w_out = I["w_in"], I["w_out"]

    ctx = ExitStack()
    with ctx:
        def sb(name, shape, dt=F32):
            return ctx.enter_context(nc.sbuf_tensor(name, shape, dt))

        def sem(name):
            return ctx.enter_context(nc.semaphore(name))

        ring = sb("ring", [P, RING, PANEL])
        arena = sb("arena", [P, 16384])
        ht = sb("ht", [P, 4096])
        x = sb("x", [P, TT, D])
        c = sb("c", [P, TT, D])
        lnp = sb("lnp", [P, 2, D])
        const = sb("const", [P, 904])
        ident, swap_mat = const[:, 0:128], const[:, 128:256]
        iota, tok_col, quad = const[:, 256:512], const[:, 512:514], const[:, 514:518]
        later_key, earlier_key = const[:, 518:646], const[:, 646:774]
        mods_now = sb("mods_now", [P, 48, 2])
        mods_0 = sb("mods_0", [P, 48, 2])
        par = sb("par", [P, 128])
        par2 = sb("par2", [P, 88])
        st = sb("st", [P, 256])
        psum = ctx.enter_context(nc.psum_tensor("psum", [P, BANKS, HALF], F32))

        bz = arena[:, 0:3072]
        bpart = view(bz, 3, 4, SEQ)
        zc, za = view(bz, HEADS, 384), view(arena[:, 3072:6144], HEADS, 384)
        aq, ak = view(arena[:, 6144:7168], 4, SEQ), arena[:, 7168:7424]
        cq, ck = view(arena[:, 7424:8448], 4, SEQ), view(arena[:, 8448:9472], 4, SEQ)
        gate_bc = view(arena[:, 6144:8192], 8, SEQ)
        gate_a = view(ht[:, 2048:4096], 8, SEQ)
        av = view(arena[:, 9472:9728], TT, P)
        cv = view(arena[:, 9728:10752], TT, HALF)
        ya, yb, yc = (view(arena[:, 10752 + 1024 * n:11776 + 1024 * n], 4, SEQ) for n in range(3))
        pt = view(arena[:, 13824:15360], 4, 384)
        dist_a, dist_c = arena[:, 15360:15744], arena[:, 15744:16128]
        cT = view(arena[:, 16128:16384], KT, 32)
        hid = view(arena[:, 0:5632], FFN_TILES, SEQ)
        sil = view(arena[:, 5632:6656], 4, SEQ)
        ada_rows = view(arena[:, 6656:6912], 2, P)
        xT = view(ht[:, 0:2048], KT, SEQ)
        merged = c[:, :, :].rearrange("p t (k s) -> p (t k) s", s=SEQ)
        par_rows, par2_rows = arena[:, 0:128], arena[:, 128:256]
        rmax, nmax, sums, recip, sink_e = (st[:, 16 * n:16 * n + 16] for n in range(5))
        nsink = st[:, 80:96]
        sinks = st[:, 96:104]
        bst = view(st[:, 104:128], TT, 2, 6)
        mv = view(st[:, 128:132], TT, 2)
        rstd = st[:, 132:134]
        conv_w = view(st[:, 134:146], 3, 4)

        panel_in = [sem(f"panel_in_{s}") for s in range(RING)]
        pe_done = sem("pe_done")
        bank_free = [sem(f"bank_free_{b}") for b in range(BANKS)]
        dve_step, act_step = sem("dve_step"), sem("act_step")
        x_loaded, const_loaded, par_loaded = sem("x_loaded"), sem("const_loaded"), sem("par_loaded")
        sinks_loaded, ln1_loaded, ln2_loaded = sem("sinks_loaded"), sem("ln1_loaded"), sem("ln2_loaded")
        x_ready, x1_ready, cT_ready = sem("x_ready"), sem("x1_ready"), sem("cT_ready")
        sinks_used, c_cols_ready = sem("sinks_used"), sem("c_cols_ready")
        yb_ready, merged_ready = sem("yb_ready"), sem("merged_ready")
        nmax_ready = {k: sem(f"nmax_{k}_ready") for k in "ac"}
        exp_ready = {k: sem(f"exp_{k}_ready") for k in "ac"}
        probs_ready = {k: sem(f"probs_{k}_ready") for k in "ac"}
        var_ready, std_ready = sem("var_ready"), sem("std_ready")
        out_stored, sil_ready = sem("out_stored"), sem("sil_ready")
        S = dict(locals())
        second = None if BLOCK1_ONLY else second_block(nc, ctx, banks, I, K, out, S)

        block = ctx.enter_context(nc.Block())

        def open_bank(pe, stage, key, i=0):
            b = banks.bank(stage, key)
            pe.wait_ge(bank_free[b], banks.free(stage, key, i))
            return psum[:, b, :]

        def full_bank(eng, stage, key, i=0):
            eng.wait_ge(pe_done, banks.full(stage, key, i))
            b = banks.bank(stage, key)
            return psum[:, b, :], bank_free[b]

        def wait_emptied(eng, stage, key, i=0):
            eng.wait_ge(bank_free[banks.bank(stage, key)], banks.emptied(stage, key, i))

        S.update(open_bank=open_bank, full_bank=full_bank, wait_emptied=wait_emptied)

        def halves(src):
            v = src.rearrange("(h k p) n -> h p k n", h=2, p=P)
            return [(slice(4 * h, 4 * h + 4), v[h]) for h in range(2)]

        def layer_panels(l):
            def cols(name, off=0, n=HALF):
                return n, halves(w_in[l][:, COLS[name] + off:COLS[name] + off + n])

            def rows(src, k0, k1):
                v = src[k0 * P:k1 * P, :].rearrange("(h k p) n -> h p k n", h=2, p=P)
                return D, [(slice(h * (k1 - k0) // 2, (h + 1) * (k1 - k0) // 2), v[h]) for h in range(2)]

            def ada(p):
                return HALF, halves(I["ada_w_2"][l][:, p * HALF:(p + 1) * HALF])

            for name in ("b_h", "b_b", "b_c", "a_q"):
                yield cols(name)
            yield cols("a_k", n=2 * P)
            for name in ("c_q", "c_k", "c_v"):
                yield cols(name)
            yield cols("g_b")
            yield cols("g_b", HALF)
            yield rows(I["w_branch_b"][l], 0, 4)
            yield cols("g_a")
            yield cols("g_a", HALF)
            va = I["w_branch_a"][l].rearrange("(g r d) n -> g d r n", g=2, r=4)
            yield D, [((slice(64 * g, 64 * g + 64), slice(0, 4)), va[g]) for g in range(2)]
            yield cols("g_c")
            yield cols("g_c", HALF)
            yield rows(I["w_branch_c"][l], 0, 4)
            for n in range(2):
                yield HALF, halves(w_out[l][:, n * HALF:(n + 1) * HALF])
            for p in range(FFN_TILES // 2):
                g = [I[w][l][:, p * SEQ:(p + 1) * SEQ].rearrange("(k p) n -> p k n", p=P)
                     for w in ("w_ffn_gate", "w_ffn_up")]
                yield HALF, [((slice(0, P), slice(0, KT), slice(u * SEQ, u * SEQ + SEQ)), g[u]) for u in range(2)]
                yield ada(p)
            yield ada(11)
            for d in range(6):
                yield rows(I["w_ffn_down"][l], 4 * d, min(4 * d + 4, FFN_TILES))

        @block.sync
        def _(sp):
            def load_panel(n, width, parts):
                if n >= RING:
                    first, _, _ = banks.release[n - RING]
                    sp.wait_ge(pe_done, first)
                slot = view(ring[:, n % RING, :], PANEL // width, width)
                for where, src in parts:
                    where = where if isinstance(where, tuple) else (slice(0, P), where)
                    sp.dma_start(slot[where], src).then_inc(panel_in[n % RING], 16)

            sp.dma_start(x[:, :, :], I["x"][0].rearrange("(t p) d -> p t d", p=P)).then_inc(x_loaded, 16)
            n = banks.stage_panels["layer"][0]
            for l in range(DEPTH):
                for width, parts in layer_panels(l):
                    load_panel(n, width, parts)
                    n += 1
            if second:
                second["sync"](sp, load_panel)
            else:
                sp.wait_ge(x_ready, 6)
                sp.dma_start(out[0].rearrange("(t p) d -> p t d", p=P), x[:, :, :]).then_inc(out_stored, 16)
            sp.wait_ge(out_stored, OUT_STORES * 16)

        @block.gpsimd
        def _(pool):
            for l in range(DEPTH):
                if l:
                    pool.wait_ge(sinks_used, l)
                pool.dma_start(sinks, I["attn_sinks"][l:l + 1, :].to_broadcast([P, HEADS])).then_inc(sinks_loaded, 16)
                if l:
                    pool.wait_ge(x_ready, 2 * l + 2)
                for m, w in enumerate(("ln1_g", "ln1_b")):
                    pool.dma_start(lnp[:, m, :], I[w][l:l + 1, :].to_broadcast([P, D])).then_inc(ln1_loaded, 16)
                pool.wait_ge(x1_ready, 2 * l + 2)
                for m, w in enumerate(("ln2_g", "ln2_b")):
                    pool.dma_start(lnp[:, m, :], I[w][l:l + 1, :].to_broadcast([P, D])).then_inc(ln2_loaded, 16)
            if second:
                second["gpsimd"](pool)

        @block.tensor
        def _(pe):
            mm = nc.tensor.matmul
            state = {"panel": banks.stage_panels["layer"][0]}

            def panel(i, width):
                n = state["panel"]
                state["panel"] += 1
                per = state.get("per", 0)
                pe.wait_ge(panel_in[n % RING], i * (32 * per // RING) + 32 * (n // RING + 1))
                return view(ring[:, n % RING, :], PANEL // width, width)

            def transposes(stage, key, tiles, i=0):
                bank = open_bank(pe, stage, key, i)
                for m, src in enumerate(tiles):
                    last = nc.tensor.transpose(bank[0:src.shape[1], 128 * m:128 * m + src.shape[0]], src,
                                               ident[0:src.shape[0], 0:src.shape[0]])
                last.then_inc(pe_done, 1)

            S.update(panel=panel, state=state, transposes=transposes)
            pe.wait_ge(const_loaded, 32)
            pe.wait_ge(par_loaded, 8 * 16)
            bank = open_bank(pe, "pre", ("par", 0))
            nc.tensor.transpose(bank[:, 0:128], par_rows[:, :], ident)
            nc.tensor.transpose(bank[:, 128:216], par2_rows[0:88, :], ident[0:88, 0:88]).then_inc(pe_done, 1)

            with pe.Fori(0, DEPTH) as l:
                state["per"] = LAYER_PANELS

                def project_T(key, slot, rhs, tiles=2, k_tiles=KT):
                    for m in range(tiles):
                        bank = open_bank(pe, "layer", key + (m,), l)
                        for h in range(2):
                            for k in range(k_tiles):
                                last = mm(bank[:, SEQ * h:SEQ * h + SEQ],
                                          slot[:, k, P * (2 * m + h):P * (2 * m + h + 1)], rhs[:, k, :],
                                          start=k == 0, stop=k == k_tiles - 1)
                        last.then_inc(pe_done, 1)

                def transpose_x(name, ready):
                    for t in range(TT):
                        pe.wait_ge(ready, 2 * l + t + 1)
                        for m in range(2):
                            transposes("layer", (name, t, m), [x[:, t, P * k:P * k + P] for k in range(4 * m, 4 * m + 4)], l)
                    for t in range(TT):
                        for m in range(2):
                            wait_emptied(pe, "layer", (name, t, m), l)

                transpose_x("xT", x_ready)
                for b in range(3):
                    project_T(("b", b), panel(l, HALF), xT)
                slot = panel(l, HALF)
                for m in range(2):
                    bank = open_bank(pe, "layer", ("aq", m), l)
                    for h in range(2):
                        for k in range(KT):
                            for g in range(2):
                                w = 64 * (4 * g + 2 * m + h)
                                last = mm(bank[64 * g:64 * g + 64, SEQ * h:SEQ * h + SEQ], slot[:, k, w:w + 64],
                                          xT[:, k, :], start=k == 0, stop=k == KT - 1)
                    last.then_inc(pe_done, 1)
                slot = panel(l, SEQ)
                bank = open_bank(pe, "layer", ("ak",), l)
                for k in range(KT):
                    last = mm(bank[:, 0:SEQ], slot[:, k, 0:P], xT[:, k, :], start=k == 0, stop=k == KT - 1)
                last.then_inc(pe_done, 1)
                bank = open_bank(pe, "layer", ("av",), l)
                for t in range(TT):
                    for k in range(KT):
                        last = mm(bank[:, P * t:P * t + P], xT[:, k, P * t:P * t + P], slot[:, k, P:2 * P],
                                  start=k == 0, stop=k == KT - 1)
                last.then_inc(pe_done, 1)

                def scores(kind, q_of, k_of):
                    for h in range(HEADS):
                        bank = open_bank(pe, "layer", (f"s{kind}", h), l)
                        q, k = q_of(h), k_of(h)
                        mm(bank[:, 0:P], q[:, 0:P], k[:, 0:P], start=True, stop=True)
                        mm(bank[:, P:3 * P], q[:, P:2 * P], k[:, 0:SEQ], start=True, stop=True).then_inc(pe_done, 1)

                for key in (("aq", 0), ("aq", 1), ("ak",)):
                    wait_emptied(pe, "layer", key, l)
                scores("a", lambda h: aq[64 * (h // 4):64 * (h // 4) + 64, h % 4, :],
                       lambda h: ak[64 * (h // 4):64 * (h // 4) + 64, :])
                project_T(("cq",), panel(l, HALF), xT)
                project_T(("ck",), panel(l, HALF), xT)
                for key in (("cq", 0), ("cq", 1), ("ck", 0), ("ck", 1)):
                    wait_emptied(pe, "layer", key, l)
                scores("c", lambda h: cq[64 * (h % 2):64 * (h % 2) + 64, h // 2, :],
                       lambda h: ck[64 * (h % 2):64 * (h % 2) + 64, h // 2, :])

                def project(keys, slot, lhs, k_tiles=KT):
                    for t, key in enumerate(keys):
                        bank = open_bank(pe, "layer", key, l)
                        for k in range(k_tiles):
                            last = mm(bank, lhs[:, k, P * t:P * t + P], slot[:, k, :], start=k == 0, stop=k == k_tiles - 1)
                        last.then_inc(pe_done, 1)

                project([("cv", 0), ("cv", 1)], panel(l, HALF), xT)

                def gate_panels(kind):
                    for n in range(2):
                        slot = panel(l, HALF)
                        for m in range(2):
                            bank = open_bank(pe, "layer", (f"g{kind}", 2 * n + m), l)
                            for h in range(2):
                                for k in range(KT):
                                    last = mm(bank[:, SEQ * h:SEQ * h + SEQ], slot[:, k, P * (2 * m + h):P * (2 * m + h + 1)],
                                              xT[:, k, :], start=k == 0, stop=k == KT - 1)
                            last.then_inc(pe_done, 1)

                def attend_values(kind, heads, probs, values, width):
                    pe.wait_ge(probs_ready[kind], l + 1)
                    for key in attend(kind):
                        if key[0] == f"pt{kind}":
                            n = key[1]
                            h = heads(n // 2, n % 2)
                            transposes("layer", key, [probs[:, h, P * m:P * m + P] for m in range(3)], l)
                        else:
                            r = key[1]
                            for g in range(2):
                                wait_emptied(pe, "layer", (f"pt{kind}", 2 * r + g), l)
                            bank = open_bank(pe, "layer", key, l)
                            for g in range(2):
                                v = width(heads(r, g))
                                p = pt[:, (2 * r + g) % 4, :]
                                o = bank[64 * g:64 * g + 64, :]
                                mm(o[:, 0:SEQ], values[:, 0, v:v + 64], p[:, 0:SEQ], start=True, stop=False)
                                last = mm(o[:, P:SEQ], values[:, 1, v:v + 64], p[:, SEQ:3 * P], start=False, stop=True)
                            last.then_inc(pe_done, 1)

                gate_panels("b")
                wait_emptied(pe, "layer", ("av",), l)
                attend_values("a", lambda r, g: r + 4 * g, za, av, lambda h: 64 * (h // 4))
                pe.wait_ge(yb_ready, l + 1)
                project_T(("mb",), panel(l, D), yb, tiles=4, k_tiles=4)
                gate_panels("a")
                wait_emptied(pe, "layer", ("pva", 3), l)
                project_T(("ma",), panel(l, D), ya, tiles=4, k_tiles=4)
                gate_panels("c")
                wait_emptied(pe, "layer", ("cv", 0), l)
                wait_emptied(pe, "layer", ("cv", 1), l)
                attend_values("c", lambda r, g: 2 * r + g, zc, cv, lambda h: 64 * h)
                wait_emptied(pe, "layer", ("pvc", 3), l)
                project_T(("mc",), panel(l, D), yc, tiles=4, k_tiles=4)
                pe.wait_ge(merged_ready, l + 1)
                for n in range(2):
                    project([("wo", n, 0), ("wo", n, 1)], panel(l, HALF), merged)
                transpose_x("x1T", x1_ready)
                pe.wait_ge(cT_ready, 1)

                def ada(p):
                    slot = panel(l, HALF)
                    bank = open_bank(pe, "layer", ("ada", p), l)
                    for k in range(KT):
                        for j in range(4):
                            last = mm(bank[32 * j:32 * j + 32, 0:P], cT[:, k, :], slot[:, k, P * j:P * j + P],
                                      start=k == 0, stop=k == KT - 1)
                    last.then_inc(pe_done, 1)

                def ada_T(p):
                    wait_emptied(pe, "layer", ("ada", p), l)
                    transposes("layer", ("adaT", p), [ada_rows[:, p % 2, :]], l)

                for p in range(FFN_TILES // 2):
                    slot = panel(l, HALF)
                    for h in range(2):
                        bank = open_bank(pe, "layer", ("ff", 2 * p + h), l)
                        for u in range(2):
                            for k in range(KT):
                                last = mm(bank[:, SEQ * u:SEQ * u + SEQ], slot[:, k, SEQ * u + P * h:SEQ * u + P * h + P],
                                          xT[:, k, :], start=k == 0, stop=k == KT - 1)
                        last.then_inc(pe_done, 1)
                    if p:
                        wait_emptied(pe, "layer", ("ada", p - 1), l)
                    ada(p)
                    if p:
                        ada_T(p - 1)
                ada(11)
                ada_T(10)
                down = {(t, n): open_bank(pe, "layer", ("dn", t, n), l) for t in range(TT) for n in range(2)}
                wait_emptied(pe, "layer", ("ff", FFN_TILES - 1), l)
                for f in range(0, FFN_TILES, 4):
                    slot = panel(l, D)
                    rows_here = range(f, min(f + 4, FFN_TILES))
                    for t in range(TT):
                        for r in rows_here:
                            for n in range(2):
                                last = mm(down[t, n], hid[:, r, P * t:P * t + P], slot[:, r - f, HALF * n:HALF * n + HALF],
                                          start=r == 0, stop=r == FFN_TILES - 1)
                                if r == FFN_TILES - 1:
                                    last.then_inc(pe_done, 1)
                    if r < FFN_TILES - 1:
                        last.then_inc(pe_done, 1)
                ada_T(11)
            state["panel"] += (DEPTH - 1) * LAYER_PANELS
            state["per"] = 0
            if second:
                second["tensor"](pe)

        @block.scalar
        def _(act):
            act.dma_start(const[:, :], K["const"]).then_inc(const_loaded, 16)
            act.dma_start(arena[:, 15360:16128], K["dist"]).then_inc(const_loaded, 16)

            def rows_of(dst, at, src):
                n = src.shape[0]
                act.dma_start(dst[at:at + n, :], src).then_inc(par_loaded, 16)
                return at + n

            at = rows_of(par_rows, 0, I["ada_b_2"].rearrange("l (m d) -> (l m) d", d=P))
            at = rows_of(par_rows, at, I["norm_mix_g_2"].rearrange("l (m d) -> (l m) d", d=P))
            rows_of(par_rows, at, I["norm_ffn_g_2"].rearrange("l (m d) -> (l m) d", d=P))
            at = rows_of(par2_rows, 0, I["mlstm_conv_w_2"].rearrange("a w (m d) -> (a w m) d", d=P))
            at = rows_of(par2_rows, at, I["mlstm_conv_b_2"].rearrange("a (m d) -> (a m) d", d=P))
            at = rows_of(par2_rows, at, I["c_2"].rearrange("a (m d) -> (a m) d", d=P))
            at = rows_of(par2_rows, at, I["c_ctx_2"].rearrange("(m d) -> m d", d=P))
            at = rows_of(par2_rows, at, I["conv_w"].rearrange("l w (m d) -> (l w m) d", d=P))
            assert at == 88
            step = Chain(act, act_step)
            S.update(astep=step)
            A = nc.scalar.activation
            act.wait_ge(c_cols_ready, 1)
            for n in range(2):
                ins = A(cT[:, :, n], par2[:, 48 + 8 * n:56 + 8 * n], ACT.Silu)
            ins.then_inc(cT_ready, 1)

            with act.Fori(0, DEPTH) as l:
                step.enter(l, 1)

                def take(key, dst, func=ACT.Copy, part=None):
                    bank, freed = full_bank(act, "layer", key, l)
                    bank = bank if part is None else bank[:, 0:part]
                    if len(dst.shape) == 3:
                        bank = view(bank, dst.shape[1], dst.shape[2])
                    A(dst, bank, func).then_inc(freed, 1)

                def exps(kind, z):
                    act.wait_ge(nmax_ready[kind], l + 1)
                    for h in range(HEADS):
                        for t, (a, b) in enumerate(((0, P), (P, 3 * P))):
                            last = A(z[:, h, a:b], z[:, h, a:b], ACT.Exp, bias=nmax[:, 8 * t + h:8 * t + h + 1],
                                     scale=SCALE, accum_out=sums[:, 8 * t + h:8 * t + h + 1])
                    return last

                def gates_out(kind, dst):
                    for m in range(4):
                        take((f"g{kind}", m), dst[:, 2 * m:2 * m + 2, :], ACT.Sigmoid)

                def values_out(kind, dst):
                    for key in attend(kind):
                        if key[0] == f"pt{kind}":
                            take(key, pt[:, key[1] % 4, :], part=384)
                        else:
                            take(key, dst[:, key[1], :], part=SEQ)

                def take_x(name):
                    for t in range(TT):
                        for m in range(2):
                            take((name, t, m), xT[:, 4 * m:4 * m + 4, P * t:P * t + P])

                take_x("xT")
                for b in range(3):
                    for m in range(2):
                        take(("b", b, m), bpart[:, b, 2 * m:2 * m + 2, :])
                for m in range(2):
                    take(("aq", m), aq[:, 2 * m:2 * m + 2, :])
                take(("ak",), ak, part=SEQ)
                take(("av",), av, part=SEQ)
                for name, dst in (("cq", cq), ("ck", ck)):
                    for m in range(2):
                        take((name, m), dst[:, 2 * m:2 * m + 2, :])
                exps("a", za).then_inc(exp_ready["a"], 1)
                act.wait_ge(exp_ready["a"], 2 * l + 1)
                step(A(sink_e, recip, ACT.Exp))
                A(sink_e[:, 0:1], sink_e[:, 0:1], ACT.Copy).then_inc(exp_ready["a"], 1)
                for t in range(TT):
                    take(("cv", t), cv[:, t, :])
                gates_out("b", gate_bc)
                exps("c", zc).then_inc(exp_ready["c"], 1)
                values_out("a", ya)
                gates_out("a", gate_a)
                wait_emptied(act, "layer", ("mb", 3), l)
                gates_out("c", gate_bc)
                values_out("c", yc)
                def roots(n):
                    for t in range(TT):
                        act.wait_ge(var_ready, 4 * l + 2 * n + t + 1)
                        A(rstd[:, t:t + 1], rstd[:, t:t + 1], ACT.Sqrt).then_inc(std_ready, 1)

                roots(0)
                take_x("x1T")
                for p in range(FFN_TILES // 2):
                    for f in (2 * p, 2 * p + 1):
                        bank, _ = full_bank(act, "layer", ("ff", f), l)
                        if f >= 4:
                            wait_emptied(act, "layer", ("ff", f - 4), l)
                        A(sil[:, f % 4, :], bank[:, 0:SEQ], ACT.Silu).then_inc(sil_ready, 1)
                    take(("ada", p), ada_rows[:, p % 2, :], part=P)
                take(("ada", 11), ada_rows[:, 1, :], part=P)
                roots(1)
            step.leave(DEPTH)
            if second:
                second["scalar"](act)

        @block.vector
        def _(dve):
            V = nc.vector
            step = Chain(dve, dve_step)
            S.update(vstep=step)
            TS, STT, TTo = V.tensor_scalar, V.scalar_tensor_tensor, V.tensor_tensor

            for b in range(BANKS):
                V.memset(st[:, b:b + 1], 0.0).then_inc(bank_free[b], 1)
            step(V.memset(mods_now[:, :, :], 0.0))
            step(V.memset(cT[:, :, :], 0.0))
            bank, freed = full_bank(dve, "pre", ("par", 0))
            V.tensor_copy(par[:, :], bank[:, 0:128])
            V.tensor_copy(par2[:, :], bank[:, 128:216]).then_inc(freed, 1)
            wait_emptied(dve, "pre", ("par", 0))
            V.memset(st[:, 253:254], 0.0).then_inc(c_cols_ready, 1)
            dve.wait_ge(x_loaded, 16)
            for m in range(TT):
                V.memset(st[:, 240 + m:241 + m], 0.0).then_inc(x_ready, 1)
            dve.wait_ge(const_loaded, 32)

            with dve.Fori(0, DEPTH) as l:
                step.enter(l, DVE_LAYER)
                step(V.tensor_copy(mods_0[:, :, :], mods_now[:, :, :]))
                step(V.tensor_copy(conv_w[:, :, :], view(par2[:, bass.ds(64 + l * 12, 12)], 3, 4)))

                for m in range(2):
                    wait_emptied(dve, "layer", ("b", 2, m), l)
                bh, bb, bc = bpart[:, 0], bpart[:, 1], bpart[:, 2]
                step(TTo(bh, bh, bc, ALU.mult))
                for tap in (2, 1, 0):
                    s = 2 - tap
                    for m in range(4):
                        w = conv_w[:, tap, m:m + 1]
                        if s == 0:
                            ins = TS(yb[:, m, :], bh[:, m, :], w, None, ALU.mult)
                        else:
                            ins = STT(out=yb[:, m, s:SEQ], in0=bh[:, m, 0:SEQ - s], scalar=w, in1=yb[:, m, s:SEQ],
                                      op0=ALU.mult, op1=ALU.add)
                    step(ins)
                TTo(yb, yb, bb, ALU.mult).then_inc(yb_ready, 1)

                def logits(kind, z, dist, slopes):
                    for h in range(HEADS):
                        bank, freed = full_bank(dve, "layer", (f"s{kind}", h), l)
                        STT(out=z[:, h, :], in0=dist, scalar=slopes[h] / SCALE, in1=bank[:, 0:384],
                            op0=ALU.mult, op1=ALU.add).then_inc(freed, 1)
                    for h in range(HEADS):
                        wait_emptied(dve, "layer", (f"s{kind}", h), l)
                    V.reduce_max(rmax[:, 0:8], z[:, :, 0:P], X_AXIS)
                    step(V.reduce_max(rmax[:, 8:16], z[:, :, P:3 * P], X_AXIS))

                def normalise(kind, z):
                    step(V.reciprocal(recip, sums))
                    TTo(z[:, :, 0:P], z[:, :, 0:P], spread(recip[:, 0:8], P), ALU.mult)
                    TTo(z[:, :, P:3 * P], z[:, :, P:3 * P], spread(recip[:, 8:16], 2 * P),
                        ALU.mult).then_inc(probs_ready[kind], 1)

                logits("a", za, dist_a, SLOPES[0:8])
                dve.wait_ge(sinks_loaded, l * 16 + 16)
                TS(nsink[:, 0:8], sinks, -1.0, None, ALU.mult)
                step(TS(nsink[:, 8:16], sinks, -1.0, None, ALU.mult))
                step(STT(out=nmax, in0=rmax, scalar=-SCALE, in1=nsink, op0=ALU.mult, op1=ALU.min))
                TTo(recip, nmax, nsink, ALU.subtract).then_inc(nmax_ready["a"], 1)
                dve.wait_ge(nmax_ready["a"], l + 1)
                V.memset(st[:, 252:253], 0.0).then_inc(sinks_used, 1)
                dve.wait_ge(exp_ready["a"], 2 * l + 2)
                step(TTo(sums, sums, sink_e, ALU.add))
                normalise("a", za)
                dve.wait_ge(probs_ready["a"], l + 1)
                logits("c", zc, dist_c, SLOPES[8:16])
                TS(nmax, rmax, -SCALE, None, ALU.mult).then_inc(nmax_ready["c"], 1)
                dve.wait_ge(exp_ready["c"], l + 1)
                normalise("c", zc)

                def merge(kind, gate, first=False):
                    for m in range(4):
                        bank, freed = full_bank(dve, "layer", (f"m{kind}", m), l)
                        wait_emptied(dve, "layer", (f"g{kind}", m), l)
                        g, o = gate[:, 2 * m:2 * m + 2, :], merged[:, 2 * m:2 * m + 2, :]
                        TTo(o if first else g, g, view(bank, 2, SEQ), ALU.mult).then_inc(freed, 1)
                        wait_emptied(dve, "layer", (f"m{kind}", m), l)
                        if not first:
                            ins = TTo(o, o, g, ALU.add)
                            if kind == "c" and m == 3:
                                ins.then_inc(merged_ready, 1)
                            else:
                                step(ins)

                merge("b", gate_bc, first=True)
                merge("a", gate_a)
                merge("c", gate_bc)

                def add_residual(keys):
                    for key in keys:
                        bank, freed = full_bank(dve, "layer", key, l)
                        t, n = (key[2], key[1]) if key[0] == "wo" else key[1:]
                        xs = x[:, t, HALF * n:HALF * n + HALF]
                        STT(out=xs, in0=xs, scalar=ALPHA, in1=bank, op0=ALU.mult, op1=ALU.add).then_inc(freed, 1)
                    for key in keys:
                        wait_emptied(dve, "layer", key, l)

                def layer_norm(n, t, loaded, done):
                    for m in range(2):
                        ins = V.bn_stats(bst[:, t, m, :], x[:, t, HALF * m:HALF * m + HALF])
                    step(ins)
                    V.memset(st[:, 255:256], 0.0)
                    step(V.bn_aggr(mv[:, t, :], bst[:, t, :, :]))
                    TS(rstd[:, t:t + 1], mv[:, t, 1:2], LN_EPS, None, ALU.add).then_inc(var_ready, 1)
                    dve.wait_ge(loaded, l * 32 + 32)
                    step(STT(out=x[:, t, :], in0=x[:, t, :], scalar=mv[:, t, 0:1], in1=lnp[:, 0, :], op0=ALU.subtract,
                             op1=ALU.mult))
                    dve.wait_ge(std_ready, 4 * l + 2 * n + t + 1)
                    step(V.reciprocal(rstd[:, t:t + 1], rstd[:, t:t + 1]))
                    STT(out=x[:, t, :], in0=x[:, t, :], scalar=rstd[:, t:t + 1], in1=lnp[:, 1, :], op0=ALU.mult,
                        op1=ALU.add).then_inc(done, 1)

                add_residual([("wo", 0, 0), ("wo", 0, 1), ("wo", 1, 0)])
                layer_norm(0, 0, ln1_loaded, x1_ready)
                add_residual([("wo", 1, 1)])
                layer_norm(0, 1, ln1_loaded, x1_ready)
                dve.wait_ge(x1_ready, 2 * l + 2)

                def mods_out(p):
                    bank, freed = full_bank(dve, "layer", ("adaT", p), l)
                    V.tensor_copy(mods_now[:, 4 * p:4 * p + 4, :], view(bank[:, 0:P], 4, 32)[:, :, 0:2]).then_inc(freed, 1)

                for p in range(FFN_TILES // 2):
                    for f in (2 * p, 2 * p + 1):
                        bank, freed = full_bank(dve, "layer", ("ff", f), l)
                        dve.wait_ge(sil_ready, l * FFN_TILES + f + 1)
                        TTo(hid[:, f, :], sil[:, f % 4, :], bank[:, SEQ:2 * SEQ], ALU.mult).then_inc(freed, 1)
                    if p:
                        mods_out(p - 1)
                mods_out(10)
                for t in range(TT):
                    add_residual([("dn", t, n) for n in range(2)])
                    layer_norm(1, t, ln2_loaded, x_ready)
                dve.wait_ge(x_ready, 2 * l + 4)
                mods_out(11)
                wait_emptied(dve, "layer", ("adaT", 11), l)
            step.leave(DEPTH)
            if second:
                second["vector"](dve)


INPUTS = [
    "x", "w_in", "attn_sinks", "conv_w", "w_branch_a", "w_branch_b", "w_branch_c", "w_out", "ln1_g", "ln1_b",
    "w_ffn_gate", "w_ffn_up", "w_ffn_down", "ln2_g", "ln2_b", "c_2", "ctx_2", "c_ctx_2", "ada_w_2", "ada_b_2",
    "norm_mix_g_2", "norm_ffn_g_2", "final_norm_g_2", "mlstm_w_in_2", "mlstm_conv_w_2", "mlstm_conv_b_2",
    "mlstm_igate_b_2", "mlstm_fgate_b_2", "mlstm_head_norm_g_2", "mlstm_w_out_2", "ret_w_in_2",
    "ret_decay_logit_2", "ret_group_norm_g_2", "ret_w_out_2", "moe_router_2", "moe_w_gate_2", "moe_w_up_2",
    "moe_w_down_2",
]


def shape_constants():
    import numpy as np
    f = np.float32
    p = np.arange(P)
    eye = np.eye(P)
    swapped = np.where((p ^ 32)[:, None] == p[None, :], 1.0, 0.0)
    iota = np.tile(np.arange(SEQ), (P, 1))
    quad = (p[:, None] // 32 == np.arange(4)[None, :])
    later = np.where(p[:, None] > p[None, :], -1e30, 0.0)
    earlier = np.where(p[:, None] < p[None, :], -1e30, 0.0)
    const = np.concatenate([eye, swapped, iota, np.stack([p, p + P], 1), quad, later, earlier,
                            np.ones((P, 2)), np.arange(P)[None, :] % 32 == p[:, None]], 1).astype(f)
    q = np.concatenate([np.tile(p[:, None], (1, P)), np.tile(p[:, None] + P, (1, 2 * P))], 1)
    k = np.concatenate([p, np.arange(2 * P)])[None, :]
    gap = q - k
    dist_a = np.where((gap >= 0) & (gap < P), -gap, -1e30)
    dist_c = np.where(gap >= 0, -gap, -1e30)
    dist = np.concatenate([dist_a, dist_c], 1).astype(f)
    kk = np.stack([p, p + P], 1)[:, :, None]
    qq = np.arange(SEQ)[None, None, :]
    ret = np.stack([np.maximum(qq - kk, 0), np.maximum(kk - qq, 0), qq + SEQ - kk, SEQ - qq + kk, (qq == kk) + 0 * kk], 1)
    ret = ret.reshape(P, 5 * 2 * SEQ).astype(f)
    nf = 32
    inv = (np.float32(10000.0) ** (-np.arange(nf, dtype=f) / f(nf))).astype(f)
    t = np.arange(SEQ)
    ang_r = ((t // 64).astype(f)[None, :] * inv[:, None]).astype(f)
    ang_c = ((t % 64).astype(f)[None, :] * inv[:, None]).astype(f)
    ang = np.concatenate([ang_r, ang_r, ang_c, ang_c], 0)
    sign = np.where((p // 32) % 2 == 0, -1.0, 1.0)[:, None]
    rope = np.concatenate([np.cos(ang), sign * np.sin(ang)], 1).astype(f)
    return {"const": const, "dist": dist, "ret": ret, "rope": rope}


def kernel(**inputs):
    import numpy as _np
    import concourse.bacc as _bacc
    from concourse.bass_utils import run_bass_kernel_spmd as _run

    nc = _bacc.Bacc("TRN2", target_bir_lowering=False, num_devices=1)
    arrays, I, K = {}, {}, {}
    for name in INPUTS:
        a = _np.ascontiguousarray(inputs[name])
        arrays[f"in_{name}"] = a
        I[name] = nc.dram_tensor(f"in_{name}", a.shape, mybir.dt.from_np(a.dtype), kind="ExternalInput").ap()
    for name, a in shape_constants().items():
        arrays[f"const_{name}"] = a
        K[name] = nc.dram_tensor(f"const_{name}", a.shape, F32, kind="ExternalInput").ap()
    out = nc.dram_tensor("out", (1, SEQ, D), F32, kind="ExternalOutput").ap()
    program(nc, I, K, out)
    r = _run(nc, [arrays], core_ids=[0])
    return r.results[0]["out"]
```

```python
import concourse.bass as bass
from concourse import mybir
from contextlib import ExitStack

F32 = mybir.dt.float32
U32 = mybir.dt.uint32
ALU = mybir.AluOpType
ACT = mybir.ActivationFunctionType
X_AXIS = mybir.AxisListType.X

P = 128
D = 1024
KT = D // P
SEQ = 256
TT = SEQ // P
DEPTH = 2
ALPHA = (2 * DEPTH) ** 0.25
LN_EPS = 1e-5
RMS_EPS = 1e-6
HEADS = 8
HD = 64
SCALE = HD ** -0.5
SLOPES = [2.0 ** (-8.0 * (i + 1.0) / 16) for i in range(16)]
HALF = 512
HIDDEN = 2816
FFN_TILES = HIDDEN // P
RING = 6
PANEL = 4096
EXPERTS = 16
SLOTS = 32
BANKS = 8
COLS = {}
_at = 0
for _name, _n in (("a_q", 512), ("a_k", 128), ("a_v", 128), ("b_h", 512), ("b_b", 512), ("b_c", 512),
                  ("c_q", 512), ("c_k", 512), ("c_v", 512), ("g_a", D), ("g_b", D), ("g_c", D)):
    COLS[_name] = _at
    _at += _n


class BankPlan:
    REL, EV = "rel", "ev"

    def __init__(self):
        self.events, self.panels = 0, 0
        self.used = [0] * BANKS
        self.units, self.release, self.stage_panels = {}, {}, {}

    def plan(self, stage, entries, times=1):
        here, ev, n, pan = [0] * BANKS, 0, 0, []
        units = []
        for e in entries:
            if e == self.REL:
                pan.append(ev)
            elif e == self.EV:
                ev += 1
                pan.append(ev)
            else:
                ev += 1
                b = n % BANKS
                units.append((e, b, ev, here[b]))
                here[b] += 1
                n += 1
        for e, b, v, u in units:
            assert (stage, e) not in self.units, (stage, e)
            self.units[stage, e] = (b, self.events + v, ev, self.used[b] + u, here[b])
        self.stage_panels[stage] = (self.panels, len(pan))
        for i in range(times):
            for m, v in enumerate(pan):
                self.release[self.panels + i * len(pan) + m] = (self.events + i * ev + v, ev, len(pan))
        self.panels += len(pan) * times
        self.events += ev * times
        self.used = [a + h * times for a, h in zip(self.used, here)]

    def bank(self, stage, key):
        return self.units[stage, key][0]

    def full(self, stage, key, i=0):
        _, v, per, _, _ = self.units[stage, key]
        return i * per + v

    def free(self, stage, key, i=0):
        _, _, _, u, per = self.units[stage, key]
        return i * per + (u + 1)

    def emptied(self, stage, key, i=0):
        _, _, _, u, per = self.units[stage, key]
        return i * per + (u + 2)


class Chain:

    def __init__(self, eng, sem):
        self.eng, self.sem, self.n, self.off = eng, sem, 0, 0

    def __call__(self, ins):
        ins.then_inc(self.sem, 1)
        self.n += 1
        self.eng.wait_ge(self.sem, self.off + self.n)

    def enter(self, i, per):
        self.start, self.off, self.per = self.n, i * per, per

    def leave(self, times):
        got = self.n - self.start
        assert got == self.per, f"steps in the loop: {got}, not {self.per}"
        self.n = self.start + self.per * times
        self.off = 0


def view(ap, *dims):
    names = "abcd"[:len(dims)]
    return ap.rearrange(f"p ({' '.join(names)}) -> p {' '.join(names)}", **dict(zip(names[1:], dims[1:])))


def spread(ap, n):
    return ap.unsqueeze(2).to_broadcast([ap.shape[0], ap.shape[1], n])
BLOCK1_ONLY = False
OUT_STORES = 2
DVE_LAYER = 36


STREAMS = 2
CTX, LAT = 0, 1
DV = D // HEADS
CONV_TAPS = 5
GROUPS = EXPERTS // 4


def fwd_col(jt, it):
    return (0, 512, 896, 1152)[jt] + P * (it - jt)


def bwd_col(jt, it):
    return {(0, 0): 0, (0, 2): 128, (0, 3): 256, (1, 0): 384, (1, 1): 512, (1, 2): 640, (1, 3): 768,
            (2, 2): 896, (3, 2): 1024, (3, 3): 1152}[jt, it]


SEEN = [[(0,), (0, 1), (0, 1, 2), (0, 1, 2, 3)], [(0, 1), (1,), (0, 1, 2, 3), (0, 1, 3)]]
COL = [fwd_col, bwd_col]


BEFORE0 = [("o", 0, 0), ("o", 0, 1)]
BESIDE0 = {0: [("o", 0, 2), ("o", 0, 3)], 1: [("v", 1, 0)], 2: [("v", 1, 1)], 3: [("v", 1, 2), ("v", 1, 3)],
           4: [("o", 1, 0), ("o", 1, 1)], 5: [("o", 1, 2), ("o", 1, 3)]}
BESIDE1 = {0: [("v", 1, 0), ("v", 1, 1)], 1: [("v", 1, 2), ("v", 1, 3)], 2: [("g", 0, 2), ("g", 0, 3)],
           4: [("g", 1, 2), ("g", 1, 3)]}


def streams_of(layer):
    return (CTX, LAT) if layer == 0 else (LAT,)


def plan_second(banks):
    R = BankPlan.REL
    hT = [("hT", k) for k in range(KT)]
    mix0 = list(hT)
    mix0 += [("qk", m) for m in range(4)] + [R] + [("qk", m) for m in range(4, 8)] + [R] + [("gr",)]
    mix0 += [("v", 0, t) for t in range(4)] + [R] + BEFORE0 + [("aT",)]
    for h in range(HEADS + 1):
        if h < HEADS:
            mix0 += [("mb", h, 0), ("mb", h, 1), ("s", h, 0), ("s", h, 1), ("s", h, 2)]
        for key in BESIDE0.get(h, ()):
            mix0 += [key] + [R] * (key[2] == 3)
        if h == HEADS - 1:
            mix0 += [("gbc", s, n) for s in (CTX, LAT) for n in range(2)]
        if h:
            mix0 += [("h", h - 1, i) for i in range(4)]
    mix0 += [("yT", k) for k in range(KT)]
    for n in range(2):
        mix0 += [("wo", n, t) for t in range(4)] + [R]
    banks.plan("mix0", mix0)
    for m in range(2):
        banks.release[banks.stage_panels["mix0"][0] + m] = (banks.full("mix0", ("h", HEADS - 1, 3)), 0, 0)
    plan_moe(banks, 0)
    mix1 = list(hT)
    for n in range(2):
        mix1 += [("q", n, 0), ("q", n, 1), R, ("qs", n, 0), ("qs", n, 1)]
    for n in range(2):
        mix1 += [("k", 4 * n + m) for m in range(4)] + [R] + [("ks", 2 * n), ("ks", 2 * n + 1)]
    mix1 += [("v", 0, t) for t in range(4)] + [R]
    for h in range(HEADS + 1):
        if h < HEADS:
            mix1 += [("s", h, 0), ("s", h, 1)]
        for key in BESIDE1.get(h, ()):
            mix1 += [key] + [R] * (key[2] == 3)
        if h == HEADS - 1:
            mix1 += [("gbc", LAT, n) for n in range(2)]
        if h:
            mix1 += [("o", h - 1)]
    mix1 += [("yT", m) for m in range(4)]
    for n in range(2):
        mix1 += [("wo", n, 2), ("wo", n, 3), R]
    banks.plan("mix1", mix1)
    banks.release[banks.stage_panels["mix1"][0] + 2] = (banks.full("mix1", ("o", HEADS - 1)), 0, 0)
    plan_moe(banks, 1)


def plan_moe(banks, layer):
    R, EV = BankPlan.REL, BankPlan.EV
    src = streams_of(layer)
    gather = [("x", s, m) for s in src for m in range(2)]
    moe = [("gbc", s, n) for s in src for n in range(2)] + [("hT", k) for k in range(KT)] + [("lgT",), ("lg",), ("afT",)]
    moe += [("idx", s) for s in src] + [("it",), ("rep",)] + gather
    banks.plan(f"moe{layer}", moe)
    per = []
    for q in range(4):
        per += [EV, ("g", q), R, EV, ("u", q), R, ("t", q)] + gather * (q == 3) + [EV, ("y", q), R]
    per += [("c", s, t, n) for s in src for t in range(TT) for n in range(2)]
    banks.plan(f"exp{layer}", per, GROUPS)


def second_block(nc, ctx, banks, I, K, out, S):
    def sb(name, shape, dt=F32):
        return ctx.enter_context(nc.sbuf_tensor(name, shape, dt))

    def sem(name):
        return ctx.enter_context(nc.semaphore(name))

    ring, arena, ht, x, c, lnp, const, st = (S[n] for n in ("ring", "arena", "ht", "x", "c", "lnp", "const", "st"))
    ident, swap_mat, iota, tok_col, quad = (S[n] for n in ("ident", "swap_mat", "iota", "tok_col", "quad"))
    later_key, earlier_key, par, par2 = (S[n] for n in ("later_key", "earlier_key", "par", "par2"))
    mods = [S["mods_0"], S["mods_now"]]
    psum, pe_done, panel_in = S["psum"], S["pe_done"], S["panel_in"]
    one_col, rep_mat = const[:, 774:775], const[0:32, 776:904]

    router = sb("router", [P, DEPTH, P])
    coef = view(st[:, 146:210], 4, STREAMS, KT)
    ss, rs = st[:, 0:4], st[:, 4:8]
    hT = view(ht[:, :], KT, 2 * SEQ)
    tokens = [c[:, 0, :], c[:, 1, :], x[:, 0, :], x[:, 1, :]]
    lflat = lnp[:, :, :].rearrange("p a b -> p (a b)")
    qk = view(arena[:, 0:4096], KT, 2 * SEQ)
    va = view(arena[:, 4096:8224], 4, HEADS, DV + 1)
    og = view(arena[:, 8224:12320], 4, D)
    qk_pad = view(arena[:, 12320:14400], 4, STREAMS, SEQ + 4)
    conv_acc = view(arena[:, 14400:15424], 2, STREAMS, SEQ)
    gate_rows = arena[:, 15424:15936]
    xh0 = view(arena[:, 8224:12320], 4, D)
    lf_rows, b_rows = arena[:, 12320:12832], arena[:, 12832:13344]
    one_rows, t_rows = arena[:, 13344:13856], arena[:, 13856:14368]
    m_diag = view(arena[:, 12832:13856], 2, HALF)
    yt = view(arena[:, 13856:14880], 2, 4, DV)
    wbuf = [[ring[:, m, 0:1280], ring[:, m, 1280:2560]] for m in range(2)]
    wg32, wg = view(arena[:, 15936:16192], KT, 32), view(lnp[:, 1, :], KT, P)
    m_neg = view(lnp[:, 1, :], 2, HALF)
    aT = view(ring[:, 0, 2560:2816], 4, 64)
    em = view(arena[:, 16160:16320], 4, 40)
    head_ss, r2 = view(st[:, 32:64], 4, HEADS), st[:, 64:72]
    gate_bias = st[:, 251:252]
    gb = view(ht[:, 0:2048], STREAMS, D)
    gate_diag = view(ht[:, 2048:4096], 4, 4, P)
    res_tmp = view(ht[:, 3072:4096], 2, HALF)
    xh = view(arena[:, 8192:12288], 4, D)
    x_four = view(arena[:, 0:2048], KT, 4, 64)
    gb_moe = view(arena[:, 2048:4096], STREAMS, D)
    y_four = view(arena[:, 4096:6144], STREAMS, D)
    sil_e = view(arena[:, 6144:7168], 2, HALF)
    pick_now = view(arena[:, 14592:15104], STREAMS, TT, P)
    back_now = view(arena[:, 15360:15872], STREAMS, SEQ)
    pick = view(ht[:, 0:2048], STREAMS, TT, GROUPS, P)
    spread_back = view(ht[:, 2048:4096], STREAMS, GROUPS, SEQ)
    hid_e, hidT = view(lflat[:, 0:1024], 2, HALF), view(lflat[:, 1024:2048], 2, HALF)
    s0 = 12288
    logit, aff2 = arena[:, s0:s0 + 64], view(arena[:, s0 + 64:s0 + 192], TT, 64)
    lmax = arena[:, s0 + 192:s0 + 196]
    aff_T, aff_work = arena[0:64, s0 + 256:s0 + 512], arena[0:64, s0 + 512:s0 + 768]
    top_val, top_idxf = arena[0:64, s0 + 768:s0 + 800], arena[0:64, s0 + 800:s0 + 832]
    top_idx = arena[0:64, s0 + 832:s0 + 864].bitcast(U32)
    block_idx = view(arena[0:64, s0 + 1024:s0 + 2048], STREAMS, HALF)
    logit_T = arena[0:EXPERTS, s0 + 1024:s0 + 1536]
    sel_T = arena[0:32, s0 + 2048:s0 + 2176]
    sel_m = view(arena[:, s0 + 2176:s0 + 2208], STREAMS, GROUPS, 4)
    sel = view(arena[:, s0 + 2240:s0 + 2256], 2, STREAMS, GROUPS)
    qT, kT = view(arena[:, 0:2048], HEADS, SEQ), view(arena[:, 2048:6144], HEADS, 2 * SEQ)
    rv, rg = view(arena[:, 6144:10240], 4, D), view(arena[:, 10240:12288], TT, D)
    xh1 = view(arena[:, 12288:16384], 4, D)
    gaps = view(arena[:, 12288:14848], 5, HALF)
    rope_t = view(arena[:, 14848:15360], 2, SEQ)
    rot_a, rot_b = arena[:, 15360:15872], arena[:, 15872:16384]
    dec = view(ring[:, 4, :], 2, 4, HALF)
    ry = c[:, :, :]
    ryT = view(arena[:, 2048:4096], KT, SEQ)
    rsq = view(arena[:, 15360:15872], TT, 2, DV)
    logg, logg_t, mean = st[:, 80:96], st[:, 96:112], st[:, 128:144]
    mean_th, var_th = view(mean, TT, HEADS), view(st[:, 112:128], TT, HEADS)

    names = ("ctx_loaded", "gain_loaded", "wg_loaded", "gbias_clear", "gbias_loaded", "router_loaded", "ret_loaded",
             "decay_loaded", "gain_free", "squares_ready", "ms_ready", "rms_ready", "xh_ready", "conv_ready", "silu_ready",
             "wg_ready", "abs_ready", "softplus_ready", "rows_ready", "mdiag_ready", "exp_w_ready", "w_ready",
             "yt_ready", "head_ss_ready", "head_ms_ready", "head_rms_ready", "og_ready", "diag_ready", "streams_ready",
             "shift_ready", "aff_exp_ready", "aff_ready", "top_ready", "block_ready", "pick_ready", "back_ready",
             "sil_e_ready", "raw_ready", "logg_abs_ready", "logg_sp_ready", "logg_ready", "decay_ready",
             "kt_ready", "final_ready", "inv_ready")
    Q = {n: sem(n) for n in names}

    def sync(sp, load_panel):
        n = [banks.stage_panels["mix0"][0]]

        def halves(src):
            v = src.rearrange("(h k p) n -> h p k n", h=2, p=P)
            return [(slice(4 * h, 4 * h + 4), v[h]) for h in range(2)]

        def load(width, parts):
            load_panel(n[0], width, parts)
            n[0] += 1

        def experts(layer):
            first = banks.stage_panels[f"exp{layer}"][0]
            assert first == n[0]
            w = [I[f"moe_w_{m}_2"] for m in ("gate", "up", "down")]
            per = 24

            def expert(q, e):
                for m in range(3):
                    for h in range(2):
                        slot = (first + 6 * q + 2 * m + h) % RING
                        src = w[m][layer, bass.ds(e, 1), :, :].rearrange("a k n -> (a k) n")
                        yield slot, 6 * q + 2 * m + h, (
                            D, src[HALF * h:HALF * h + HALF, :].rearrange("(g k p) n -> g p k n", g=2, p=P))

            for q in range(4):
                for slot, m, (width, halves_) in expert(q, q):
                    k = PANEL // width // 2
                    load(width, [(slice(k * g, k * g + k), halves_[g]) for g in range(2)])
            with sp.Fori(1, GROUPS) as g4:
                for q in range(4):
                    for slot, m, (width, halves_) in expert(q, g4 * 4 + q):
                        if m >= RING:
                            v, ev, _ = banks.release[first + m - RING]
                            sp.wait_ge(pe_done, g4 * ev + v)
                        else:
                            v, ev, _ = banks.release[first + per + m - RING]
                            sp.wait_ge(pe_done, g4 * ev + (v - ev))
                        k = PANEL // width // 2
                        s_ = view(ring[:, slot, :], PANEL // width, width)
                        for g in range(2):
                            sp.dma_start(s_[:, k * g:k * g + k, :], halves_[g]).then_inc(panel_in[slot], 16)
            n[0] += per * (GROUPS - 1)

        wi = I["mlstm_w_in_2"][0]
        for m in (0, 1, 2, 4, 3, 5):
            load(HALF, halves(wi[:, HALF * m:HALF * m + HALF]))
        for m in range(2):
            load(HALF, halves(I["mlstm_w_out_2"][0][:, HALF * m:HALF * m + HALF]))
        experts(0)
        assert n[0] == banks.stage_panels["mix1"][0]
        for m in range(8):
            load(HALF, halves(I["ret_w_in_2"][0][:, HALF * m:HALF * m + HALF]))
        for m in range(2):
            load(HALF, halves(I["ret_w_out_2"][0][:, HALF * m:HALF * m + HALF]))
        experts(1)
        for t in range(TT):
            sp.wait_ge(Q["final_ready"], t + 1)
            sp.dma_start(out[0, P * t:P * t + P, :], x[:, t, :]).then_inc(S["out_stored"], 16)

    def gpsimd(pool):
        pool.dma_start(c[:, :, :], I["ctx_2"][0].rearrange("(t p) d -> p t d", p=P)).then_inc(Q["ctx_loaded"], 16)
        for l in range(DEPTH):
            pool.dma_start(view(router[:, l, :], KT, EXPERTS),
                           I["moe_router_2"][l].rearrange("(k p) e -> p k e", p=P)).then_inc(Q["router_loaded"], 16)
        pool.wait_ge(Q["gbias_clear"], 1)
        pool.dma_start(wg32, I["mlstm_w_in_2"][0][:, 3072:3104].rearrange("(k p) n -> p k n", p=P)).then_inc(Q["wg_loaded"], 16)
        for m, name in enumerate(("igate", "fgate")):
            for d in range(2):
                r = 64 * m + 32 * d
                pool.dma_start(gate_bias[r:r + 8, :], I[f"mlstm_{name}_b_2"][0, d].rearrange("(h a) -> h a", a=1)
                               ).then_inc(Q["gbias_loaded"], 16)
        pool.dma_start(lnp[:, 0, :], I["mlstm_head_norm_g_2"].to_broadcast([P, D])).then_inc(Q["gain_loaded"], 16)
        pool.wait_ge(Q["gain_free"], 1)
        pool.dma_start(lnp[:, 0, :], I["ret_group_norm_g_2"].to_broadcast([P, D])).then_inc(Q["gain_loaded"], 16)
        pool.dma_start(logg, I["ret_decay_logit_2"].rearrange("a b h -> a (b h)").to_broadcast([P, 16])
                       ).then_inc(Q["decay_loaded"], 16)
        pool.wait_ge(pe_done, banks.full("mix1", ("hT", KT - 1)))
        pool.dma_start(arena[:, 12288:14848], K["ret"]).then_inc(Q["ret_loaded"], 16)
        pool.dma_start(arena[:, 14848:15360], K["rope"]).then_inc(Q["ret_loaded"], 16)
        pool.wait_ge(Q["gain_free"], 2)
        pool.dma_start(lnp[:, 0, :], I["final_norm_g_2"].rearrange("(a d) -> a d", a=1).to_broadcast([P, D])
                       ).then_inc(Q["gain_loaded"], 16)

    def tensor(pe):
        mm, panel, state, transposes = nc.tensor.matmul, S["panel"], S["state"], S["transposes"]
        open_bank, wait_emptied = S["open_bank"], S["wait_emptied"]

        def norm_T(stage, n, src, tiles):
            pe.wait_ge(Q["xh_ready"], 2 * n)
            for k in range(KT):
                transposes(stage, ("hT", k), [src[:, t, P * k:P * k + P] for t in tiles])
            for k in range(KT):
                wait_emptied(pe, stage, ("hT", k))

        def project_wide(stage, keys, slot, rhs, n=2 * SEQ):
            for m, key in enumerate(keys):
                bank = open_bank(pe, stage, key)
                for k in range(KT):
                    last = mm(bank[:, 0:n], slot[:, k, P * m:P * m + P], rhs[:, k, :], start=k == 0, stop=k == KT - 1)
                last.then_inc(pe_done, 1)

        def project(stage, keys, slot, lhs):
            for t, key in keys:
                bank = open_bank(pe, stage, key)
                for k in range(KT):
                    last = mm(bank, lhs[:, k, P * t:P * t + P], slot[:, k, :], start=k == 0, stop=k == KT - 1)
                last.then_inc(pe_done, 1)

        def gate_rows_bcast(stage, src, first):
            for m, (s, n) in enumerate((s, n) for s in src for n in range(2)):
                bank = open_bank(pe, stage, ("gbc", s, n))
                pe.wait_ge(Q["diag_ready"], first + m + 1)
                diag = gate_diag_of(stage)
                mm(bank, one_col.to_broadcast([P, P]), diag[:, m % diag.shape[1]].rearrange("p a b -> p (a b)"),
                   start=True, stop=True).then_inc(pe_done, 1)

        norm_T("mix0", 1, xh0, range(4))
        for n in range(2):
            project_wide("mix0", [("qk", 4 * n + m) for m in range(4)], panel(0, HALF), hT)
        bank = open_bank(pe, "mix0", ("gr",))
        pe.wait_ge(Q["wg_ready"], 1)
        for k in range(KT):
            last = mm(bank, wg[:, k, :], hT[:, k, :], start=k == 0, stop=k == KT - 1)
        last.then_inc(pe_done, 1)
        project("mix0", [(t, ("v", 0, t)) for t in range(4)], panel(0, HALF), hT)

        def beside(stage, keys):
            for key in keys:
                if key[2] == (2 if key[0] == "g" else 0):
                    state["beside"] = panel(0, HALF)
                project(stage, [(key[2], key)], state["beside"], hT)

        beside("mix0", BEFORE0)
        pe.wait_ge(Q["rows_ready"], 1)
        bank = open_bank(pe, "mix0", ("aT",))
        for m, rows in enumerate((gate_rows, b_rows)):
            for t in range(4):
                last = nc.tensor.transpose(bank[:, 256 * m + 64 * t:256 * m + 64 * t + 64], rows[0:64, P * t:P * t + P],
                                           ident[0:64, 0:64])
        last.then_inc(pe_done, 1)
        pe.wait_ge(Q["silu_ready"], 8)
        for h in range(HEADS + 1):
            if h in (1, 5):
                for t in range(4):
                    wait_emptied(pe, "mix0", ("v", h // 4, t))
            if h < HEADS:
                for d in range(2):
                    bank = open_bank(pe, "mix0", ("mb", h, d))
                    r = 32 * d + h
                    mm(bank, ident[0:64, r:r + 1].to_broadcast([64, P]), lf_rows[0:64, :], start=True,
                       stop=True).then_inc(pe_done, 1)
                q = qk[64 * (h % 2):64 * (h % 2) + 64, h // 2, :]
                k = qk[64 * (h % 2):64 * (h % 2) + 64, 4 + h // 2, :]
                for j in range(2):
                    bank = open_bank(pe, "mix0", ("s", h, j))
                    mm(bank, k[:, P * j:P * j + P], q, start=True, stop=True).then_inc(pe_done, 1)
                bank = open_bank(pe, "mix0", ("s", h, 2))
                for j in range(2):
                    last = mm(bank[:, SEQ * j:SEQ * j + SEQ], k[:, SEQ + P * j:SEQ + P * j + P], q[:, SEQ:2 * SEQ],
                              start=True, stop=True)
                last.then_inc(pe_done, 1)
            beside("mix0", BESIDE0.get(h, ()))
            if h == HEADS - 1:
                gate_rows_bcast("mix0", (CTX, LAT), 0)
            if h:
                w = wbuf[(h - 1) % 2]
                pe.wait_ge(Q["w_ready"], h)
                for i in range(4):
                    bank = open_bank(pe, "mix0", ("h", h - 1, i))
                    for d in range(2):
                        for j in SEEN[d][i]:
                            a = COL[d](j, i)
                            last = mm(bank[:, (DV + 1) * d:(DV + 1) * (d + 1)], w[d][:, a:a + P], va[:, j, h - 1, :],
                                      start=j == SEEN[d][i][0], stop=j == SEEN[d][i][-1])
                    last.then_inc(pe_done, 1)
        for k in range(KT):
            if k in (0, 6):
                pe.wait_ge(Q["og_ready"], 1 + k // 6)
            transposes("mix0", ("yT", k), [og[:, t, P * k:P * k + P] for t in range(4)])
        for k in range(KT):
            wait_emptied(pe, "mix0", ("yT", k))
        for n in range(2):
            project("mix0", [(t, ("wo", n, t)) for t in range(4)], panel(0, HALF), qk)

        def moe(layer):
            src = streams_of(layer)
            tiles = range(4) if layer == 0 else (2, 3)
            stage = f"moe{layer}"
            tok = SLOTS * len(src)
            col_groups = P // tok
            width = D // col_groups
            gate_rows_bcast(stage, src, 4 if layer == 0 else 10)
            norm_T(stage, 2 * layer + 2, xh, tiles)
            pe.wait_ge(Q["router_loaded"], 32)
            rt = view(router[:, layer, :], KT, EXPERTS)
            bank = open_bank(pe, stage, ("lgT",))
            lo = P * tiles[0]
            for k in range(KT):
                last = mm(bank[0:EXPERTS, lo:2 * SEQ], rt[:, k, :], hT[:, k, lo:2 * SEQ], start=k == 0, stop=k == KT - 1)
            last.then_inc(pe_done, 1)
            wait_emptied(pe, stage, ("lgT",))
            bank = open_bank(pe, stage, ("lg",))
            for t in tiles:
                last = nc.tensor.transpose(bank[:, 16 * t:16 * t + 16], logit_T[:, P * t:P * t + P],
                                           ident[0:EXPERTS, 0:EXPERTS])
            last.then_inc(pe_done, 1)
            pe.wait_ge(Q["aff_ready"], layer + 1)
            transposes(stage, ("afT",), [aff2[:, t, :] for t in range(TT)])
            for m, s in enumerate(src):
                bank = open_bank(pe, stage, ("idx", s))
                pe.wait_ge(Q["block_ready"], 2 * layer + m + 1)
                mm(bank, one_col[0:64, :].to_broadcast([64, P]), block_idx[:, s, :], start=True, stop=True).then_inc(pe_done, 1)
            transposes(stage, ("it",), [top_idxf, top_val])
            wait_emptied(pe, stage, ("it",))
            bank = open_bank(pe, stage, ("rep",))
            mm(bank[:, 0:P], rep_mat, sel_T, start=True, stop=True).then_inc(pe_done, 1)

            def gather(stage, i=0):
                for s in src:
                    for m in range(2):
                        bank = open_bank(pe, stage, ("x", s, m), i)
                        for k in range(4):
                            c0 = HALF * m + P * k
                            for t in range(TT):
                                last = mm(bank[:, P * k:P * k + P], xh[:, 2 * s + t, c0:c0 + P], pick_now[:, s, t, :],
                                          start=t == 0, stop=t == 1)
                        last.then_inc(pe_done, 1)

            pe.wait_ge(Q["pick_ready"], 5 * layer + 1)
            gather(stage)
            for s in src:
                for m in range(2):
                    wait_emptied(pe, stage, ("x", s, m))

            stage = f"exp{layer}"
            per = banks.stage_panels[stage][1]
            with pe.Fori(0, GROUPS) as g4:
                state["per"] = per
                for q in range(4):
                    xe = x_four[:, :, q, :]

                    def up(key):
                        bank = open_bank(pe, stage, key, g4)
                        for k in range(KT):
                            if k % 4 == 0:
                                slot = panel(g4, D)
                            for j in range(col_groups):
                                last = mm(bank[tok * j:tok * j + tok, 0:width], xe[:, k, 0:tok],
                                          slot[:, k % 4, width * j:width * j + width], start=k == 0, stop=k == KT - 1)
                            if k % 4 == 3:
                                last.then_inc(pe_done, 1)

                    up(("g", q))
                    up(("u", q))
                    wait_emptied(pe, stage, ("u", q), g4)
                    transposes(stage, ("t", q), [hid_e[:, q % 2, P * m:P * m + P] for m in range(width // P)], g4)
                    if q == 3:
                        pe.wait_ge(Q["pick_ready"], g4 + (5 * layer + 2))
                        gather(stage, g4)
                    wait_emptied(pe, stage, ("t", q), g4)
                    bank = open_bank(pe, stage, ("y", q), g4)
                    for f in range(KT):
                        if f % 4 == 0:
                            slot = panel(g4, D)
                        jf, m = divmod(f, width // P)
                        hcol = P * m + tok * jf
                        for j in range(col_groups):
                            last = mm(bank[tok * j:tok * j + tok, 0:width], hidT[:, q % 2, hcol:hcol + tok],
                                      slot[:, f % 4, width * j:width * j + width], start=f == 0, stop=f == KT - 1)
                        if f % 4 == 3:
                            last.then_inc(pe_done, 1)
                wait_emptied(pe, stage, ("y", 3), g4)
                for s in src:
                    for m in range(2):
                        wait_emptied(pe, stage, ("x", s, m), g4)
                for s in src:
                    for t in range(TT):
                        for n in range(2):
                            bank = open_bank(pe, stage, ("c", s, t, n), g4)
                            mm(bank, back_now[:, s, P * t:P * t + P], y_four[:, s, HALF * n:HALF * n + HALF],
                               start=True, stop=True).then_inc(pe_done, 1)
            state["panel"] += (GROUPS - 1) * per
            state["per"] = 0

        moe(0)

        norm_T("mix1", 3, xh1, range(4))
        hT_lat = view(ht[:, :], KT, 2, SEQ)[:, :, 1, :]
        for n in range(2):
            slot = panel(0, HALF)
            for m in range(2):
                bank = open_bank(pe, "mix1", ("q", n, m))
                for h in range(2):
                    for k in range(KT):
                        last = mm(bank[:, SEQ * h:SEQ * h + SEQ], slot[:, k, P * (2 * m + h):P * (2 * m + h + 1)],
                                  hT_lat[:, k, :], start=k == 0, stop=k == KT - 1)
                last.then_inc(pe_done, 1)
            for m in range(2):
                wait_emptied(pe, "mix1", ("q", n, m))
                bank = open_bank(pe, "mix1", ("qs", n, m))
                h = 4 * n + 2 * m
                mm(bank, swap_mat, qT[:, h:h + 2, :], start=True, stop=True).then_inc(pe_done, 1)
        for n in range(2):
            project_wide("mix1", [("k", 4 * n + m) for m in range(4)], panel(0, HALF), hT)
            for m in range(2):
                h = 4 * n + 2 * m
                wait_emptied(pe, "mix1", ("k", h))
                wait_emptied(pe, "mix1", ("k", h + 1))
                bank = open_bank(pe, "mix1", ("ks", 2 * n + m))
                mm(bank, swap_mat, kT[:, h:h + 2, SEQ:2 * SEQ], start=True, stop=True).then_inc(pe_done, 1)
        project("mix1", [(t, ("v", 0, t)) for t in range(4)], panel(0, HALF), hT)
        pe.wait_ge(Q["kt_ready"], 8)
        for h in range(HEADS + 1):
            if h in (1, 5):
                for t in range(4):
                    wait_emptied(pe, "mix1", ("v", h // 4, t))
            if h < HEADS:
                for s in (CTX, LAT):
                    bank = open_bank(pe, "mix1", ("s", h, s))
                    for j in range(2):
                        a = SEQ * s + P * j
                        last = mm(bank[:, SEQ * j:SEQ * j + SEQ], kT[:, h, a:a + P], qT[:, h, :], start=True, stop=True)
                    last.then_inc(pe_done, 1)
            beside("mix1", BESIDE1.get(h, ()))
            if h == HEADS - 1:
                gate_rows_bcast("mix1", (LAT,), 8)
            if h:
                pe.wait_ge(Q["w_ready"], HEADS + h)
                bank = open_bank(pe, "mix1", ("o", h - 1))
                for i in range(TT):
                    m = 0
                    for s, e in ((CTX, 2), (LAT, 0)):
                        for j in range(2):
                            a = SEQ * j + P * i
                            last = mm(bank[:, P * i:P * i + P], dec[:, (h - 1) % 2, e, a:a + P],
                                      rv[:, 2 * s + j, DV * (h - 1):DV * h], start=m == 0, stop=m == 3)
                            m += 1
                last.then_inc(pe_done, 1)
        for m in range(4):
            if m in (0, 3):
                pe.wait_ge(Q["og_ready"], 3 + m // 3)
            transposes("mix1", ("yT", m), [ry[:, t, P * k:P * k + P] for k in (2 * m, 2 * m + 1) for t in range(TT)])
        for m in range(4):
            wait_emptied(pe, "mix1", ("yT", m))
        for n in range(2):
            slot = panel(0, HALF)
            for t in range(TT):
                bank = open_bank(pe, "mix1", ("wo", n, 2 + t))
                for k in range(KT):
                    last = mm(bank, ryT[:, k, P * t:P * t + P], slot[:, k, :], start=k == 0, stop=k == KT - 1)
                last.then_inc(pe_done, 1)
        moe(1)

    def gate_diag_of(stage):
        return gate_diag if stage.startswith("mix") else view(lflat[:, 0:2048], 4, 4, P)

    def scalar(act):
        step, full_bank, wait_emptied = S["astep"], S["full_bank"], S["wait_emptied"]
        A = nc.scalar.activation

        def tile_ready(n, t):
            if n == 1 and t < 2:
                act.wait_ge(Q["ctx_loaded"], 16)
            elif n == 1:
                act.wait_ge(S["x_ready"], TT * DEPTH + t - 1)
            elif n in (2, 4):
                act.wait_ge(Q["streams_ready"], t + 1 + (2 if n == 4 else 0))
            else:
                for half in range(2):
                    wait_emptied(act, f"exp{n // 4}", ("c", t // 2, t % 2, half), GROUPS - 1)

        def squares(tiles, scratch, n):
            for t in list(tiles)[:-1]:
                tile_ready(n, t)
                ins = A(scratch[:, t, :], tokens[t], ACT.Square, accum_out=ss[:, t:t + 1])
            ins.then_inc(Q["squares_ready"], 1)
            act.wait_ge(Q["ms_ready"], n)
            A(rs, rs, ACT.Sqrt).then_inc(Q["rms_ready"], 1)
            if n < 5:
                act.wait_ge(Q["inv_ready"], n)
                for t in list(tiles)[:len(tiles) // 2]:
                    ins = A(scratch[:, t, :], tokens[t], ACT.Copy, scale=rs[:, t:t + 1])
                ins.then_inc(Q["xh_ready"], 1)

        def take(stage, key, dst, func=ACT.Copy, part=None, scale=1.0, i=0):
            bank, freed = full_bank(act, stage, key, i)
            bank = bank if part is None else bank[:, 0:part]
            if len(dst.shape) == 3:
                bank = view(bank, dst.shape[1], dst.shape[2])
            A(dst, bank, func, scale=scale).then_inc(freed, 1)

        def modulated(stage, n, src):
            for k in range(0, KT, 2):
                bank, freed = full_bank(act, stage, ("hT", k))
                for m, s in enumerate(src):
                    ins = A(hT[:, k, SEQ * s:SEQ * s + SEQ], bank[:, SEQ * m:SEQ * m + SEQ], ACT.Identity,
                            scale=coef[:, n, s, k:k + 1], bias=shift_of(n, s, k))
                ins.then_inc(freed, 1)

        def gates_out(stage, src, dst):
            for s in src:
                for n in range(2):
                    take(stage, ("gbc", s, n), dst[:, s, HALF * n:HALF * n + HALF])

        squares(range(4), xh0, 1)
        modulated("mix0", 0, (CTX, LAT))
        for m in range(8):
            if m >= 4:
                act.wait_ge(Q["conv_ready"], m - 3)
            bank, freed = full_bank(act, "mix0", ("qk", m))
            A(qk_pad[:, m % 4, :, 2:2 + SEQ], view(bank, STREAMS, SEQ), ACT.Copy).then_inc(freed, 1)
            if m % 2 and m >= 3:
                silus(act, m - 3)
        silus(act, 6)

        def value_out(n, t):
            take("mix0", ("v", n, t), va[:, t, 4 * n:4 * n + 4, 0:DV])

        for t in range(4):
            value_out(0, t)
        act.wait_ge(Q["abs_ready"], 1)
        step(A(t_rows[64:128, :], t_rows[64:128, :], ACT.Exp, scale=-1.0))
        A(t_rows[64:128, :], t_rows[64:128, :], ACT.Ln, bias=1.0).then_inc(Q["softplus_ready"], 1)
        for kind, n, t in BEFORE0:
            take("mix0", (kind, n, t), og[:, t, HALF * n:HALF * n + HALF], ACT.Sigmoid)
        bank, freed = full_bank(act, "mix0", ("aT",))
        A(aT, view(bank[:, 0:256], 4, 64), ACT.Copy)
        step(A(em, view(bank[:, 256:512], 4, 64)[:, :, 0:40], ACT.Exp))
        A(st[:, 248:249], em[:, 0, 0:1], ACT.Copy).then_inc(freed, 1)
        wait_emptied(act, "mix0", ("aT",))
        for h in range(HEADS + 1):
            if h < HEADS:
                if h:
                    act.wait_ge(Q["mdiag_ready"], 2 * h)
                    act.wait_ge(Q["exp_w_ready"], h)
                for d in range(2):
                    take("mix0", ("mb", h, d), m_neg[:, d, :])
                w = wbuf[h % 2]
                if h >= 2:
                    act.wait_ge(pe_done, banks.full("mix0", ("h", h - 2, 3)))
                for d in range(2):
                    wait_emptied(act, "mix0", ("mb", h, d))
                    act.wait_ge(Q["mdiag_ready"], 2 * h + d + 1)
                    for j in range(4):
                        bias = aT[:, j, 32 * d + h:32 * d + h + 1]
                        a = COL[d](j, j)
                        A(w[d][:, a:a + P], m_diag[:, d, P * j:P * j + P], ACT.Exp, bias=bias)
                        if d == 0 and j < 3:
                            A(w[d][:, a + P:a + P * (4 - j)], m_neg[:, d, P * (j + 1):HALF], ACT.Exp, bias=bias)
                        elif d == 1 and j == 0:
                            A(w[d][:, P:3 * P], m_neg[:, d, SEQ:HALF], ACT.Exp, bias=bias)
                        elif d == 1 and j == 1:
                            A(w[d][:, a - P:a], m_neg[:, d, 0:P], ACT.Exp, bias=bias)
                            A(w[d][:, a + P:a + 3 * P], m_neg[:, d, SEQ:HALF], ACT.Exp, bias=bias)
                        elif d == 1 and j == 3:
                            A(w[d][:, a - P:a], m_neg[:, d, SEQ:SEQ + P], ACT.Exp, bias=bias)
                A(st[:, 249:250], em[:, 0, 0:1], ACT.Copy).then_inc(Q["exp_w_ready"], 1)
            for kind, n, t in BESIDE0.get(h, ()):
                if kind == "v":
                    value_out(n, t)
                else:
                    take("mix0", (kind, n, t), og[:, t, HALF * n:HALF * n + HALF], ACT.Sigmoid)
            if h == HEADS - 1:
                gates_out("mix0", (CTX, LAT), gb)
            if h == HEADS:
                act.wait_ge(Q["head_ms_ready"], 1)
                A(head_ss[:, :, 0:6], head_ss[:, :, 0:6], ACT.Sqrt).then_inc(Q["head_rms_ready"], 1)
            if h:
                act.wait_ge(Q["yt_ready"], h)
                for i in range(4):
                    ins = A(sq_dump[:, :], yt[:, (h - 1) % 2, i, :], ACT.Square, accum_out=head_ss[:, i, h - 1:h])
                    if i < 3:
                        step(ins)
                ins.then_inc(Q["head_ss_ready"], 1)
                act.wait_ge(Q["head_ss_ready"], h)
        act.wait_ge(Q["head_ms_ready"], 2)
        A(head_ss[:, :, 6:8], head_ss[:, :, 6:8], ACT.Sqrt).then_inc(Q["head_rms_ready"], 1)
        for k in range(0, KT, 2):
            take("mix0", ("yT", k), qk[:, k, :])

        def moe(layer):
            src = streams_of(layer)
            tiles = range(4) if layer == 0 else (2, 3)
            stage = f"moe{layer}"
            gates_out(stage, src, gb_moe)
            squares(tiles, xh, 2 * layer + 2)
            modulated(stage, 2 * layer + 1, src)
            bank, freed = full_bank(act, stage, ("lgT",))
            lo = P * tiles[0]
            A(logit_T[:, lo:2 * SEQ], bank[0:EXPERTS, lo:2 * SEQ], ACT.Copy).then_inc(freed, 1)
            act.wait_ge(Q["shift_ready"], layer + 1)
            A(logit, logit, ACT.Exp).then_inc(Q["aff_exp_ready"], 1)

            def gathered(stage, i=0):
                for m, s in enumerate(src):
                    bank, freed = full_bank(act, stage, ("x", s, 0), i)
                    for k in range(4):
                        ins = A(x_four[:, k, :, SLOTS * m:SLOTS * m + SLOTS], view(bank[:, P * k:P * k + P], 4, SLOTS),
                                ACT.Identity, scale=coef[:, 2 * layer + 1, s, k:k + 1],
                                bias=shift_of(2 * layer + 1, s, k))
                    ins.then_inc(freed, 1)

            gathered(stage)
            stage = f"exp{layer}"
            width = HALF if layer == 0 else SEQ
            with act.Fori(0, GROUPS) as g4:
                for q in range(4):
                    bank, freed = full_bank(act, stage, ("g", q), g4)
                    if q >= 2:
                        wait_emptied(act, stage, ("u", q - 2), g4)
                    else:
                        wait_emptied(act, stage, ("u", q + 2), g4 - 1)
                    A(sil_e[:, q % 2, 0:width], bank[:, 0:width], ACT.Silu).then_inc(freed, 1)
                    bank, freed = full_bank(act, stage, ("t", q), g4)
                    A(hidT[:, q % 2, 0:width], bank[:, 0:width], ACT.Copy).then_inc(freed, 1)
                gathered(stage, g4)

        moe(0)

        squares(range(4), xh1, 3)
        modulated("mix1", 2, (CTX, LAT))
        for n in range(2):
            for m in range(2):
                h = 4 * n + 2 * m
                take("mix1", ("q", n, m), qT[:, h:h + 2, :])
        for h in range(HEADS):
            take("mix1", ("k", h), kT[:, h, :], scale=DV ** -0.5)
        for t in range(4):
            take("mix1", ("v", 0, t), rv[:, t, 0:HALF])
        act.wait_ge(Q["logg_abs_ready"], 1)
        step(A(logg_t, logg_t, ACT.Exp, scale=-1.0))
        A(logg_t, logg_t, ACT.Ln, bias=1.0).then_inc(Q["logg_sp_ready"], 1)
        act.wait_ge(Q["logg_ready"], 1)
        act.wait_ge(Q["ret_loaded"], 32)
        for h in range(HEADS + 1):
            if h < HEADS:
                if h >= 2:
                    act.wait_ge(pe_done, banks.full("mix1", ("o", h - 2)))
                for m in range(4):
                    lg = logg[:, 8 * (m % 2) + h:8 * (m % 2) + h + 1]
                    ins = A(dec[:, h % 2, m, :], gaps[:, m, :], ACT.Exp, scale=lg)
                ins.then_inc(Q["decay_ready"], 1)
            for kind, n, t in BESIDE1.get(h, ()):
                if kind == "v":
                    take("mix1", (kind, n, t), rv[:, t, HALF * n:HALF * n + HALF])
                else:
                    take("mix1", (kind, n, t), rg[:, t - 2, HALF * n:HALF * n + HALF], ACT.Silu)
            if h == HEADS - 1:
                gates_out("mix1", (LAT,), gb)
            if h:
                bank, freed = full_bank(act, "mix1", ("o", h - 1))
                A(ry[:, :, DV * (h - 1):DV * h], view(bank[:, 0:SEQ], TT, DV), ACT.Copy).then_inc(freed, 1)
        for m, (a, b) in enumerate(((0, 6), (6, 8))):
            act.wait_ge(Q["head_ms_ready"], 3 + m)
            A(var_th[:, :, a:b], var_th[:, :, a:b], ACT.Sqrt).then_inc(Q["head_rms_ready"], 1)
        for m in range(0, 4, 2):
            take("mix1", ("yT", m), ryT[:, 2 * m:2 * m + 2, :])
        moe(1)
        squares((2, 3), xh, 5)

    sq_dump = sb("sq_dump", [P, DV])

    def silus(act, m):
        for j in (m, m + 1):
            act.wait_ge(Q["conv_ready"], j + 1)
            nc.scalar.activation(qk[:, j, :], conv_acc[:, j % 2].rearrange("p a b -> p (a b)"), ACT.Silu
                                 ).then_inc(Q["silu_ready"], 1)

    def shift_of(n, s, k):
        return mods[n // 2][:, 24 * (n % 2) + k, 1 - s:2 - s]

    def vector(dve):
        V = nc.vector
        step, full_bank, wait_emptied = S["vstep"], S["full_bank"], S["wait_emptied"]
        TS, STT, TTo = V.tensor_scalar, V.scalar_tensor_tensor, V.tensor_tensor
        count = {"diag": 0, "tiles": 0}

        def spot(m):
            return st[:, 240 + m:241 + m]

        def mark(name, m):
            step(V.memset(spot(m), 0.0))
            V.memset(spot(m), 0.0).then_inc(Q[name], 1)

        def own_squares(tiles, scratch):
            for t in list(tiles)[-1:]:
                ins = V.tensor_tensor_reduce(out=scratch[:, t, :], in0=tokens[t], in1=tokens[t], scale=1.0, scalar=0.0,
                                             op0=ALU.mult, op1=ALU.add, accum_out=ss[:, t:t + 1])
            step(ins)

        def rms(n, tiles, dst, meanwhile=None):
            own_squares(tiles, dst)
            dve.wait_ge(Q["squares_ready"], n)
            TS(rs, ss, 1.0 / D, RMS_EPS, ALU.mult, ALU.add).then_inc(Q["ms_ready"], 1)
            if meanwhile:
                meanwhile()
            dve.wait_ge(Q["rms_ready"], n)
            V.reciprocal(rs, rs).then_inc(Q["inv_ready"], 1)
            dve.wait_ge(Q["inv_ready"], n)
            for t in list(tiles)[len(tiles) // 2:]:
                ins = TS(dst[:, t, :], tokens[t], rs[:, t:t + 1], None, ALU.mult)
            ins.then_inc(Q["xh_ready"], 1)

        def modulated(stage, n, src):
            for k in range(1, KT, 2):
                bank, freed = full_bank(dve, stage, ("hT", k))
                for m, s in enumerate(src):
                    ins = TS(hT[:, k, SEQ * s:SEQ * s + SEQ], bank[:, SEQ * m:SEQ * m + SEQ], coef[:, n, s, k:k + 1],
                             shift_of(n, s, k), ALU.mult, ALU.add)
                ins.then_inc(freed, 1)

        def diagonals(stage, layer, part, src):
            buf = gate_diag_of(stage)
            for m, (s, n) in enumerate((s, n) for s in src for n in range(2)):
                if m >= buf.shape[1]:
                    dve.wait_ge(pe_done, banks.full(stage, ("gbc", src[(m - 2) // 2], m % 2)))
                col = mods[layer][:, 8 * part + 4 * n:8 * part + 4 * n + 4, 1 - s]
                TTo(buf[:, m % buf.shape[1]], ident.unsqueeze(1).to_broadcast([P, 4, P]), spread(col, P), ALU.mult
                    ).then_inc(Q["diag_ready"], 1)

        def residual(stage, keys, gates):
            for s, n in sorted({(s, n) for _, s, _, n in keys}):
                wait_emptied(dve, stage, ("gbc", s, n))
            for m, (key, s, t, n) in enumerate(keys):
                bank, freed = full_bank(dve, stage, key)
                tmp = res_tmp[:, m % 2, :]
                TTo(tmp, bank, gates[:, s, HALF * n:HALF * n + HALF], ALU.mult).then_inc(freed, 1)
                wait_emptied(dve, stage, key)
                xs_ = tokens[2 * s + t][:, HALF * n:HALF * n + HALF]
                if n:
                    TTo(xs_, xs_, tmp, ALU.add).then_inc(Q["streams_ready"], 1)
                else:
                    step(TTo(xs_, xs_, tmp, ALU.add))
            count["tiles"] += len(keys) // 2
            dve.wait_ge(Q["streams_ready"], count["tiles"])

        def with_bias(l):
            step(TTo(mods[l][:, :, :], mods[l][:, :, :], spread(par[:, 48 * l:48 * l + 48], 2), ALU.add))

        def scales(n):
            for s in (CTX, LAT):
                scale = mods[n // 2][:, 24 * (n % 2) + 8:24 * (n % 2) + 16, 1 - s]
                gain = par[:, 96 + 16 * (n % 2) + 8 * (n // 2):104 + 16 * (n % 2) + 8 * (n // 2)]
                step(STT(out=coef[:, n, s, :], in0=scale, scalar=1.0, in1=gain, op0=ALU.add, op1=ALU.mult))

        def first_scales():
            with_bias(0)
            scales(0)

        rms(1, range(4), xh0, first_scales)
        step(V.memset(gate_bias, 0.0))
        V.memset(spot(8), 0.0).then_inc(Q["gbias_clear"], 1)
        modulated("mix0", 0, (CTX, LAT))
        step(V.memset(wg[:, :, :], 0.0))
        step(V.memset(qk_pad[:, :, :, 0:2], 0.0))
        step(V.memset(qk_pad[:, :, :, 2 + SEQ:4 + SEQ], 0.0))
        with_bias(1)
        for n in range(1, 4):
            scales(n)
        step(V.memset(va[:, :, :, DV:DV + 1], 1.0))
        dve.wait_ge(Q["wg_loaded"], 16)
        for m in range(4):
            ins = V.tensor_copy(wg[:, :, 32 * m:32 * m + 8], wg32[:, :, 8 * m:8 * m + 8])
        ins.then_inc(Q["wg_ready"], 1)
        for m in range(0, 8, 2):
            pair = (m, m + 1)
            for j in pair:
                wait_emptied(dve, "mix0", ("qk", j))
            if m:
                dve.wait_ge(Q["silu_ready"], m)
            for tap in range(CONV_TAPS):
                for j in pair:
                    src, w = qk_pad[:, j % 4, :, tap:tap + SEQ], par2[:, 8 * tap + j:8 * tap + j + 1]
                    acc = conv_acc[:, j % 2]
                    if tap == 0:
                        ins = TS(acc, src, w, par2[:, 40 + j:41 + j], ALU.mult, ALU.add)
                    else:
                        ins = STT(out=acc, in0=src, scalar=w, in1=acc, op0=ALU.mult, op1=ALU.add)
                    if tap == CONV_TAPS - 1:
                        ins.then_inc(Q["conv_ready"], 1)
                if tap < CONV_TAPS - 1:
                    step(ins)
        dve.wait_ge(Q["silu_ready"], 8)
        dve.wait_ge(Q["gbias_loaded"], 64)
        dve.wait_ge(Q["conv_ready"], 8)
        bank, freed = full_bank(dve, "mix0", ("gr",))
        TS(gate_rows, bank, gate_bias, None, ALU.add).then_inc(freed, 1)
        wait_emptied(dve, "mix0", ("gr",))
        STT(out=t_rows[64:128, :], in0=gate_rows[64:128, :], scalar=-1.0, in1=gate_rows[64:128, :], op0=ALU.mult,
            op1=ALU.max).then_inc(Q["abs_ready"], 1)
        step(V.memset(one_rows, 1.0))
        dve.wait_ge(Q["softplus_ready"], 1)
        step(STT(out=lf_rows[0:64, :], in0=gate_rows[64:128, :], scalar=0.0, in1=t_rows[64:128, :], op0=ALU.min,
                 op1=ALU.subtract))
        scan = V.tensor_tensor_scan

        def scans(dst, src, op0, op1):
            scan(dst[0:32, :], one_rows[0:32, :], src[0:32, :], 0.0, op0, op1)
            step(scan(dst[32:64, 0:SEQ][:, ::-1], one_rows[32:64, 0:SEQ], src[32:64, 0:SEQ][:, ::-1], 0.0, op0, op1))
            step(scan(dst[32:64, SEQ:][:, ::-1], one_rows[32:64, 0:SEQ], src[32:64, SEQ:][:, ::-1], dst[32:64, 0:1],
                      op0, op1))

        scans(b_rows, lf_rows, ALU.mult, ALU.add)
        step(TTo(gate_rows[0:64, :], gate_rows[0:64, :], b_rows[0:64, :], ALU.subtract))
        scans(lf_rows, gate_rows, ALU.mult, ALU.max)
        step(STT(out=b_rows[0:64, :], in0=b_rows[0:64, :], scalar=-1.0, in1=lf_rows[0:64, :], op0=ALU.mult,
                 op1=ALU.subtract))
        step(TS(lf_rows[0:64, :], lf_rows[0:64, :], -1.0, None, ALU.mult))
        V.memset(spot(9), 0.0).then_inc(Q["rows_ready"], 1)
        wait_emptied(dve, "mix0", ("aT",))
        masks = (later_key, earlier_key)

        def scale_heads(a, b, n):
            dve.wait_ge(Q["head_rms_ready"], n)
            step(V.reciprocal(head_ss[:, :, a:b], head_ss[:, :, a:b]))
            o = og[:, :, DV * a:DV * b].rearrange("p t (h d) -> p t h d", h=b - a)
            step(TTo(o, o, head_ss[:, :, a:b].unsqueeze(3).to_broadcast([P, 4, b - a, DV]), ALU.mult))
            V.memset(spot(4), 0.0).then_inc(Q["og_ready"], 1)

        for h in range(HEADS + 1):
            if h < HEADS:
                if h:
                    dve.wait_ge(Q["exp_w_ready"], h)
                for d in range(2):
                    wait_emptied(dve, "mix0", ("mb", h, d))
                    TTo(view(m_diag[:, d, :], 4, P), view(m_neg[:, d, :], 4, P),
                        masks[d].unsqueeze(1).to_broadcast([P, 4, P]), ALU.add).then_inc(Q["mdiag_ready"], 1)
                dve.wait_ge(Q["exp_w_ready"], h + 1)
                w = wbuf[h % 2]

                def weigh(d, a, bank, col, n):
                    return STT(out=w[d][:, a:a + n], in0=bank[:, col:col + n], scalar=SCALE, in1=w[d][:, a:a + n],
                               op0=ALU.mult, op1=ALU.mult)

                bank, freed = full_bank(dve, "mix0", ("s", h, 0))
                weigh(0, 0, bank, 0, HALF)
                weigh(1, 0, bank, 0, P)
                weigh(1, P, bank, SEQ, SEQ).then_inc(freed, 1)
                bank, freed = full_bank(dve, "mix0", ("s", h, 1))
                weigh(0, 512, bank, P, 3 * P)
                weigh(1, 384, bank, 0, HALF).then_inc(freed, 1)
                bank, freed = full_bank(dve, "mix0", ("s", h, 2))
                weigh(0, 896, bank, 0, SEQ)
                weigh(0, 1152, bank, SEQ + P, P)
                weigh(1, 896, bank, 0, P)
                weigh(1, 1024, bank, SEQ, SEQ).then_inc(freed, 1)
                wait_emptied(dve, "mix0", ("s", h, 2))
                V.memset(spot(6), 0.0).then_inc(Q["w_ready"], 1)
            if h == HEADS:
                scale_heads(0, 6, 1)
            if h:
                y = yt[:, (h - 1) % 2]
                if h >= 3:
                    dve.wait_ge(Q["head_ss_ready"], h - 2)
                both = []
                for i in range(4):
                    bank, freed = full_bank(dve, "mix0", ("h", h - 1, i))
                    both.append((view(bank[:, 0:2 * (DV + 1)], 2, DV + 1), freed))
                    ins = STT(out=r2[:, 2 * i:2 * i + 2], in0=both[i][0][:, :, DV], scalar=-1.0,
                              in1=em[:, i, h - 1:h + 32:32], op0=ALU.mult, op1=ALU.max)
                step(ins)
                for i in range(4):
                    ins = TTo(r2[:, 2 * i:2 * i + 2], r2[:, 2 * i:2 * i + 2], both[i][0][:, :, DV], ALU.max)
                step(ins)
                step(V.reciprocal(r2, r2))
                for i in range(4):
                    ins = TS(y[:, i, :], both[i][0][:, 0, 0:DV], r2[:, 2 * i:2 * i + 1], None, ALU.mult)
                step(ins)
                for i in range(4):
                    STT(out=y[:, i, :], in0=both[i][0][:, 1, 0:DV], scalar=r2[:, 2 * i + 1:2 * i + 2], in1=y[:, i, :],
                        op0=ALU.mult, op1=ALU.add).then_inc(both[i][1], 1)
                for i in range(4):
                    wait_emptied(dve, "mix0", ("h", h - 1, i))
                V.memset(spot(5), 0.0).then_inc(Q["yt_ready"], 1)
                if h in (1, 5):
                    n = h // 4
                    for t in range(4):
                        wait_emptied(dve, "mix0", ("o", n, t))
                    if n == 0:
                        dve.wait_ge(Q["gain_loaded"], 16)
                    for t in range(4):
                        half = og[:, t, HALF * n:HALF * n + HALF]
                        ins = TTo(half, half, lnp[:, 0, HALF * n:HALF * n + HALF], ALU.mult)
                    step(ins)
                o = og[:, :, DV * (h - 1):DV * h]
                step(TTo(o, o, y, ALU.mult))
            if h == 6:
                dve.wait_ge(pe_done, banks.full("mix0", ("o", 1, 3)))
                diagonals("mix0", 0, 2, (CTX, LAT))
            if h == HEADS - 1:
                dve.wait_ge(Q["head_ss_ready"], 6)
                TS(head_ss[:, :, 0:6], head_ss[:, :, 0:6], 1.0 / DV, RMS_EPS, ALU.mult, ALU.add
                   ).then_inc(Q["head_ms_ready"], 1)
        dve.wait_ge(Q["head_ss_ready"], HEADS)
        TS(head_ss[:, :, 6:8], head_ss[:, :, 6:8], 1.0 / DV, RMS_EPS, ALU.mult, ALU.add).then_inc(Q["head_ms_ready"], 1)
        scale_heads(6, 8, 2)
        for k in range(1, KT, 2):
            bank, freed = full_bank(dve, "mix0", ("yT", k))
            V.tensor_copy(qk[:, k, :], bank).then_inc(freed, 1)
        diagonals("moe0", 0, 5, (CTX, LAT))
        residual("mix0", [(("wo", n, t), t // 2, t % 2, n) for n in range(2) for t in range(4)], gb)

        def moe(layer):
            src = streams_of(layer)
            tiles = range(4) if layer == 0 else (2, 3)
            lo = 16 * tiles[0]
            stage = f"moe{layer}"
            rms(2 * layer + 2, tiles, xh)
            modulated(stage, 2 * layer + 1, src)
            step(V.memset(aff2, 0.0))
            bank, freed = full_bank(dve, stage, ("lg",))
            lv = view(logit, 4, EXPERTS)[:, tiles[0]:4, :]
            V.tensor_copy(logit[:, lo:64], bank[:, lo:64]).then_inc(freed, 1)
            wait_emptied(dve, stage, ("lg",))
            if lo:
                step(V.memset(logit[:, 0:lo], 0.0))
            mx = lmax[:, tiles[0]:4]
            step(V.reduce_max(mx, lv, X_AXIS))
            TTo(lv, lv, spread(mx, EXPERTS), ALU.subtract).then_inc(Q["shift_ready"], 1)
            dve.wait_ge(Q["aff_exp_ready"], layer + 1)
            step(V.reduce_sum(mx, lv, X_AXIS))
            step(V.reciprocal(mx, mx))
            for s in src:
                ins = TTo(aff2[:, :, 32 * s:32 * s + 16], view(logit, 4, EXPERTS)[:, 2 * s:2 * s + 2, :],
                          spread(lmax[:, 2 * s:2 * s + 2], EXPERTS), ALU.mult)
            ins.then_inc(Q["aff_ready"], 1)
            bank, freed = full_bank(dve, stage, ("afT",))
            V.tensor_copy(aff_T, bank[0:64, 0:SEQ]).then_inc(freed, 1)
            wait_emptied(dve, stage, ("afT",))
            row = aff_T
            for r in range(0, SLOTS, 8):
                step(V.max(top_val[:, r:r + 8], row))
                step(V.max_index(top_idx[:, r:r + 8], top_val[:, r:r + 8], row))
                if r + 8 < SLOTS:
                    step(V.match_replace(aff_work, top_val[:, r:r + 8], row, -1.0))
                    row = aff_work
            step(V.tensor_copy(top_idxf, top_idx))
            for s in src:
                TTo(view(block_idx[:, s, :], EXPERTS, SLOTS), spread(ident[0:64, 32 * s:32 * s + 16], SLOTS),
                    top_idxf.unsqueeze(1).to_broadcast([64, EXPERTS, SLOTS]), ALU.mult).then_inc(Q["block_ready"], 1)
            if layer:
                V.memset(spot(3), 0.0).then_inc(Q["block_ready"], 1)
            for s in src:
                bank, freed = full_bank(dve, stage, ("idx", s))
                for t in range(TT):
                    ins = TS(pick[:, s, t].rearrange("p a b -> p (a b)"), bank, tok_col[:, t:t + 1], None, ALU.is_equal)
                ins.then_inc(freed, 1)
                wait_emptied(dve, stage, ("idx", s))

            def pick_group(g):
                for s in src:
                    ins = TS(pick_now[:, s], pick[:, s, :, bass.ds(g, 1), :].rearrange("p t a n -> p t (a n)")
                             if not isinstance(g, int) else pick[:, s, :, g, :], 1.0, None, ALU.mult)
                ins.then_inc(Q["pick_ready"], 1)

            def gathered(stage, i=0):
                for m, s in enumerate(src):
                    bank, freed = full_bank(dve, stage, ("x", s, 1), i)
                    for k in range(4):
                        ins = TS(x_four[:, 4 + k, :, SLOTS * m:SLOTS * m + SLOTS], view(bank[:, P * k:P * k + P], 4, SLOTS),
                                 coef[:, 2 * layer + 1, s, 4 + k:5 + k], shift_of(2 * layer + 1, s, 4 + k), ALU.mult,
                                 ALU.add)
                    ins.then_inc(freed, 1)

            pick_group(0)
            bank, freed = full_bank(dve, stage, ("it",))
            V.tensor_copy(view(sel_T, 2, 64), view(bank[0:32, 0:256], 2, P)[:, :, 0:64]).then_inc(freed, 1)
            bank, freed = full_bank(dve, stage, ("rep",))
            for w in range(2):
                rows = view(bank[:, 64 * w:64 * w + 64], STREAMS, 8, 4)[:, :, 0:4, :]
                ins = TTo(sel_m, rows, quad.unsqueeze(1).unsqueeze(1).to_broadcast([P, 2, 4, 4]), ALU.mult)
                step(ins)
                ins = V.reduce_sum(sel[:, w], sel_m, X_AXIS)
                if w:
                    ins.then_inc(freed, 1)
                    wait_emptied(dve, stage, ("rep",))
                else:
                    step(ins)
            for s in src:
                for g in range(GROUPS):
                    ins = TS(spread_back[:, s, g, :], iota, sel[:, 0, s, g:g + 1], sel[:, 1, s, g:g + 1], ALU.is_equal,
                             ALU.mult)
            step(ins)
            gathered(stage)

            tok = SLOTS * len(src)
            col_groups, width = P // tok, D * tok // P
            stage = f"exp{layer}"

            for s in src:
                for n in range(2):
                    wait_emptied(dve, f"moe{layer}", ("gbc", s, n))
            with dve.Fori(0, GROUPS) as g4:
                for s in src:
                    TS(back_now[:, s, :], spread_back[:, s, bass.ds(g4, 1), :].rearrange("p a n -> p (a n)"), 1.0, None,
                       ALU.mult)
                for q in range(4):
                    bank, freed = full_bank(dve, stage, ("u", q), g4)
                    wait_emptied(dve, stage, ("g", q), g4)
                    TTo(hid_e[:, q % 2, 0:width], sil_e[:, q % 2, 0:width], bank[:, 0:width], ALU.mult).then_inc(freed, 1)
                    if q == 3:
                        pick_group((g4 + 1) % GROUPS)
                        gathered(stage, g4)
                    bank, freed = full_bank(dve, stage, ("y", q), g4)
                    for j in range(col_groups):
                        for m, s in enumerate(src):
                            r = tok * j + SLOTS * m
                            cols = slice(width * j, width * j + width)
                            ins = TTo(y_four[32 * q:32 * q + 32, s, cols], bank[r:r + 32, 0:width],
                                      gb_moe[r:r + 32, s, cols], ALU.mult)
                    ins.then_inc(freed, 1)
                for s in src:
                    for t in range(TT):
                        for n in range(2):
                            bank, freed = full_bank(dve, stage, ("c", s, t, n), g4)
                            xs_ = tokens[2 * s + t][:, HALF * n:HALF * n + HALF]
                            TTo(xs_, xs_, bank, ALU.add).then_inc(freed, 1)
                for s in src:
                    for t in range(TT):
                        for n in range(2):
                            wait_emptied(dve, stage, ("c", s, t, n), g4)
            V.memset(spot(1), 0.0).then_inc(Q["gain_free"], 1)

        moe(0)

        rms(3, range(4), xh1)
        modulated("mix1", 2, (CTX, LAT))
        dve.wait_ge(Q["decay_loaded"], 16)
        STT(out=logg_t, in0=logg, scalar=-1.0, in1=logg, op0=ALU.mult, op1=ALU.max).then_inc(Q["logg_abs_ready"], 1)
        dve.wait_ge(Q["ret_loaded"], 32)
        cos, sin = (rope_t[:, m, :].unsqueeze(1).to_broadcast([P, 2, SEQ]) for m in range(2))
        ra, rb = view(rot_a, 2, SEQ), view(rot_b, 2, SEQ)

        def rotate(heads, key, raw_keys):
            for k_ in raw_keys:
                wait_emptied(dve, "mix1", k_)
            step(TTo(ra, heads, cos, ALU.mult))
            bank, freed = full_bank(dve, "mix1", key)
            TTo(rb, view(bank, 2, SEQ), sin, ALU.mult).then_inc(freed, 1)
            wait_emptied(dve, "mix1", key)
            TTo(heads, ra, rb, ALU.add).then_inc(Q["kt_ready"], 1)
            dve.wait_ge(Q["kt_ready"], count["diag"] + 1)
            count["diag"] += 1

        for n in range(2):
            for m in range(2):
                h = 4 * n + 2 * m
                rotate(qT[:, h:h + 2, :], ("qs", n, m), [("q", n, m)])
        for n in range(2):
            for m in range(2):
                h = 4 * n + 2 * m
                rotate(kT[:, h:h + 2, SEQ:2 * SEQ], ("ks", 2 * n + m), [("k", h), ("k", h + 1)])
        dve.wait_ge(Q["logg_sp_ready"], 1)
        STT(out=logg, in0=logg, scalar=0.0, in1=logg_t, op0=ALU.min, op1=ALU.subtract).then_inc(Q["logg_ready"], 1)
        yv = ry.rearrange("p t (h d) -> p t h d", h=HEADS)

        def group_stats(a):
            wait_emptied(dve, "mix1", ("o", a + 1))
            y, mu, var = yv[:, :, a:a + 2, :], mean_th[:, :, a:a + 2], var_th[:, :, a:a + 2]
            step(V.reduce_sum(mu, y, X_AXIS))
            step(TS(mu, mu, 1.0 / DV, None, ALU.mult))
            step(TTo(y, y, mu.unsqueeze(3).to_broadcast([P, TT, 2, DV]), ALU.subtract))
            step(TTo(rsq, y, y, ALU.mult))
            step(V.reduce_sum(var, rsq, X_AXIS))

        def group_scale(a, b, n):
            dve.wait_ge(Q["head_rms_ready"], n)
            y, var = yv[:, :, a:b, :], var_th[:, :, a:b]
            step(V.reciprocal(var, var))
            step(TTo(y, y, var.unsqueeze(3).to_broadcast([P, TT, b - a, DV]), ALU.mult))
            TTo(ry[:, :, DV * a:DV * b], ry[:, :, DV * a:DV * b], rg[:, :, DV * a:DV * b], ALU.mult
                ).then_inc(Q["og_ready"], 1)

        for h in range(HEADS):
            e = dec[:, h % 2]
            dve.wait_ge(Q["decay_ready"], h + 1)
            step(TTo(e[:, 0, :], e[:, 0, :], e[:, 1, :], ALU.mult))
            TTo(e[:, 0, :], e[:, 0, :], gaps[:, 4, :], ALU.add)
            step(TTo(e[:, 2, :], e[:, 2, :], e[:, 3, :], ALU.add))
            for s, m in ((CTX, 2), (LAT, 0)):
                bank, freed = full_bank(dve, "mix1", ("s", h, s))
                TTo(e[:, m, :], e[:, m, :], bank, ALU.mult).then_inc(freed, 1)
            wait_emptied(dve, "mix1", ("s", h, LAT))
            V.memset(spot(6), 0.0).then_inc(Q["w_ready"], 1)
            if h in (3, 5):
                group_stats(h - 3)
            elif h == 6:
                dve.wait_ge(Q["gain_loaded"], 32)
                for n in range(2):
                    for t in range(TT):
                        wait_emptied(dve, "mix1", ("g", n, 2 + t))
                for t in range(TT):
                    ins = TTo(rg[:, t, :], rg[:, t, :], lnp[:, 0, :], ALU.mult)
                step(ins)
                diagonals("mix1", 1, 2, (LAT,))
        group_stats(4)
        TS(var_th[:, :, 0:6], var_th[:, :, 0:6], 1.0 / DV, RMS_EPS, ALU.mult, ALU.add).then_inc(Q["head_ms_ready"], 1)
        group_scale(0, 6, 3)
        group_stats(6)
        TS(var_th[:, :, 6:8], var_th[:, :, 6:8], 1.0 / DV, RMS_EPS, ALU.mult, ALU.add).then_inc(Q["head_ms_ready"], 1)
        group_scale(6, 8, 4)
        for m in range(1, 4, 2):
            bank, freed = full_bank(dve, "mix1", ("yT", m))
            V.tensor_copy(ryT[:, 2 * m:2 * m + 2, :], view(bank, 2, SEQ)).then_inc(freed, 1)
        diagonals("moe1", 1, 5, (LAT,))
        residual("mix1", [(("wo", n, 2 + t), LAT, t, n) for n in range(2) for t in range(TT)], gb)
        moe(1)

        own_squares((2, 3), xh)
        dve.wait_ge(Q["squares_ready"], 5)
        TS(rs, ss, 1.0 / D, RMS_EPS, ALU.mult, ALU.add).then_inc(Q["ms_ready"], 1)
        dve.wait_ge(Q["rms_ready"], 5)
        step(V.reciprocal(rs, rs))
        dve.wait_ge(Q["gain_loaded"], 48)
        for t in range(TT):
            STT(out=x[:, t, :], in0=x[:, t, :], scalar=rs[:, 2 + t:3 + t], in1=lnp[:, 0, :], op0=ALU.mult,
                op1=ALU.mult).then_inc(Q["final_ready"], 1)

    return {"sync": sync, "gpsimd": gpsimd, "tensor": tensor, "scalar": scalar, "vector": vector}


def program(nc, I, K, out):
    banks = BankPlan()
    R, EV = BankPlan.REL, BankPlan.EV

    def attend(kind):
        return [(f"pt{kind}", 0), (f"pt{kind}", 1), (f"pt{kind}", 2), (f"pt{kind}", 3), (f"pv{kind}", 0),
                (f"pt{kind}", 4), (f"pt{kind}", 5), (f"pv{kind}", 1), (f"pt{kind}", 6), (f"pt{kind}", 7),
                (f"pv{kind}", 2), (f"pv{kind}", 3)]

    def gates(kind):
        return [(f"g{kind}", 0), (f"g{kind}", 1), R, (f"g{kind}", 2), (f"g{kind}", 3), R]

    def branch(kind):
        return [(f"m{kind}", m) for m in range(4)] + [R]

    layer = [("xT", t, m) for t in range(TT) for m in range(2)]
    for b in range(3):
        layer += [("b", b, 0), ("b", b, 1), R]
    layer += [("aq", 0), ("aq", 1), R, ("ak",), ("av",), R] + [("sa", h) for h in range(HEADS)]
    layer += [("cq", 0), ("cq", 1), R, ("ck", 0), ("ck", 1), R] + [("sc", h) for h in range(HEADS)]
    layer += [("cv", 0), ("cv", 1), R] + gates("b") + attend("a") + branch("b") + gates("a") + branch("a")
    layer += gates("c") + attend("c") + branch("c")
    layer += [("wo", 0, 0), ("wo", 0, 1), R, ("wo", 1, 0), ("wo", 1, 1), R, ("ada", 0), R, ("ada", 1), R]
    layer += [("x1T", t, m) for t in range(TT) for m in range(2)]
    for p in range(FFN_TILES // 2):
        layer += [("ff", 2 * p), ("ff", 2 * p + 1), R]
        layer += [("adaT", p)] * (p < 10) + [("ada", p + 2), R] * (p < 8)
    layer += [EV] * 5 + [("dn", t, n) for t in range(TT) for n in range(2)]
    layer += [R, ("ada", 10), R, ("ada", 11), R, ("adaT", 10), ("adaT", 11)]
    banks.plan("pre", [("par", 0)])
    banks.plan("layer", layer, DEPTH)
    LAYER_PANELS = banks.stage_panels["layer"][1]
    assert LAYER_PANELS % RING == 0
    if not BLOCK1_ONLY:
        plan_second(banks)

    w_in, w_out = I["w_in"], I["w_out"]

    ctx = ExitStack()
    with ctx:
        def sb(name, shape, dt=F32):
            return ctx.enter_context(nc.sbuf_tensor(name, shape, dt))

        def sem(name):
            return ctx.enter_context(nc.semaphore(name))

        ring = sb("ring", [P, RING, PANEL])
        arena = sb("arena", [P, 16384])
        ht = sb("ht", [P, 4096])
        x = sb("x", [P, TT, D])
        c = sb("c", [P, TT, D])
        lnp = sb("lnp", [P, 2, D])
        const = sb("const", [P, 904])
        ident, swap_mat = const[:, 0:128], const[:, 128:256]
        iota, tok_col, quad = const[:, 256:512], const[:, 512:514], const[:, 514:518]
        later_key, earlier_key = const[:, 518:646], const[:, 646:774]
        mods_now = sb("mods_now", [P, 48, 2])
        mods_0 = sb("mods_0", [P, 48, 2])
        par = sb("par", [P, 128])
        par2 = sb("par2", [P, 88])
        st = sb("st", [P, 256])
        psum = ctx.enter_context(nc.psum_tensor("psum", [P, BANKS, HALF], F32))

        bz = arena[:, 0:3072]
        bpart = view(bz, 3, 4, SEQ)
        zc, za = view(bz, HEADS, 384), view(arena[:, 3072:6144], HEADS, 384)
        aq, ak = view(arena[:, 6144:7168], 4, SEQ), arena[:, 7168:7424]
        cq, ck = view(arena[:, 7424:8448], 4, SEQ), view(arena[:, 8448:9472], 4, SEQ)
        gate_bc = view(arena[:, 6144:8192], 8, SEQ)
        gate_a = view(ht[:, 2048:4096], 8, SEQ)
        av = view(arena[:, 9472:9728], TT, P)
        cv = view(arena[:, 9728:10752], TT, HALF)
        ya, yb, yc = (view(arena[:, 10752 + 1024 * n:11776 + 1024 * n], 4, SEQ) for n in range(3))
        pt = view(arena[:, 13824:15360], 4, 384)
        dist_a, dist_c = arena[:, 15360:15744], arena[:, 15744:16128]
        cT = view(arena[:, 16128:16384], KT, 32)
        hid = view(arena[:, 0:5632], FFN_TILES, SEQ)
        sil = view(arena[:, 5632:6656], 4, SEQ)
        ada_rows = view(arena[:, 6656:6912], 2, P)
        xT = view(ht[:, 0:2048], KT, SEQ)
        merged = c[:, :, :].rearrange("p t (k s) -> p (t k) s", s=SEQ)
        par_rows, par2_rows = arena[:, 0:128], arena[:, 128:256]
        rmax, nmax, sums, recip, sink_e = (st[:, 16 * n:16 * n + 16] for n in range(5))
        nsink = st[:, 80:96]
        sinks = st[:, 96:104]
        bst = view(st[:, 104:128], TT, 2, 6)
        mv = view(st[:, 128:132], TT, 2)
        rstd = st[:, 132:134]
        conv_w = view(st[:, 134:146], 3, 4)

        panel_in = [sem(f"panel_in_{s}") for s in range(RING)]
        pe_done = sem("pe_done")
        bank_free = [sem(f"bank_free_{b}") for b in range(BANKS)]
        dve_step, act_step = sem("dve_step"), sem("act_step")
        x_loaded, const_loaded, par_loaded = sem("x_loaded"), sem("const_loaded"), sem("par_loaded")
        sinks_loaded, ln1_loaded, ln2_loaded = sem("sinks_loaded"), sem("ln1_loaded"), sem("ln2_loaded")
        x_ready, x1_ready, cT_ready = sem("x_ready"), sem("x1_ready"), sem("cT_ready")
        sinks_used, c_cols_ready = sem("sinks_used"), sem("c_cols_ready")
        yb_ready, merged_ready = sem("yb_ready"), sem("merged_ready")
        nmax_ready = {k: sem(f"nmax_{k}_ready") for k in "ac"}
        exp_ready = {k: sem(f"exp_{k}_ready") for k in "ac"}
        probs_ready = {k: sem(f"probs_{k}_ready") for k in "ac"}
        var_ready, std_ready = sem("var_ready"), sem("std_ready")
        out_stored, sil_ready = sem("out_stored"), sem("sil_ready")
        S = dict(locals())
        second = None if BLOCK1_ONLY else second_block(nc, ctx, banks, I, K, out, S)

        block = ctx.enter_context(nc.Block())

        def open_bank(pe, stage, key, i=0):
            b = banks.bank(stage, key)
            pe.wait_ge(bank_free[b], banks.free(stage, key, i))
            return psum[:, b, :]

        def full_bank(eng, stage, key, i=0):
            eng.wait_ge(pe_done, banks.full(stage, key, i))
            b = banks.bank(stage, key)
            return psum[:, b, :], bank_free[b]

        def wait_emptied(eng, stage, key, i=0):
            eng.wait_ge(bank_free[banks.bank(stage, key)], banks.emptied(stage, key, i))

        S.update(open_bank=open_bank, full_bank=full_bank, wait_emptied=wait_emptied)

        def halves(src):
            v = src.rearrange("(h k p) n -> h p k n", h=2, p=P)
            return [(slice(4 * h, 4 * h + 4), v[h]) for h in range(2)]

        def layer_panels(l):
            def cols(name, off=0, n=HALF):
                return n, halves(w_in[l][:, COLS[name] + off:COLS[name] + off + n])

            def rows(src, k0, k1):
                v = src[k0 * P:k1 * P, :].rearrange("(h k p) n -> h p k n", h=2, p=P)
                return D, [(slice(h * (k1 - k0) // 2, (h + 1) * (k1 - k0) // 2), v[h]) for h in range(2)]

            def ada(p):
                return HALF, halves(I["ada_w_2"][l][:, p * HALF:(p + 1) * HALF])

            for name in ("b_h", "b_b", "b_c", "a_q"):
                yield cols(name)
            yield cols("a_k", n=2 * P)
            for name in ("c_q", "c_k", "c_v"):
                yield cols(name)
            yield cols("g_b")
            yield cols("g_b", HALF)
            yield rows(I["w_branch_b"][l], 0, 4)
            yield cols("g_a")
            yield cols("g_a", HALF)
            va = I["w_branch_a"][l].rearrange("(g r d) n -> g d r n", g=2, r=4)
            yield D, [((slice(64 * g, 64 * g + 64), slice(0, 4)), va[g]) for g in range(2)]
            yield cols("g_c")
            yield cols("g_c", HALF)
            yield rows(I["w_branch_c"][l], 0, 4)
            for n in range(2):
                yield HALF, halves(w_out[l][:, n * HALF:(n + 1) * HALF])
            yield ada(0)
            yield ada(1)
            for p in range(FFN_TILES // 2):
                g = [I[w][l][:, p * SEQ:(p + 1) * SEQ].rearrange("(k p) n -> p k n", p=P)
                     for w in ("w_ffn_gate", "w_ffn_up")]
                yield HALF, [((slice(0, P), slice(0, KT), slice(u * SEQ, u * SEQ + SEQ)), g[u]) for u in range(2)]
                if p < 8:
                    yield ada(p + 2)
            for d in range(6):
                yield rows(I["w_ffn_down"][l], 4 * d, min(4 * d + 4, FFN_TILES))
            yield ada(10)
            yield ada(11)

        @block.sync
        def _(sp):
            def load_panel(n, width, parts):
                if n >= RING:
                    first, _, _ = banks.release[n - RING]
                    sp.wait_ge(pe_done, first)
                slot = view(ring[:, n % RING, :], PANEL // width, width)
                for where, src in parts:
                    where = where if isinstance(where, tuple) else (slice(0, P), where)
                    sp.dma_start(slot[where], src).then_inc(panel_in[n % RING], 16)

            sp.dma_start(x[:, :, :], I["x"][0].rearrange("(t p) d -> p t d", p=P)).then_inc(x_loaded, 16)
            n = banks.stage_panels["layer"][0]
            for l in range(DEPTH):
                for width, parts in layer_panels(l):
                    if n == 0:
                        sp.wait_ge(const_loaded, 32)
                        sp.wait_ge(par_loaded, 8 * 16)
                    load_panel(n, width, parts)
                    n += 1
            if second:
                second["sync"](sp, load_panel)
            else:
                sp.wait_ge(x_ready, 6)
                sp.dma_start(out[0].rearrange("(t p) d -> p t d", p=P), x[:, :, :]).then_inc(out_stored, 16)
            sp.wait_ge(out_stored, OUT_STORES * 16)

        @block.gpsimd
        def _(pool):
            for l in range(DEPTH):
                if l:
                    pool.wait_ge(sinks_used, l)
                pool.dma_start(sinks, I["attn_sinks"][l:l + 1, :].to_broadcast([P, HEADS])).then_inc(sinks_loaded, 16)
                if l:
                    pool.wait_ge(x_ready, 2 * l + 2)
                for m, w in enumerate(("ln1_g", "ln1_b")):
                    pool.dma_start(lnp[:, m, :], I[w][l:l + 1, :].to_broadcast([P, D])).then_inc(ln1_loaded, 16)
                pool.wait_ge(x1_ready, 2 * l + 2)
                for m, w in enumerate(("ln2_g", "ln2_b")):
                    pool.dma_start(lnp[:, m, :], I[w][l:l + 1, :].to_broadcast([P, D])).then_inc(ln2_loaded, 16)
            if second:
                second["gpsimd"](pool)

        @block.tensor
        def _(pe):
            mm = nc.tensor.matmul
            state = {"panel": banks.stage_panels["layer"][0]}

            def panel(i, width):
                n = state["panel"]
                state["panel"] += 1
                per = state.get("per", 0)
                pe.wait_ge(panel_in[n % RING], i * (32 * per // RING) + 32 * (n // RING + 1))
                return view(ring[:, n % RING, :], PANEL // width, width)

            def transposes(stage, key, tiles, i=0):
                bank = open_bank(pe, stage, key, i)
                for m, src in enumerate(tiles):
                    last = nc.tensor.transpose(bank[0:src.shape[1], 128 * m:128 * m + src.shape[0]], src,
                                               ident[0:src.shape[0], 0:src.shape[0]])
                last.then_inc(pe_done, 1)

            S.update(panel=panel, state=state, transposes=transposes)
            pe.wait_ge(const_loaded, 32)
            pe.wait_ge(par_loaded, 8 * 16)
            bank = open_bank(pe, "pre", ("par", 0))
            nc.tensor.transpose(bank[:, 0:128], par_rows[:, :], ident)
            nc.tensor.transpose(bank[:, 128:216], par2_rows[0:88, :], ident[0:88, 0:88]).then_inc(pe_done, 1)

            with pe.Fori(0, DEPTH) as l:
                state["per"] = LAYER_PANELS

                def project_T(key, slot, rhs, tiles=2, k_tiles=KT):
                    for m in range(tiles):
                        bank = open_bank(pe, "layer", key + (m,), l)
                        for h in range(2):
                            for k in range(k_tiles):
                                last = mm(bank[:, SEQ * h:SEQ * h + SEQ],
                                          slot[:, k, P * (2 * m + h):P * (2 * m + h + 1)], rhs[:, k, :],
                                          start=k == 0, stop=k == k_tiles - 1)
                        last.then_inc(pe_done, 1)

                def transpose_x(name, ready):
                    for t in range(TT):
                        pe.wait_ge(ready, 2 * l + t + 1)
                        for m in range(2):
                            transposes("layer", (name, t, m), [x[:, t, P * k:P * k + P] for k in range(4 * m, 4 * m + 4)], l)
                    for t in range(TT):
                        for m in range(2):
                            wait_emptied(pe, "layer", (name, t, m), l)

                transpose_x("xT", x_ready)
                for b in range(3):
                    project_T(("b", b), panel(l, HALF), xT)
                slot = panel(l, HALF)
                for m in range(2):
                    bank = open_bank(pe, "layer", ("aq", m), l)
                    for h in range(2):
                        for k in range(KT):
                            for g in range(2):
                                w = 64 * (4 * g + 2 * m + h)
                                last = mm(bank[64 * g:64 * g + 64, SEQ * h:SEQ * h + SEQ], slot[:, k, w:w + 64],
                                          xT[:, k, :], start=k == 0, stop=k == KT - 1)
                    last.then_inc(pe_done, 1)
                slot = panel(l, SEQ)
                bank = open_bank(pe, "layer", ("ak",), l)
                for k in range(KT):
                    last = mm(bank[:, 0:SEQ], slot[:, k, 0:P], xT[:, k, :], start=k == 0, stop=k == KT - 1)
                last.then_inc(pe_done, 1)
                bank = open_bank(pe, "layer", ("av",), l)
                for t in range(TT):
                    for k in range(KT):
                        last = mm(bank[:, P * t:P * t + P], xT[:, k, P * t:P * t + P], slot[:, k, P:2 * P],
                                  start=k == 0, stop=k == KT - 1)
                last.then_inc(pe_done, 1)

                def scores(kind, q_of, k_of):
                    for h in range(HEADS):
                        bank = open_bank(pe, "layer", (f"s{kind}", h), l)
                        q, k = q_of(h), k_of(h)
                        mm(bank[:, 0:P], q[:, 0:P], k[:, 0:P], start=True, stop=True)
                        mm(bank[:, P:3 * P], q[:, P:2 * P], k[:, 0:SEQ], start=True, stop=True).then_inc(pe_done, 1)

                for key in (("aq", 0), ("aq", 1), ("ak",)):
                    wait_emptied(pe, "layer", key, l)
                scores("a", lambda h: aq[64 * (h // 4):64 * (h // 4) + 64, h % 4, :],
                       lambda h: ak[64 * (h // 4):64 * (h // 4) + 64, :])
                project_T(("cq",), panel(l, HALF), xT)
                project_T(("ck",), panel(l, HALF), xT)
                for key in (("cq", 0), ("cq", 1), ("ck", 0), ("ck", 1)):
                    wait_emptied(pe, "layer", key, l)
                scores("c", lambda h: cq[64 * (h % 2):64 * (h % 2) + 64, h // 2, :],
                       lambda h: ck[64 * (h % 2):64 * (h % 2) + 64, h // 2, :])

                def project(keys, slot, lhs, k_tiles=KT):
                    for t, key in enumerate(keys):
                        bank = open_bank(pe, "layer", key, l)
                        for k in range(k_tiles):
                            last = mm(bank, lhs[:, k, P * t:P * t + P], slot[:, k, :], start=k == 0, stop=k == k_tiles - 1)
                        last.then_inc(pe_done, 1)

                project([("cv", 0), ("cv", 1)], panel(l, HALF), xT)

                def gate_panels(kind):
                    for n in range(2):
                        slot = panel(l, HALF)
                        for m in range(2):
                            bank = open_bank(pe, "layer", (f"g{kind}", 2 * n + m), l)
                            for h in range(2):
                                for k in range(KT):
                                    last = mm(bank[:, SEQ * h:SEQ * h + SEQ], slot[:, k, P * (2 * m + h):P * (2 * m + h + 1)],
                                              xT[:, k, :], start=k == 0, stop=k == KT - 1)
                            last.then_inc(pe_done, 1)

                def attend_values(kind, heads, probs, values, width):
                    pe.wait_ge(probs_ready[kind], l + 1)
                    for key in attend(kind):
                        if key[0] == f"pt{kind}":
                            n = key[1]
                            h = heads(n // 2, n % 2)
                            transposes("layer", key, [probs[:, h, P * m:P * m + P] for m in range(3)], l)
                        else:
                            r = key[1]
                            for g in range(2):
                                wait_emptied(pe, "layer", (f"pt{kind}", 2 * r + g), l)
                            bank = open_bank(pe, "layer", key, l)
                            for g in range(2):
                                v = width(heads(r, g))
                                p = pt[:, (2 * r + g) % 4, :]
                                o = bank[64 * g:64 * g + 64, :]
                                mm(o[:, 0:SEQ], values[:, 0, v:v + 64], p[:, 0:SEQ], start=True, stop=False)
                                last = mm(o[:, P:SEQ], values[:, 1, v:v + 64], p[:, SEQ:3 * P], start=False, stop=True)
                            last.then_inc(pe_done, 1)

                gate_panels("b")
                wait_emptied(pe, "layer", ("av",), l)
                attend_values("a", lambda r, g: r + 4 * g, za, av, lambda h: 64 * (h // 4))
                pe.wait_ge(yb_ready, l + 1)
                project_T(("mb",), panel(l, D), yb, tiles=4, k_tiles=4)
                gate_panels("a")
                wait_emptied(pe, "layer", ("pva", 3), l)
                project_T(("ma",), panel(l, D), ya, tiles=4, k_tiles=4)
                gate_panels("c")
                wait_emptied(pe, "layer", ("cv", 0), l)
                wait_emptied(pe, "layer", ("cv", 1), l)
                attend_values("c", lambda r, g: 2 * r + g, zc, cv, lambda h: 64 * h)
                wait_emptied(pe, "layer", ("pvc", 3), l)
                project_T(("mc",), panel(l, D), yc, tiles=4, k_tiles=4)
                pe.wait_ge(merged_ready, l + 1)
                for n in range(2):
                    project([("wo", n, 0), ("wo", n, 1)], panel(l, HALF), merged)
                pe.wait_ge(cT_ready, 1)

                def ada(p):
                    slot = panel(l, HALF)
                    bank = open_bank(pe, "layer", ("ada", p), l)
                    for k in range(KT):
                        for j in range(4):
                            last = mm(bank[32 * j:32 * j + 32, 0:P], cT[:, k, :], slot[:, k, P * j:P * j + P],
                                      start=k == 0, stop=k == KT - 1)
                    last.then_inc(pe_done, 1)

                def ada_T(p):
                    wait_emptied(pe, "layer", ("ada", p), l)
                    transposes("layer", ("adaT", p), [ada_rows[:, p % 2, :]], l)

                ada(0)
                ada(1)
                transpose_x("x1T", x1_ready)
                for p in range(FFN_TILES // 2):
                    slot = panel(l, HALF)
                    for h in range(2):
                        bank = open_bank(pe, "layer", ("ff", 2 * p + h), l)
                        for u in range(2):
                            for k in range(KT):
                                last = mm(bank[:, SEQ * u:SEQ * u + SEQ], slot[:, k, SEQ * u + P * h:SEQ * u + P * h + P],
                                          xT[:, k, :], start=k == 0, stop=k == KT - 1)
                        last.then_inc(pe_done, 1)
                    if p < 10:
                        ada_T(p)
                    if p < 8:
                        ada(p + 2)
                down = {(t, n): open_bank(pe, "layer", ("dn", t, n), l) for t in range(TT) for n in range(2)}
                wait_emptied(pe, "layer", ("ff", FFN_TILES - 1), l)
                for f in range(0, FFN_TILES, 4):
                    slot = panel(l, D)
                    rows_here = range(f, min(f + 4, FFN_TILES))
                    for t in range(TT):
                        for r in rows_here:
                            for n in range(2):
                                last = mm(down[t, n], hid[:, r, P * t:P * t + P], slot[:, r - f, HALF * n:HALF * n + HALF],
                                          start=r == 0, stop=r == FFN_TILES - 1)
                                if r == FFN_TILES - 1:
                                    last.then_inc(pe_done, 1)
                    if r < FFN_TILES - 1:
                        last.then_inc(pe_done, 1)
                ada(10)
                ada(11)
                ada_T(10)
                ada_T(11)
            state["panel"] += (DEPTH - 1) * LAYER_PANELS
            state["per"] = 0
            if second:
                second["tensor"](pe)

        @block.scalar
        def _(act):
            act.dma_start(const[:, :], K["const"]).then_inc(const_loaded, 16)
            act.dma_start(arena[:, 15360:16128], K["dist"]).then_inc(const_loaded, 16)

            def rows_of(dst, at, src):
                n = src.shape[0]
                act.dma_start(dst[at:at + n, :], src).then_inc(par_loaded, 16)
                return at + n

            at = rows_of(par_rows, 0, I["ada_b_2"].rearrange("l (m d) -> (l m) d", d=P))
            at = rows_of(par_rows, at, I["norm_mix_g_2"].rearrange("l (m d) -> (l m) d", d=P))
            rows_of(par_rows, at, I["norm_ffn_g_2"].rearrange("l (m d) -> (l m) d", d=P))
            at = rows_of(par2_rows, 0, I["mlstm_conv_w_2"].rearrange("a w (m d) -> (a w m) d", d=P))
            at = rows_of(par2_rows, at, I["mlstm_conv_b_2"].rearrange("a (m d) -> (a m) d", d=P))
            at = rows_of(par2_rows, at, I["c_2"].rearrange("a (m d) -> (a m) d", d=P))
            at = rows_of(par2_rows, at, I["c_ctx_2"].rearrange("(m d) -> m d", d=P))
            at = rows_of(par2_rows, at, I["conv_w"].rearrange("l w (m d) -> (l w m) d", d=P))
            assert at == 88
            step = Chain(act, act_step)
            S.update(astep=step)
            A = nc.scalar.activation
            act.wait_ge(c_cols_ready, 1)
            for n in range(2):
                ins = A(cT[:, :, n], par2[:, 48 + 8 * n:56 + 8 * n], ACT.Silu)
            ins.then_inc(cT_ready, 1)

            with act.Fori(0, DEPTH) as l:
                step.enter(l, 1)

                def take(key, dst, func=ACT.Copy, part=None):
                    bank, freed = full_bank(act, "layer", key, l)
                    bank = bank if part is None else bank[:, 0:part]
                    if len(dst.shape) == 3:
                        bank = view(bank, dst.shape[1], dst.shape[2])
                    A(dst, bank, func).then_inc(freed, 1)

                def exps(kind, z):
                    act.wait_ge(nmax_ready[kind], l + 1)
                    for h in range(HEADS):
                        for t, (a, b) in enumerate(((0, P), (P, 3 * P))):
                            last = A(z[:, h, a:b], z[:, h, a:b], ACT.Exp, bias=nmax[:, 8 * t + h:8 * t + h + 1],
                                     scale=SCALE, accum_out=sums[:, 8 * t + h:8 * t + h + 1])
                    return last

                def gates_out(kind, dst):
                    for m in range(4):
                        take((f"g{kind}", m), dst[:, 2 * m:2 * m + 2, :], ACT.Sigmoid)

                def values_out(kind, dst):
                    for key in attend(kind):
                        if key[0] == f"pt{kind}":
                            take(key, pt[:, key[1] % 4, :], part=384)
                        else:
                            take(key, dst[:, key[1], :], part=SEQ)

                def take_x(name):
                    for t in range(TT):
                        for m in range(2):
                            take((name, t, m), xT[:, 4 * m:4 * m + 4, P * t:P * t + P])

                take_x("xT")
                for b in range(3):
                    for m in range(2):
                        take(("b", b, m), bpart[:, b, 2 * m:2 * m + 2, :])
                for m in range(2):
                    take(("aq", m), aq[:, 2 * m:2 * m + 2, :])
                take(("ak",), ak, part=SEQ)
                take(("av",), av, part=SEQ)
                take(("cq", 0), cq[:, 0:2, :])
                exps("a", za).then_inc(exp_ready["a"], 1)
                act.wait_ge(exp_ready["a"], 2 * l + 1)
                step(A(sink_e, recip, ACT.Exp))
                A(sink_e[:, 0:1], sink_e[:, 0:1], ACT.Copy).then_inc(exp_ready["a"], 1)
                take(("cq", 1), cq[:, 2:4, :])
                for m in range(2):
                    take(("ck", m), ck[:, 2 * m:2 * m + 2, :])
                for t in range(TT):
                    take(("cv", t), cv[:, t, :])
                exps("c", zc).then_inc(exp_ready["c"], 1)
                gates_out("b", gate_bc)
                values_out("a", ya)
                gates_out("a", gate_a)
                wait_emptied(act, "layer", ("mb", 3), l)
                gates_out("c", gate_bc)
                values_out("c", yc)

                def root(n, t):
                    act.wait_ge(var_ready, 4 * l + 2 * n + t + 1)
                    A(rstd[:, t:t + 1], rstd[:, t:t + 1], ACT.Sqrt).then_inc(std_ready, 1)

                def ada_out(p):
                    take(("ada", p), ada_rows[:, p % 2, :], part=P)

                root(0, 0)
                ada_out(0)
                ada_out(1)
                root(0, 1)
                take_x("x1T")
                for p in range(FFN_TILES // 2):
                    for f in (2 * p, 2 * p + 1):
                        bank, _ = full_bank(act, "layer", ("ff", f), l)
                        if f >= 4:
                            wait_emptied(act, "layer", ("ff", f - 4), l)
                        A(sil[:, f % 4, :], bank[:, 0:SEQ], ACT.Silu).then_inc(sil_ready, 1)
                    if p < 8:
                        ada_out(p + 2)
                root(1, 0)
                ada_out(10)
                ada_out(11)
                root(1, 1)
            step.leave(DEPTH)
            if second:
                second["scalar"](act)

        @block.vector
        def _(dve):
            V = nc.vector
            step = Chain(dve, dve_step)
            S.update(vstep=step)
            TS, STT, TTo = V.tensor_scalar, V.scalar_tensor_tensor, V.tensor_tensor

            for b in range(BANKS):
                V.memset(st[:, b:b + 1], 0.0).then_inc(bank_free[b], 1)
            step(V.memset(mods_now[:, :, :], 0.0))
            step(V.memset(cT[:, :, :], 0.0))
            bank, freed = full_bank(dve, "pre", ("par", 0))
            V.tensor_copy(par[:, :], bank[:, 0:128])
            V.tensor_copy(par2[:, :], bank[:, 128:216]).then_inc(freed, 1)
            wait_emptied(dve, "pre", ("par", 0))
            V.memset(st[:, 253:254], 0.0).then_inc(c_cols_ready, 1)
            dve.wait_ge(x_loaded, 16)
            for m in range(TT):
                V.memset(st[:, 240 + m:241 + m], 0.0).then_inc(x_ready, 1)
            dve.wait_ge(const_loaded, 32)

            with dve.Fori(0, DEPTH) as l:
                step.enter(l, DVE_LAYER)
                step(V.tensor_copy(mods_0[:, :, :], mods_now[:, :, :]))
                step(V.tensor_copy(conv_w[:, :, :], view(par2[:, bass.ds(64 + l * 12, 12)], 3, 4)))

                for m in range(2):
                    wait_emptied(dve, "layer", ("b", 2, m), l)
                bh, bb, bc = bpart[:, 0], bpart[:, 1], bpart[:, 2]
                step(TTo(bh, bh, bc, ALU.mult))
                for tap in (2, 1, 0):
                    s = 2 - tap
                    for m in range(4):
                        w = conv_w[:, tap, m:m + 1]
                        if s == 0:
                            ins = TS(yb[:, m, :], bh[:, m, :], w, None, ALU.mult)
                        else:
                            ins = STT(out=yb[:, m, s:SEQ], in0=bh[:, m, 0:SEQ - s], scalar=w, in1=yb[:, m, s:SEQ],
                                      op0=ALU.mult, op1=ALU.add)
                    step(ins)
                TTo(yb, yb, bb, ALU.mult).then_inc(yb_ready, 1)

                def logits(kind, z, dist, slopes):
                    for h in range(HEADS):
                        bank, freed = full_bank(dve, "layer", (f"s{kind}", h), l)
                        STT(out=z[:, h, :], in0=dist, scalar=slopes[h] / SCALE, in1=bank[:, 0:384],
                            op0=ALU.mult, op1=ALU.add).then_inc(freed, 1)
                    for h in range(HEADS):
                        wait_emptied(dve, "layer", (f"s{kind}", h), l)
                    V.reduce_max(rmax[:, 0:8], z[:, :, 0:P], X_AXIS)
                    step(V.reduce_max(rmax[:, 8:16], z[:, :, P:3 * P], X_AXIS))

                def normalise(kind, z):
                    step(V.reciprocal(recip, sums))
                    TTo(z[:, :, 0:P], z[:, :, 0:P], spread(recip[:, 0:8], P), ALU.mult)
                    TTo(z[:, :, P:3 * P], z[:, :, P:3 * P], spread(recip[:, 8:16], 2 * P),
                        ALU.mult).then_inc(probs_ready[kind], 1)

                logits("a", za, dist_a, SLOPES[0:8])
                dve.wait_ge(sinks_loaded, l * 16 + 16)
                TS(nsink[:, 0:8], sinks, -1.0, None, ALU.mult)
                step(TS(nsink[:, 8:16], sinks, -1.0, None, ALU.mult))
                step(STT(out=nmax, in0=rmax, scalar=-SCALE, in1=nsink, op0=ALU.mult, op1=ALU.min))
                TTo(recip, nmax, nsink, ALU.subtract).then_inc(nmax_ready["a"], 1)
                dve.wait_ge(nmax_ready["a"], l + 1)
                V.memset(st[:, 252:253], 0.0).then_inc(sinks_used, 1)
                dve.wait_ge(exp_ready["a"], 2 * l + 2)
                step(TTo(sums, sums, sink_e, ALU.add))
                normalise("a", za)
                dve.wait_ge(probs_ready["a"], l + 1)
                logits("c", zc, dist_c, SLOPES[8:16])
                TS(nmax, rmax, -SCALE, None, ALU.mult).then_inc(nmax_ready["c"], 1)
                dve.wait_ge(exp_ready["c"], l + 1)
                normalise("c", zc)

                def merge(kind, gate, first=False):
                    for m in range(4):
                        bank, freed = full_bank(dve, "layer", (f"m{kind}", m), l)
                        wait_emptied(dve, "layer", (f"g{kind}", m), l)
                        g, o = gate[:, 2 * m:2 * m + 2, :], merged[:, 2 * m:2 * m + 2, :]
                        TTo(o if first else g, g, view(bank, 2, SEQ), ALU.mult).then_inc(freed, 1)
                        wait_emptied(dve, "layer", (f"m{kind}", m), l)
                        if not first:
                            ins = TTo(o, o, g, ALU.add)
                            if kind == "c" and m == 3:
                                ins.then_inc(merged_ready, 1)
                            else:
                                step(ins)

                merge("b", gate_bc, first=True)
                merge("a", gate_a)
                merge("c", gate_bc)

                def add_residual(keys):
                    for key in keys:
                        bank, freed = full_bank(dve, "layer", key, l)
                        t, n = (key[2], key[1]) if key[0] == "wo" else key[1:]
                        xs = x[:, t, HALF * n:HALF * n + HALF]
                        STT(out=xs, in0=xs, scalar=ALPHA, in1=bank, op0=ALU.mult, op1=ALU.add).then_inc(freed, 1)
                    for key in keys:
                        wait_emptied(dve, "layer", key, l)

                def layer_norm(n, t, loaded, done):
                    for m in range(2):
                        ins = V.bn_stats(bst[:, t, m, :], x[:, t, HALF * m:HALF * m + HALF])
                    step(ins)
                    V.memset(st[:, 255:256], 0.0)
                    step(V.bn_aggr(mv[:, t, :], bst[:, t, :, :]))
                    TS(rstd[:, t:t + 1], mv[:, t, 1:2], LN_EPS, None, ALU.add).then_inc(var_ready, 1)
                    dve.wait_ge(loaded, l * 32 + 32)
                    step(STT(out=x[:, t, :], in0=x[:, t, :], scalar=mv[:, t, 0:1], in1=lnp[:, 0, :], op0=ALU.subtract,
                             op1=ALU.mult))
                    dve.wait_ge(std_ready, 4 * l + 2 * n + t + 1)
                    step(V.reciprocal(rstd[:, t:t + 1], rstd[:, t:t + 1]))
                    STT(out=x[:, t, :], in0=x[:, t, :], scalar=rstd[:, t:t + 1], in1=lnp[:, 1, :], op0=ALU.mult,
                        op1=ALU.add).then_inc(done, 1)

                add_residual([("wo", 0, 0), ("wo", 0, 1), ("wo", 1, 0)])
                layer_norm(0, 0, ln1_loaded, x1_ready)
                add_residual([("wo", 1, 1)])
                layer_norm(0, 1, ln1_loaded, x1_ready)
                dve.wait_ge(x1_ready, 2 * l + 2)

                def mods_out(p):
                    bank, freed = full_bank(dve, "layer", ("adaT", p), l)
                    V.tensor_copy(mods_now[:, 4 * p:4 * p + 4, :], view(bank[:, 0:P], 4, 32)[:, :, 0:2]).then_inc(freed, 1)

                for p in range(FFN_TILES // 2):
                    for f in (2 * p, 2 * p + 1):
                        bank, freed = full_bank(dve, "layer", ("ff", f), l)
                        dve.wait_ge(sil_ready, l * FFN_TILES + f + 1)
                        TTo(hid[:, f, :], sil[:, f % 4, :], bank[:, SEQ:2 * SEQ], ALU.mult).then_inc(freed, 1)
                    if p < 10:
                        mods_out(p)
                for t in range(TT):
                    add_residual([("dn", t, n) for n in range(2)])
                    layer_norm(1, t, ln2_loaded, x_ready)
                dve.wait_ge(x_ready, 2 * l + 4)
                for p in (10, 11):
                    mods_out(p)
                for p in (10, 11):
                    wait_emptied(dve, "layer", ("adaT", p), l)
            step.leave(DEPTH)
            if second:
                second["vector"](dve)


INPUTS = [
    "x", "w_in", "attn_sinks", "conv_w", "w_branch_a", "w_branch_b", "w_branch_c", "w_out", "ln1_g", "ln1_b",
    "w_ffn_gate", "w_ffn_up", "w_ffn_down", "ln2_g", "ln2_b", "c_2", "ctx_2", "c_ctx_2", "ada_w_2", "ada_b_2",
    "norm_mix_g_2", "norm_ffn_g_2", "final_norm_g_2", "mlstm_w_in_2", "mlstm_conv_w_2", "mlstm_conv_b_2",
    "mlstm_igate_b_2", "mlstm_fgate_b_2", "mlstm_head_norm_g_2", "mlstm_w_out_2", "ret_w_in_2",
    "ret_decay_logit_2", "ret_group_norm_g_2", "ret_w_out_2", "moe_router_2", "moe_w_gate_2", "moe_w_up_2",
    "moe_w_down_2",
]


def shape_constants():
    import numpy as np
    f = np.float32
    p = np.arange(P)
    eye = np.eye(P)
    swapped = np.where((p ^ 32)[:, None] == p[None, :], 1.0, 0.0)
    iota = np.tile(np.arange(SEQ), (P, 1))
    quad = (p[:, None] // 32 == np.arange(4)[None, :])
    later = np.where(p[:, None] > p[None, :], -1e30, 0.0)
    earlier = np.where(p[:, None] < p[None, :], -1e30, 0.0)
    const = np.concatenate([eye, swapped, iota, np.stack([p, p + P], 1), quad, later, earlier,
                            np.ones((P, 2)), np.arange(P)[None, :] % 32 == p[:, None]], 1).astype(f)
    q = np.concatenate([np.tile(p[:, None], (1, P)), np.tile(p[:, None] + P, (1, 2 * P))], 1)
    k = np.concatenate([p, np.arange(2 * P)])[None, :]
    gap = q - k
    dist_a = np.where((gap >= 0) & (gap < P), -gap, -1e30)
    dist_c = np.where(gap >= 0, -gap, -1e30)
    dist = np.concatenate([dist_a, dist_c], 1).astype(f)
    kk = np.stack([p, p + P], 1)[:, :, None]
    qq = np.arange(SEQ)[None, None, :]
    ret = np.stack([np.maximum(qq - kk, 0), np.maximum(kk - qq, 0), qq + SEQ - kk, SEQ - qq + kk, (qq == kk) + 0 * kk], 1)
    ret = ret.reshape(P, 5 * 2 * SEQ).astype(f)
    nf = 32
    inv = (np.float32(10000.0) ** (-np.arange(nf, dtype=f) / f(nf))).astype(f)
    t = np.arange(SEQ)
    ang_r = ((t // 64).astype(f)[None, :] * inv[:, None]).astype(f)
    ang_c = ((t % 64).astype(f)[None, :] * inv[:, None]).astype(f)
    ang = np.concatenate([ang_r, ang_r, ang_c, ang_c], 0)
    sign = np.where((p // 32) % 2 == 0, -1.0, 1.0)[:, None]
    rope = np.concatenate([np.cos(ang), sign * np.sin(ang)], 1).astype(f)
    return {"const": const, "dist": dist, "ret": ret, "rope": rope}


def kernel(**inputs):
    import numpy as _np
    import concourse.bacc as _bacc
    from concourse.bass_utils import run_bass_kernel_spmd as _run

    nc = _bacc.Bacc("TRN2", target_bir_lowering=False, num_devices=1)
    arrays, I, K = {}, {}, {}
    for name in INPUTS:
        a = _np.ascontiguousarray(inputs[name])
        arrays[f"in_{name}"] = a
        I[name] = nc.dram_tensor(f"in_{name}", a.shape, mybir.dt.from_np(a.dtype), kind="ExternalInput").ap()
    for name, a in shape_constants().items():
        arrays[f"const_{name}"] = a
        K[name] = nc.dram_tensor(f"const_{name}", a.shape, F32, kind="ExternalInput").ap()
    out = nc.dram_tensor("out", (1, SEQ, D), F32, kind="ExternalOutput").ap()
    program(nc, I, K, out)
    r = _run(nc, [arrays], core_ids=[0])
    return r.results[0]["out"]
```
